# Optimizing a Trainium2 kernel written in Bass

```python
import jax, jax.numpy as jnp
from jax import lax
import numpy as np

D_MODEL = 1024
BATCH = 1
SEQ = 256
DEPTH = 1

MIX_WIDTH = D_MODEL
MOBA_HEAD_DIM = 64
MOBA_WIDTH = MIX_WIDTH // 2
MOBA_HEADS = MOBA_WIDTH // MOBA_HEAD_DIM
MOBA_BLOCK = 256
MOBA_TOPK = 3
MOBA_Q_CHUNK = 64
GDN_HEAD_DIM = 128
GDN_WIDTH = MIX_WIDTH - MOBA_WIDTH
GDN_HEADS = GDN_WIDTH // GDN_HEAD_DIM
GDN_CONV = 4
GDN_CHUNK = 64
N_GROUPS = 4
EXPERTS_PER_GROUP = 8
EXPERT_TOPK = 2
EXPERT_FF = D_MODEL // 4
RMS_EPS = 1e-6
IN_SPLITS = (MOBA_WIDTH, MOBA_WIDTH, MOBA_WIDTH, 3 * GDN_WIDTH, GDN_WIDTH, GDN_HEADS, GDN_HEADS)
IN_PROJ_WIDTH = 3 * MOBA_WIDTH + 4 * GDN_WIDTH + 2 * GDN_HEADS


def rmsnorm(x, gain):
    x32 = x.astype(jnp.float32)
    y = x32 * lax.rsqrt(jnp.mean(x32 * x32, axis=-1, keepdims=True) + RMS_EPS)
    return (y * gain.astype(jnp.float32)).astype(x.dtype)

def l2norm(x):
    return x * lax.rsqrt(jnp.sum(x * x, axis=-1, keepdims=True) + 1e-6)

def moba_attention(q, k, v):
    B, S, H, Dh = q.shape
    nb = -(-S // MOBA_BLOCK)
    pad = nb * MOBA_BLOCK - S
    topk = min(MOBA_TOPK, nb)
    scale = Dh ** -0.5
    q = q.transpose(0, 2, 1, 3)
    kp = jnp.pad(k.transpose(0, 2, 1, 3), ((0, 0), (0, 0), (0, pad), (0, 0)))
    vp = jnp.pad(v.transpose(0, 2, 1, 3), ((0, 0), (0, 0), (0, pad), (0, 0)))
    kb = kp.reshape(B, H, nb, MOBA_BLOCK, Dh)
    vb = vp.reshape(B, H, nb, MOBA_BLOCK, Dh)
    k_mean = jnp.mean(kb.astype(jnp.float32), axis=3)
    b_idx = jnp.arange(B)[:, None, None, None]
    h_idx = jnp.arange(H)[None, :, None, None]
    blk_ids = jnp.arange(nb)
    n_chunks = S // MOBA_Q_CHUNK

    def chunk(c):
        start = c * MOBA_Q_CHUNK
        qc = lax.dynamic_slice_in_dim(q, start, MOBA_Q_CHUNK, axis=2)
        qpos = start + jnp.arange(MOBA_Q_CHUNK)
        own = start // MOBA_BLOCK
        gate = jnp.einsum('bhqd,bhnd->bhqn', qc.astype(jnp.float32), k_mean)
        gate = jnp.where(blk_ids < own, gate, -jnp.inf)
        _, gidx = lax.top_k(gate, topk)
        sel_ok = jnp.arange(topk) < own
        k_sel = kb[b_idx, h_idx, gidx]
        v_sel = vb[b_idx, h_idx, gidx]
        s_sel = jnp.einsum('bhqd,bhqkld->bhqkl', qc, k_sel).astype(jnp.float32) * scale
        s_sel = jnp.where(sel_ok[:, None], s_sel, -jnp.inf)
        k_own = lax.dynamic_slice_in_dim(kb, own, 1, axis=2)[:, :, 0]
        v_own = lax.dynamic_slice_in_dim(vb, own, 1, axis=2)[:, :, 0]
        s_own = jnp.einsum('bhqd,bhld->bhql', qc, k_own).astype(jnp.float32) * scale
        kpos = own * MOBA_BLOCK + jnp.arange(MOBA_BLOCK)
        s_own = jnp.where(kpos[None, :] <= qpos[:, None], s_own, -jnp.inf)
        s = jnp.concatenate([s_sel.reshape(B, H, MOBA_Q_CHUNK, topk * MOBA_BLOCK), s_own], axis=-1)
        p = jax.nn.softmax(s, axis=-1).astype(v.dtype)
        p_sel = p[..., :topk * MOBA_BLOCK].reshape(B, H, MOBA_Q_CHUNK, topk, MOBA_BLOCK)
        p_own = p[..., topk * MOBA_BLOCK:]
        return (jnp.einsum('bhqkl,bhqkld->bhqd', p_sel, v_sel)
                + jnp.einsum('bhql,bhld->bhqd', p_own, v_own))

    out = lax.map(chunk, jnp.arange(n_chunks))
    return out.transpose(1, 0, 3, 2, 4).reshape(B, S, H, Dh)

def causal_depthwise_conv(x, w):
    C = x.shape[-1]
    return lax.conv_general_dilated(
        x, w[:, None, :].astype(x.dtype), window_strides=(1,),
        padding=((GDN_CONV - 1, 0),), dimension_numbers=('NWC', 'WIO', 'NWC'),
        feature_group_count=C)

def gated_delta_rule(q, k, v, g, beta):
    B, S, H, Dk = q.shape
    Dv = v.shape[-1]
    C = GDN_CHUNK
    N = S // C

    def to_chunks(t):
        return t.reshape(B, N, C, H, *t.shape[3:]).swapaxes(2, 3)

    q, k, v, g, beta = (to_chunks(t) for t in (q, k, v, g, beta))
    G = jnp.cumsum(g, axis=-1)
    incl = jnp.tril(jnp.ones((C, C), dtype=bool))
    strict = jnp.tril(jnp.ones((C, C), dtype=bool), k=-1)
    decay = jnp.exp(jnp.where(incl, G[..., :, None] - G[..., None, :], -jnp.inf))
    kk = jnp.einsum('bnhid,bnhjd->bnhij', k, k)
    A = jnp.where(strict, beta[..., :, None] * kk * decay, 0.0)
    eye = jnp.eye(C, dtype=A.dtype)
    gam = jnp.exp(G)
    rhs = jnp.concatenate([beta[..., None] * v, (beta * gam)[..., None] * k], axis=-1)
    sol = lax.linalg.triangular_solve(eye + A, rhs, left_side=True, lower=True, unit_diagonal=True)
    u_v, w = sol[..., :Dv], sol[..., Dv:]
    qk = jnp.einsum('bnhid,bnhjd->bnhij', q, k) * decay
    q_dec = q * gam[..., None]
    k_dec = k * jnp.exp(G[..., -1:] - G)[..., None]
    g_last = jnp.exp(G[..., -1])

    def step(state, xs):
        u_v_c, w_c, qk_c, q_dec_c, k_dec_c, g_last_c = xs
        u = u_v_c - jnp.einsum('bhck,bhkv->bhcv', w_c, state)
        o = jnp.einsum('bhck,bhkv->bhcv', q_dec_c, state) + jnp.einsum('bhij,bhjv->bhiv', qk_c, u)
        new_state = g_last_c[..., None, None] * state + jnp.einsum('bhck,bhcv->bhkv', k_dec_c, u)
        return new_state, o

    xs = tuple(t.swapaxes(0, 1) for t in (u_v, w, qk, q_dec, k_dec, g_last))
    state0 = jnp.zeros((B, H, Dk, Dv), dtype=q.dtype)
    _, o = lax.scan(step, state0, xs)
    return o.transpose(1, 0, 3, 2, 4).reshape(B, S, H, Dv)

def hierarchical_moe(h, w_group, w_router, w_gate, w_up, w_down):
    T = h.shape[0]
    group_logits = jnp.einsum('td,dg->tg', h, w_group).astype(jnp.float32)
    group_prob = jax.nn.softmax(group_logits, axis=-1)
    g_sel = jnp.argmax(group_logits, axis=-1)
    p_group = jnp.take_along_axis(group_prob, g_sel[:, None], axis=-1)
    expert_logits = jnp.einsum('td,de->te', h, w_router).astype(jnp.float32)
    expert_logits = expert_logits.reshape(T, N_GROUPS, EXPERTS_PER_GROUP)
    in_group = jnp.take_along_axis(expert_logits, g_sel[:, None, None], axis=1)[:, 0]
    in_prob = jax.nn.softmax(in_group, axis=-1)
    top_p, top_i = lax.top_k(in_prob, EXPERT_TOPK)
    top_p = top_p / jnp.sum(top_p, axis=-1, keepdims=True)
    within = jnp.sum(jax.nn.one_hot(top_i, EXPERTS_PER_GROUP, dtype=jnp.float32) * top_p[..., None], axis=1)
    combine = (jax.nn.one_hot(g_sel, N_GROUPS, dtype=jnp.float32)[:, :, None]
               * p_group[:, :, None] * within[:, None, :]).astype(h.dtype)
    y = jnp.zeros_like(h)
    for grp in range(N_GROUPS):
        hid = (jax.nn.silu(jnp.einsum('td,edf->tef', h, w_gate[grp]))
               * jnp.einsum('td,edf->tef', h, w_up[grp])) * combine[:, grp, :, None]
        y = y + jnp.einsum('tef,efd->td', hid, w_down[grp])
    return y

def first_inputs(seed: int = 0) -> dict:
    key = jax.random.key(seed)
    ks = jax.random.split(key, 16)
    f32 = jnp.float32
    D = D_MODEL
    x = jax.random.normal(ks[0], (BATCH, SEQ, D), f32)
    attn_norm = 1.0 + 0.02 * jax.random.normal(ks[1], (DEPTH, D), f32)
    w_in = jax.random.normal(ks[2], (DEPTH, D, IN_PROJ_WIDTH), f32) * D ** -0.5
    conv_w = jax.random.normal(ks[3], (DEPTH, GDN_CONV, 3 * GDN_WIDTH), f32) * GDN_CONV ** -0.5
    A_log = jnp.log(jax.random.uniform(ks[4], (DEPTH, GDN_HEADS), f32, 1.0, 16.0))
    dt = jnp.exp(jax.random.uniform(ks[5], (DEPTH, GDN_HEADS), f32, np.log(1e-3), np.log(1e-1)))
    dt_bias = dt + jnp.log(-jnp.expm1(-dt))
    gdn_norm = 1.0 + 0.02 * jax.random.normal(ks[6], (DEPTH, GDN_HEAD_DIM), f32)
    w_out = jax.random.normal(ks[7], (DEPTH, MIX_WIDTH, D), f32) * MIX_WIDTH ** -0.5
    ffn_norm = 1.0 + 0.02 * jax.random.normal(ks[8], (DEPTH, D), f32)
    w_group = jax.random.normal(ks[9], (DEPTH, D, N_GROUPS), f32) * D ** -0.5
    w_router = jax.random.normal(ks[10], (DEPTH, D, N_GROUPS * EXPERTS_PER_GROUP), f32) * D ** -0.5
    w_gate = jax.random.normal(ks[11], (DEPTH, N_GROUPS, EXPERTS_PER_GROUP, D, EXPERT_FF), f32) * D ** -0.5
    w_up = jax.random.normal(ks[12], (DEPTH, N_GROUPS, EXPERTS_PER_GROUP, D, EXPERT_FF), f32) * D ** -0.5
    w_down = jax.random.normal(ks[13], (DEPTH, N_GROUPS, EXPERTS_PER_GROUP, EXPERT_FF, D), f32) * EXPERT_FF ** -0.5
    final_norm = 1.0 + 0.02 * jax.random.normal(ks[14], (D,), f32)
    return {'x': x, 'attn_norm': attn_norm, 'w_in': w_in, 'conv_w': conv_w, 'A_log': A_log,
            'dt_bias': dt_bias, 'gdn_norm': gdn_norm, 'w_out': w_out, 'ffn_norm': ffn_norm,
            'w_group': w_group, 'w_router': w_router, 'w_gate': w_gate, 'w_up': w_up,
            'w_down': w_down, 'final_norm': final_norm}

def first_block(x, attn_norm, w_in, conv_w, A_log, dt_bias, gdn_norm, w_out, ffn_norm,
              w_group, w_router, w_gate, w_up, w_down, final_norm):
    B, S, D = x.shape
    offsets = np.cumsum(IN_SPLITS)[:-1].tolist()
    f32 = jnp.float32
    for l in range(DEPTH):
        h = rmsnorm(x, attn_norm[l])
        proj = jnp.einsum('bsd,de->bse', h, w_in[l])
        mq, mk, mv, gqkv, gz, ga, gb = jnp.split(proj, offsets, axis=-1)
        to_a = lambda t: t.reshape(B, S, MOBA_HEADS, MOBA_HEAD_DIM)
        y_a = moba_attention(to_a(mq), to_a(mk), to_a(mv)).reshape(B, S, MOBA_WIDTH)
        gqkv = jax.nn.silu(causal_depthwise_conv(gqkv, conv_w[l]))
        gq, gk, gv = jnp.split(gqkv, 3, axis=-1)
        to_b = lambda t: t.reshape(B, S, GDN_HEADS, GDN_HEAD_DIM).astype(f32)
        gq = l2norm(to_b(gq)) * GDN_HEAD_DIM ** -0.5
        gk = l2norm(to_b(gk))
        log_decay = -jnp.exp(A_log[l].astype(f32)) * jax.nn.softplus(ga.astype(f32) + dt_bias[l].astype(f32))
        beta = jax.nn.sigmoid(gb.astype(f32))
        o_b = gated_delta_rule(gq, gk, to_b(gv), log_decay, beta)
        o_b = rmsnorm(o_b, gdn_norm[l]) * jax.nn.silu(to_b(gz))
        y_b = o_b.reshape(B, S, GDN_WIDTH).astype(x.dtype)
        mix = jnp.concatenate([y_a, y_b], axis=-1)
        x = x + jnp.einsum('bse,ed->bsd', mix, w_out[l])
        h = rmsnorm(x, ffn_norm[l]).reshape(B * S, D)
        y = hierarchical_moe(h, w_group[l], w_router[l], w_gate[l], w_up[l], w_down[l])
        x = x + y.reshape(B, S, D)
    return rmsnorm(x, final_norm)


GRID_W = 64
CTX_LEN = 256
HEAD_DIM = 64
A_HEADS = 8
A_KV_HEADS = 2
A_WINDOW = 128
A_BLOCK = 128
B_HEADS = 8
NA_MAX_KH = 8
NA_KW = 16
NA_ROW_BLOCK = 2
A_WIDTH = A_HEADS * HEAD_DIM
A_KV_WIDTH = A_KV_HEADS * HEAD_DIM
B_WIDTH = B_HEADS * HEAD_DIM
MIX_WIDTH_2 = A_WIDTH + B_WIDTH
IN_COLS = A_WIDTH + 2 * A_KV_WIDTH + 3 * B_WIDTH
FFN_HIDDEN = -(-8 * D_MODEL // (3 * 256)) * 256
N_MOD = 6
ROPE_BASE = 10000.0
EPS = 1e-6


def _rms_norm(x, g):
    xf = x.astype(jnp.float32)
    y = xf * lax.rsqrt(jnp.mean(xf * xf, axis=-1, keepdims=True) + EPS)
    return (y * g.astype(jnp.float32)).astype(x.dtype)

def _modulate(h, shift, scale):
    return h * (1 + scale) + shift

def _axial_rope(x, rows, cols):
    half = HEAD_DIM // 2
    quarter = half // 2
    inv_freq = 1.0 / (ROPE_BASE ** (jnp.arange(quarter, dtype=jnp.float32) / quarter))

    def rot(xh, pos):
        ang = pos.astype(jnp.float32)[:, None] * inv_freq[None, :]
        cos = jnp.cos(ang)[None, :, None, :]
        sin = jnp.sin(ang)[None, :, None, :]
        x1 = xh[..., :quarter].astype(jnp.float32)
        x2 = xh[..., quarter:].astype(jnp.float32)
        return jnp.concatenate([x1 * cos - x2 * sin, x1 * sin + x2 * cos], axis=-1)

    out = jnp.concatenate([rot(x[..., :half], rows), rot(x[..., half:], cols)], axis=-1)
    return out.astype(x.dtype)

def _in_proj(h, w_in):
    B, L, _ = h.shape
    p = h @ w_in
    offs = np.cumsum([A_WIDTH, A_KV_WIDTH, A_KV_WIDTH, B_WIDTH, B_WIDTH])
    q_a, k_a, v_a, q_b, k_b, v_b = jnp.split(p, offs, axis=-1)
    hd = lambda t, n: t.reshape(B, L, n, HEAD_DIM)
    return (hd(q_a, A_HEADS), hd(k_a, A_KV_HEADS), hd(v_a, A_KV_HEADS),
            hd(q_b, B_HEADS), hd(k_b, B_HEADS), hd(v_b, B_HEADS))

def _band_mask(S):
    nb = S // A_BLOCK
    span = A_BLOCK + 2 * A_WINDOW
    qpos = np.arange(nb)[:, None, None] * A_BLOCK + np.arange(A_BLOCK)[None, :, None]
    kpos = np.arange(nb)[:, None, None] * A_BLOCK - A_WINDOW + np.arange(span)[None, None, :]
    return (np.abs(kpos - qpos) <= A_WINDOW) & (kpos >= 0) & (kpos < S)

def _window_gqa_latent(q, k, v, k_ctx, v_ctx, sink):
    B, S = q.shape[:2]
    nb = S // A_BLOCK
    G = A_HEADS // A_KV_HEADS
    n_side = A_WINDOW // A_BLOCK
    scale = HEAD_DIM ** -0.5
    pad = ((0, 0), (A_WINDOW, A_WINDOW), (0, 0), (0, 0))
    kp = jnp.pad(k, pad).reshape(B, nb + 2 * n_side, A_BLOCK, A_KV_HEADS, HEAD_DIM)
    vp = jnp.pad(v, pad).reshape(B, nb + 2 * n_side, A_BLOCK, A_KV_HEADS, HEAD_DIM)
    kb = jnp.concatenate([kp[:, o:o + nb] for o in range(2 * n_side + 1)], axis=2)
    vb = jnp.concatenate([vp[:, o:o + nb] for o in range(2 * n_side + 1)], axis=2)
    span = kb.shape[2]
    qb = q.reshape(B, nb, A_BLOCK, A_KV_HEADS, G, HEAD_DIM)
    mask = jnp.asarray(_band_mask(S))[:, None, None]
    s_loc = jnp.einsum('bnqkgd,bnjkd->bnkgqj', qb, kb).astype(jnp.float32) * scale
    s_loc = jnp.where(mask, s_loc, -jnp.inf)
    s_ctx = jnp.einsum('bnqkgd,bjkd->bnkgqj', qb, k_ctx).astype(jnp.float32) * scale
    sink_col = jnp.broadcast_to(sink.astype(jnp.float32).reshape(1, 1, A_KV_HEADS, G, 1, 1),
                                s_loc.shape[:-1] + (1,))
    p = jax.nn.softmax(jnp.concatenate([s_loc, s_ctx, sink_col], axis=-1), axis=-1)
    L = k_ctx.shape[1]
    p_loc = p[..., :span].astype(v.dtype)
    p_ctx = p[..., span:span + L].astype(v.dtype)
    o = (jnp.einsum('bnkgqj,bnjkd->bnqkgd', p_loc, vb)
         + jnp.einsum('bnkgqj,bjkd->bnqkgd', p_ctx, v_ctx))
    return o.reshape(B, S, A_WIDTH)

def _na_pattern(rows):
    kh = min(NA_MAX_KH, rows)
    n_blk = rows // NA_ROW_BLOCK
    n_kr = min(NA_ROW_BLOCK + kh - 1, rows)
    r0 = np.arange(n_blk) * NA_ROW_BLOCK
    row_start = lambda r: np.clip(r - kh // 2, 0, rows - kh)
    k_start = np.minimum(row_start(r0), rows - n_kr)
    key_rows = k_start[:, None] + np.arange(n_kr)[None, :]
    qi = np.arange(NA_ROW_BLOCK * GRID_W)
    q_r = r0[:, None] + qi[None, :] // GRID_W
    q_c = qi % GRID_W
    kj = np.arange(n_kr * GRID_W)
    k_r = key_rows[:, kj // GRID_W]
    k_c = kj % GRID_W
    rs = row_start(q_r)
    cs = np.clip(q_c - NA_KW // 2, 0, GRID_W - NA_KW)
    row_ok = (k_r[:, None, :] >= rs[:, :, None]) & (k_r[:, None, :] < rs[:, :, None] + kh)
    col_ok = (k_c[None, :] >= cs[:, None]) & (k_c[None, :] < cs[:, None] + NA_KW)
    mask = row_ok & col_ok[None]
    dr = np.clip(k_r[:, None, :] - q_r[:, :, None] + NA_MAX_KH - 1, 0, 2 * NA_MAX_KH - 2)
    dc = np.broadcast_to(np.clip(k_c[None, :] - q_c[:, None] + NA_KW - 1, 0, 2 * NA_KW - 2)[None],
                         mask.shape)
    return key_rows, mask, dr, dc

def _neighbourhood_latent(q, k, v, k_ctx, v_ctx, rpb):
    B, S = q.shape[:2]
    rows = S // GRID_W
    key_rows, mask, dr, dc = _na_pattern(rows)
    n_blk, n_kr = key_rows.shape
    scale = HEAD_DIM ** -0.5
    idx = jnp.asarray(key_rows)
    kg = k.reshape(B, rows, GRID_W, B_HEADS, HEAD_DIM)[:, idx].reshape(
        B, n_blk, n_kr * GRID_W, B_HEADS, HEAD_DIM)
    vg = v.reshape(B, rows, GRID_W, B_HEADS, HEAD_DIM)[:, idx].reshape(
        B, n_blk, n_kr * GRID_W, B_HEADS, HEAD_DIM)
    qb = q.reshape(B, n_blk, NA_ROW_BLOCK * GRID_W, B_HEADS, HEAD_DIM)
    bias = jnp.transpose(rpb[:, jnp.asarray(dr), jnp.asarray(dc)], (1, 0, 2, 3)).astype(jnp.float32)
    s_loc = jnp.einsum('bnqhd,bnjhd->bnhqj', qb, kg).astype(jnp.float32) * scale + bias
    s_loc = jnp.where(jnp.asarray(mask)[:, None], s_loc, -jnp.inf)
    s_ctx = jnp.einsum('bnqhd,bjhd->bnhqj', qb, k_ctx).astype(jnp.float32) * scale
    p = jax.nn.softmax(jnp.concatenate([s_loc, s_ctx], axis=-1), axis=-1)
    kb_len = kg.shape[2]
    p_loc = p[..., :kb_len].astype(v.dtype)
    p_ctx = p[..., kb_len:].astype(v.dtype)
    o = (jnp.einsum('bnhqj,bnjhd->bnqhd', p_loc, vg)
         + jnp.einsum('bnhqj,bjhd->bnqhd', p_ctx, v_ctx))
    return o.reshape(B, S, B_WIDTH)

def _ctx_self_attention(q, k, v, n_kv, sink=None):
    B, L, H, _ = q.shape
    G = H // n_kv
    qg = q.reshape(B, L, n_kv, G, HEAD_DIM)
    s = jnp.einsum('blkgd,bjkd->bkglj', qg, k).astype(jnp.float32) * HEAD_DIM ** -0.5
    if sink is not None:
        sink_col = jnp.broadcast_to(sink.astype(jnp.float32).reshape(1, n_kv, G, 1, 1), s.shape[:-1] + (1,))
        s = jnp.concatenate([s, sink_col], axis=-1)
    p = jax.nn.softmax(s, axis=-1)[..., :L].astype(v.dtype)
    o = jnp.einsum('bkglj,bjkd->blkgd', p, v)
    return o.reshape(B, L, H * HEAD_DIM)

def _merge(o_a, o_b, g_a, g_b, w_out):
    return jnp.concatenate([_rms_norm(o_a, g_a), _rms_norm(o_b, g_b)], axis=-1) @ w_out

def _swiglu(h, w_gate, w_up, w_down):
    return (jax.nn.silu(h @ w_gate) * (h @ w_up)) @ w_down

def second_inputs(seed: int = 0) -> dict:
    key = jax.random.key(seed)
    ks = jax.random.split(key, 24)
    nrm = lambda k, shape: jax.random.normal(k, shape, dtype=jnp.float32)
    gain = lambda k, shape: 1.0 + 0.05 * nrm(k, shape)
    D = D_MODEL
    return {
        "x": nrm(ks[0], (BATCH, SEQ, D)),
        "c": nrm(ks[1], (BATCH, D)),
        "ctx": nrm(ks[2], (BATCH, CTX_LEN, D)),
        "c_ctx": nrm(ks[3], (D,)),
        "w_mod": nrm(ks[4], (DEPTH, D, N_MOD * D)) * (0.5 * D ** -0.5),
        "b_mod": 0.01 * nrm(ks[5], (DEPTH, N_MOD * D)),
        "norm1_g": gain(ks[6], (DEPTH, D)),
        "w_in": nrm(ks[7], (DEPTH, D, IN_COLS)) * D ** -0.5,
        "qn_a": gain(ks[8], (DEPTH, HEAD_DIM)),
        "kn_a": gain(ks[9], (DEPTH, HEAD_DIM)),
        "sink_a": 0.5 * nrm(ks[10], (DEPTH, A_HEADS)),
        "qn_b": gain(ks[11], (DEPTH, HEAD_DIM)),
        "kn_b": gain(ks[12], (DEPTH, HEAD_DIM)),
        "rpb_b": 0.1 * nrm(ks[13], (DEPTH, B_HEADS, 2 * NA_MAX_KH - 1, 2 * NA_KW - 1)),
        "on_a": gain(ks[14], (DEPTH, A_WIDTH)),
        "on_b": gain(ks[15], (DEPTH, B_WIDTH)),
        "w_out": nrm(ks[16], (DEPTH, MIX_WIDTH_2, D)) * MIX_WIDTH_2 ** -0.5,
        "norm2_g": gain(ks[17], (DEPTH, D)),
        "w_gate": nrm(ks[18], (DEPTH, D, FFN_HIDDEN)) * D ** -0.5,
        "w_up": nrm(ks[19], (DEPTH, D, FFN_HIDDEN)) * D ** -0.5,
        "w_down": nrm(ks[20], (DEPTH, FFN_HIDDEN, D)) * FFN_HIDDEN ** -0.5,
    }

def second_block(x, c, ctx, c_ctx, w_mod, b_mod, norm1_g, w_in, qn_a, kn_a, sink_a, qn_b, kn_b,
              rpb_b, on_a, on_b, w_out, norm2_g, w_gate, w_up, w_down):
    S = x.shape[1]
    t = jnp.arange(S)
    row_pos = t // GRID_W
    col_pos = t % GRID_W
    for l in range(DEPTH):
        mod = (jax.nn.silu(c) @ w_mod[l] + b_mod[l])[:, None, :]
        mod_c = (jax.nn.silu(c_ctx) @ w_mod[l] + b_mod[l])[None, None, :]
        sh1, sc1, g1, sh2, sc2, g2 = jnp.split(mod, N_MOD, axis=-1)
        csh1, csc1, cg1, csh2, csc2, cg2 = jnp.split(mod_c, N_MOD, axis=-1)

        h = _modulate(_rms_norm(x, norm1_g[l]), sh1, sc1)
        hc = _modulate(_rms_norm(ctx, norm1_g[l]), csh1, csc1)
        q_a, k_a, v_a, q_b, k_b, v_b = _in_proj(h, w_in[l])
        q_ac, k_ac, v_ac, q_bc, k_bc, v_bc = _in_proj(hc, w_in[l])

        q_a = _axial_rope(_rms_norm(q_a, qn_a[l]), row_pos, col_pos)
        k_a = _axial_rope(_rms_norm(k_a, kn_a[l]), row_pos, col_pos)
        q_ac, k_ac = _rms_norm(q_ac, qn_a[l]), _rms_norm(k_ac, kn_a[l])
        q_b, k_b = _rms_norm(q_b, qn_b[l]), _rms_norm(k_b, kn_b[l])
        q_bc, k_bc = _rms_norm(q_bc, qn_b[l]), _rms_norm(k_bc, kn_b[l])

        o_a = _window_gqa_latent(q_a, k_a, v_a, k_ac, v_ac, sink_a[l])
        o_b = _neighbourhood_latent(q_b, k_b, v_b, k_bc, v_bc, rpb_b[l])
        x_new = x + g1 * _merge(o_a, o_b, on_a[l], on_b[l], w_out[l])
        h2 = _modulate(_rms_norm(x_new, norm2_g[l]), sh2, sc2)
        x_new = x_new + g2 * _swiglu(h2, w_gate[l], w_up[l], w_down[l])

        if l < DEPTH - 1:
            o_ac = _ctx_self_attention(q_ac, k_ac, v_ac, A_KV_HEADS, sink_a[l])
            o_bc = _ctx_self_attention(q_bc, k_bc, v_bc, B_HEADS)
            ctx = ctx + cg1 * _merge(o_ac, o_bc, on_a[l], on_b[l], w_out[l])
            hc2 = _modulate(_rms_norm(ctx, norm2_g[l]), csh2, csc2)
            ctx = ctx + cg2 * _swiglu(hc2, w_gate[l], w_up[l], w_down[l])
        x = x_new
    return x


def setup_inputs(seed=0):
    out = dict(first_inputs(seed))
    for name, value in second_inputs(seed + 1).items():
        if name != "x":
            out[name + "_2"] = value
    return out


def reference(
    x, attn_norm, w_in, conv_w, A_log, dt_bias, gdn_norm, w_out, ffn_norm, w_group, w_router,
    w_gate, w_up, w_down, final_norm, c_2, ctx_2, c_ctx_2, w_mod_2, b_mod_2, norm1_g_2, w_in_2,
    qn_a_2, kn_a_2, sink_a_2, qn_b_2, kn_b_2, rpb_b_2, on_a_2, on_b_2, w_out_2, norm2_g_2,
    w_gate_2, w_up_2, w_down_2,
):
    x = first_block(
        x, attn_norm, w_in, conv_w, A_log, dt_bias, gdn_norm, w_out, ffn_norm, w_group,
        w_router, w_gate, w_up, w_down, final_norm,
    )
    return second_block(
        x, c_2, ctx_2, c_ctx_2, w_mod_2, b_mod_2, norm1_g_2, w_in_2, qn_a_2, kn_a_2, sink_a_2,
        qn_b_2, kn_b_2, rpb_b_2, on_a_2, on_b_2, w_out_2, norm2_g_2, w_gate_2, w_up_2, w_down_2,
    )


_drawn_inputs = setup_inputs


def setup_inputs(seed=0):
    import zlib

    import numpy as np

    out = dict(_drawn_inputs(seed))
    spreads = {}
    factors = {'gdn_norm': 3.549,
     'final_norm': 2.919,
     'b_mod_2': 3.455,
     'norm1_g_2': 6.725,
     'qn_a_2': 8.0,
     'kn_a_2': 8.0,
     'sink_a_2': 8.0,
     'qn_b_2': 8.0,
     'kn_b_2': 8.0,
     'rpb_b_2': 25.646,
     'on_a_2': 13.955,
     'on_b_2': 19.901,
     'norm2_g_2': 3.933}
    for name, (base, spread) in spreads.items():
        noise = np.random.default_rng([zlib.crc32(name.encode()), seed]).standard_normal(out[name].shape)
        drawn = base * np.exp(spread * noise) if base else spread * noise
        out[name] = __import__('jax').numpy.asarray(drawn.astype(out[name].dtype))
    for name, factor in factors.items():
        out[name] = (out[name] * factor).astype(out[name].dtype)
    return out
```

```python
from contextlib import ExitStack

import concourse.bass as bass
import numpy as np
from concourse import mybir

F32 = mybir.dt.float32
I32 = mybir.dt.int32
ALU = mybir.AluOpType
ACT = mybir.ActivationFunctionType
AX = mybir.AxisListType.X

P = 128
T = 256
NB = T // P
D = 1024
KD = D // P
EPS = 1e-6
BIG = 1e30

MH, MD = 8, 64
GH, GD = 4, 128
TAPS = 4
GQKV = 3 * GH
W_IN = 3592
NG, EG, NE, FF = 4, 8, 32, 256
NR = NG + NE
SLOTS = 32
EPG = P // SLOTS
ROUNDS = T // SLOTS
PASSES = NE // EPG

GRID = 64
AH, BH, HD = 8, 8, 64
CTX = 256
IN2 = 2304
FFN = 2816
NMOD = 6 * D // 512

SLOT = 2048
NS = 8
MU = 12

LEVELS = 7


def constants():
    cols, at = [], {}

    def put(name, a):
        full = np.zeros((P, a.shape[1]), np.float32)
        full[:a.shape[0]] = a
        at[name] = (sum(c.shape[1] for c in cols), a.shape[1])
        cols.append(full)

    i = np.arange(P)
    put("ident", np.eye(P))
    put("upto", (i[:, None] <= i[None, :]).astype(np.float64))
    put("before", (i[:, None] < i[None, :]).astype(np.float64))
    put("ones", np.ones((P, P)))
    put("future", np.where(i[None, :] < i[:, None], BIG, 0.0))
    key = np.arange(T)
    put("causal", np.concatenate([np.where(i[None, :] > i[:, None], -BIG, 0.0),
                                  np.where(key[None, :] > P + i[:, None], -BIG, 0.0)], 1))
    for n in range(LEVELS):
        b = 1 << n
        put(f"level{n}", ((i[:, None] // (2 * b) == i[None, :] // (2 * b)) & (i[:, None] // b % 2 == 0)
                          & (i[None, :] // b % 2 == 1)).astype(np.float64))
    put("slots", np.tile(np.tile(np.arange(SLOTS), EPG)[None], (P, 1)))
    put("sum2", np.stack([(i % 32 == 0), (i % 32 == 1)], 1).astype(np.float64))
    put("sumrow", np.tile((i % 32 == 0)[:, None], (1, P)).astype(np.float64))
    pick = np.zeros((NMOD, NMOD, 32))
    for n in range(NMOD):
        pick[n, n, 0:2] = 1
    put("pick", pick.reshape(NMOD, NMOD * 32))
    q = np.arange(T)
    near = np.where(np.abs(key[None] - q[:, None]) <= 128, 0.0, -BIG)
    put("window", near.reshape(NB, P, T).transpose(1, 0, 2).reshape(P, NB * T))
    qc, kc = q % GRID, key % GRID
    cs = np.clip(qc - 8, 0, GRID - 16)
    ok = (kc[None] >= cs[:, None]) & (kc[None] < cs[:, None] + 16)
    ok = ok.reshape(T // GRID, GRID, T)[:, ::-1].reshape(T, T)
    flip = np.kron(np.eye(P // GRID), np.eye(GRID)[::-1])
    put("flip", flip)
    put("columns", np.where(ok, 0.0, -BIG).reshape(NB, P, T).transpose(1, 0, 2).reshape(P, NB * T))
    inv = (1.0 / (np.float32(10000.0) ** (np.arange(16, dtype=np.float32) / np.float32(16)))).astype(np.float32)
    ang = lambda pos: pos.astype(np.float32)[:, None] * inv[None]
    r, c = ang(q // GRID), ang(q % GRID)
    cos = np.concatenate([np.cos(r), np.cos(r), np.cos(c), np.cos(c)], 1)
    sin = np.concatenate([-np.sin(r), np.sin(r), -np.sin(c), np.sin(c)], 1)
    put("cos", cos.reshape(NB, P, HD).transpose(1, 0, 2).reshape(P, NB * HD))
    put("sin", sin.reshape(NB, P, HD).transpose(1, 0, 2).reshape(P, NB * HD))
    put("tie", np.tile(np.concatenate([np.arange(NG, 0, -1), np.arange(EG, 0, -1)])[None], (P, 1)))
    put("neghalf", np.full((P, 16), -0.5))
    put("epsq", np.full((P, 1), GD * EPS))
    put("epsk", np.full((P, 1), EPS))
    return np.ascontiguousarray(np.concatenate(cols, 1).astype(np.float32)), at


ROWS = {}
_n = 0
for _name, _k in (("attn", 8), ("norm1", 8), ("norm2", 8), ("on_a", 4), ("on_b", 4), ("conv", TAPS * GQKV),
                  ("gdn", 1), ("c", 8), ("c_ctx", 8)):
    ROWS[_name] = _n
    _n += _k
N_ROWS = _n


def two_blocks(nc, consts, where, i, out):
    with ExitStack() as ctx:
        def sb(name, shape, dt=F32):
            return ctx.enter_context(nc.sbuf_tensor(name, shape, dt))

        def sem(name):
            return ctx.enter_context(nc.semaphore(name))

        C = sb("consts", [P, consts.shape[1]])

        def c(name):
            a, n = where[name]
            return C[:, a:a + n]

        ring = sb("ring", [P, NS, SLOT])
        xres = sb("residual", [P, NB, D])
        arena = sb("arena", [P, 28836])
        vc = sb("vec_cols", [P, N_ROWS])
        modT = sb("mod_cols", [P, 48, 2])
        modA = sb("mod_gains", [P, 3, KD])
        wr = sb("w_route", [P, KD, NR])
        qkn = sb("qk_gains", [P, 4, HD])
        head4 = sb("per_head4", [P, 2, 4])
        sink = sb("sinks", [P, AH])
        bmod = sb("bmod_rows", [NMOD, 512])
        col = sb("small", [P, 512])

        def ar(a, *dims):
            n = int(np.prod(dims))
            v = arena[:, a:a + n]
            if len(dims) == 1:
                return v
            names = "abcd"[:len(dims)]
            return v.rearrange(f"p ({' '.join(names)}) -> p {' '.join(names)}", **dict(zip(names[1:], dims[1:])))

        hn, hT = ar(0, NB, D), ar(2048, KD, T)
        Wm, u = ar(0, NB, GH, P), ar(1024, NB, GH, P)
        BTm = ar(2048, 2, NB, 512)
        qk, v_nat, z = ar(4096, 8, T), ar(6144, NB, 512), ar(7168, NB, 512)
        g = ar(8192, GQKV, T)
        convin = ar(11264, GQKV, T + 3)
        bv, DU, PT = ar(11264, NB, GH, P), ar(12288, NB, GH, P), ar(13312, NB, GH, P)
        sq = ar(14372, 8, T)
        X, Y = ar(14372, NB, GH, P), ar(15396, NB, GH, P)
        BT = ar(16420, NB, 512)
        kdec, S1, R = ar(17444, GH, P), ar(17956, GH, P), ar(18468, GH, P)
        o = ar(18980, NB, GH, P)
        mS, mE, mP = ar(20004, 2, 384), ar(20772, 2, 384), ar(21540, 2, 384)
        mixT = ar(22308, 8, T)
        mp = ar(24356, 2, 512)
        csil = ar(25380, KD, 32)
        rows = ar(25636, P)
        padr = ar(25764, 1024)
        gbc = ar(26788, 2, D)
        xslot = ar(0, 4, SLOT)
        h2, h2T = ar(8192, NB, D), ar(10240, KD, T)
        XT = ar(12288, KD, P)
        sg, hid, hidT, CT = ar(13312, FF), ar(13568, FF), ar(13824, FF), ar(14080, NB * P)
        Pd, PdC = ar(14336, NB, EPG, SLOTS), ar(14592, NB, EPG, SLOTS)
        Ysb = ar(14848, 2, 512)
        posall, comball = ar(15872, NB, ROUNDS * NE), ar(16384, NB, ROUNDS * NE)
        ffn_bc, fin_bc = ar(16896, D), ar(17920, D)
        rt = ar(18944, 1024)
        hTx, hTc = ar(0, KD, T), ar(2048, KD, T)
        E2, PT2 = ar(0, 2, 512), ar(1024, 2, 512)
        oT, h3T = ar(2048, KD, T), ar(0, KD, T)
        hnx, hnc = ar(4096, NB, D), ar(6144, NB, D)
        onat = ar(4096, NB, D)
        ctx_raw = ar(8192, NB, D)
        pA = ar(8192, NB, 768)
        pB = ar(9728, NB, 1536)
        cA = ar(12800, NB, 256)
        cB = ar(13312, NB, 1024)
        qaT, kaT, qbT, kbT = ar(15360, 4, T), ar(16384, 1, T), ar(16640, 4, T), ar(17664, 4, T)
        kcaT, kcbT = ar(18688, 1, T), ar(18944, 4, T)
        bias = ar(19968, NB, BH, T)
        t0, t1 = ar(24064, 512), ar(24576, 512)
        fhid, fsg = ar(6144, 2, 512), ar(7168, 2, 512)

        tabs = ar(25088, 4, NB, HD)
        grows = ar(17444, NB, 512)
        PSV = [ctx.enter_context(nc.psum_tensor(f"psv{n}", [P, 512], F32)) for n in range(3)]
        PSA = [ctx.enter_context(nc.psum_tensor(f"psa{n}", [P, 512], F32)) for n in range(3)]
        PSX = [ctx.enter_context(nc.psum_tensor(f"psx{n}", [P, 512], F32)) for n in range(2)]

        rpb_pad = nc.dram_tensor("rpb_pad", (BH, 1024), F32, kind="Internal").ap()

        s_const, s_x, s_rows, s_small, s_wr = map(sem, ("s_const", "s_x", "s_rows", "s_small", "s_wr"))
        s_ctx, s_fin_bc, s_ffn_bc, s_out = map(sem, ("s_ctx", "s_fin_bc", "s_ffn_bc", "s_out"))
        s_pad0, s_pad1, s_pad2, s_toep, s_bias = map(sem, ("s_pad0", "s_pad1", "s_pad2", "s_toep", "s_bias"))
        v_ready, v_free, a_ready, a_free = map(sem, ("v_ready", "v_free", "a_ready", "a_free"))
        x_ready, x_free = sem("x_ready"), sem("x_free")
        rs_req, rs_done, dve_chain, act_chain, pool_chain = map(
            sem, ("rs_req", "rs_done", "dve_chain", "act_chain", "pool_chain"))
        m_used, m_pc = sem("m_used"), sem("m_pc")
        ld = [sem(f"ld{n}") for n in range(NS)]
        mld = [sem(f"mld{n}") for n in range(MU)]
        ld2 = [sem(f"ldb{n}") for n in range(NS)]
        sq_done, hn_done, pad_done, silu_done, conv_done, sqg_done, qkn_done = map(
            sem, ("sq_done", "hn_done", "pad_done", "silu_done", "conv_done", "sqg_done", "qkn_done"))
        g_ready, G_ready, gexp_done, DU_raw, DU_done, csil_ready, csil_done, sp_req, sp_done = map(
            sem, ("g_ready", "G_ready", "gexp_done", "DU_raw", "DU_done", "csil_ready", "csil_done", "sp_req",
                  "sp_done"))
        xy0, btm_done, mv_done, mv_free = map(sem, ("xy0", "btm_done", "mv_done", "mv_free"))
        ms_ready, me_done, mn_done, o_done, xo_done, x3_done = map(
            sem, ("ms_ready", "me_done", "mn_done", "o_done", "xo_done", "x3_done"))
        rt_exp, rt_exped, sel_done, n_ready = map(
            sem, ("rt_exp", "rt_exped", "sel_done", "n_ready"))
        m_pd, m_xtp, m_xt, m_ctp, m_ct, m_gp, m_sg, m_hid, m_htp, m_ht, m_yp, m_y, m_sp, m_s = map(
            sem, ("m_pd", "m_xtp", "m_xt", "m_ctp", "m_ct", "m_gp", "m_sg", "m_hid", "m_htp", "m_ht", "m_yp",
                  "m_y", "m_sp", "m_s"))
        qk2_done, mx_done, sk_req, sk_done, o2_done, o2_free, on_done = map(
            sem, ("qk2_done", "mx_done", "sk_req", "sk_done", "o2_done", "o2_free", "on_done"))
        fg_ready, down_done, fsg_done, fh_done, fd_done, y_done = map(
            sem, ("fg_ready", "down_done", "fsg_done", "fh_done", "fd_done", "y_done"))

        ss = col[:, 0:2]
        ms = col[:, 2:4]
        rstd = col[:, 4:6]
        gab = col[:, 8:24].rearrange("p (b n) -> p b n", b=NB)
        beta = col[:, 24:32].rearrange("p (b n) -> p b n", b=NB)
        gl = col[:, 32:40].rearrange("p (b n) -> p b n", b=NB)
        Gc = col[:, 40:48].rearrange("p (b n) -> p b n", b=NB)
        gam = col[:, 48:56].rearrange("p (b n) -> p b n", b=NB)
        bgam = col[:, 56:60]
        nbeta = col[:, 60:68].rearrange("p (b n) -> p b n", b=NB)
        kd_arg, kd = col[:, 68:72], col[:, 72:76]
        gt = col[:, 76:100].rearrange("p (n b k) -> p n b k", n=3, b=NB)
        alog = col[:, 100:104]
        mmax = col[:, 104:108]
        msum = col[:, 108:112]
        minv = col[:, 112:116]
        ssg = col[:, 116:124]
        msg = col[:, 124:132]
        rsg = col[:, 132:140]
        nm2 = col[:, 144:176]
        rs2 = col[:, 176:208]
        den = col[:, 208:240]
        ssn = col[:, 240:304]
        msn = col[:, 304:368]
        rsn = col[:, 368:432]
        mxt = col[:, 432:434]
        ss5, ms5, rs5 = col[:, 440:444], col[:, 444:448], col[:, 448:452]
        nrm2 = col[:, 456:460]
        trips_f, trips_i = col[:, 464:468], sb("trips", [P, 2], I32)


        def slot_of(n):
            return ring[:, n % NS, :]

        pre = []

        def unit512(lst, w, c0, ncols=512):
            kk = SLOT // ncols
            for k0 in range(0, KD, kk):
                lst.append((ncols, w[k0 * P:(k0 + kk) * P, c0:c0 + ncols].rearrange("(k p) n -> p k n", p=P)))

        w_in = i["w_in"].rearrange("l d n -> (l d) n")
        w_mod = i["w_mod_2"].rearrange("l d n -> (l d) n")
        w_out = i["w_out"].rearrange("l d n -> (l d) n")
        for c0 in (1536, 2048, 2560):
            unit512(pre, w_in, c0)
        pre.append((8, w_in[:, 3584:3592].rearrange("(k p) n -> p k n", p=P)))
        for c0 in (3072, 1024, 0, 512):
            unit512(pre, w_in, c0)
        for n in range(NMOD):
            unit512(pre, w_mod, n * 512)
        for n in range(2):
            unit512(pre, w_out, n * 512)
        NPRE = len(pre)
        mslot = [(NPRE + n) % NS if n < NS else n for n in range(MU)]

        def mview(n):
            return ring[:, mslot[n], :] if n < NS else xslot[:, n - NS, :]

        w_gate = i["w_gate"].rearrange("l g e d f -> (l g e) d f")
        w_up = i["w_up"].rearrange("l g e d f -> (l g e) d f")
        w_down = i["w_down"].rearrange("l g e f d -> (l g e) f d")

        def load_expert_unit(sp, n, e0):
            v = mview(n).rearrange("p (e n) -> p e n", e=EPG)
            if n < KD:
                for w, c0 in ((w_gate, 0), (w_up, FF)):
                    src = w[bass.ds(e0, EPG), n * P:(n + 1) * P, :].rearrange("e p f -> p e f")
                    sp.dma_start(v[:, :, c0:c0 + FF], src).then_inc(mld[n], 16)
            else:
                half, fc = divmod(n - KD, 2)
                src = w_down[bass.ds(e0, EPG), fc * P:(fc + 1) * P, half * 512:half * 512 + 512]
                sp.dma_start(v, src.rearrange("e p d -> p e d")).then_inc(mld[n], 32)

        post = []
        w_in2 = i["w_in_2"].rearrange("l d n -> (l d) n")
        w_out2 = i["w_out_2"].rearrange("l d n -> (l d) n")
        wg2 = i["w_gate_2"].rearrange("l d n -> (l d) n")
        wu2 = i["w_up_2"].rearrange("l d n -> (l d) n")
        wd2 = i["w_down_2"].rearrange("l d n -> (l d) n")
        unit512(post, w_in2, 512, 256)
        for c0 in (0, 1280, 768, 1792):
            unit512(post, w_in2, c0)
        for n in range(2):
            unit512(post, w_out2, n * 512)
        FP = FFN // 256
        for n in range(FP):
            unit512(post, wg2, n * 256, 256)
            unit512(post, wu2, n * 256, 256)
            post.append((D, wd2[n * 256:(n + 1) * 256, :].rearrange("(k p) n -> p k n", p=P)))

        def slot_view(n, ncols, src):
            k = src.shape[1]
            return ring[:, n % NS, 0:k * ncols].rearrange("p (k n) -> p k n", k=k)

        def value_trips(eng):
            return eng.value_load(trips_i[0:1, 1:2], min_val=PASSES, max_val=PASSES * ROUNDS)

        block = ctx.enter_context(nc.Block())
        at = {}
        freed, freed2 = [], []

        @block.tensor
        def _(pe):
            nv = na = nu = 0

            def v_bank():
                nonlocal nv
                nv += 1
                if nv > 3:
                    pe.wait_ge(v_free, nv - 3)
                return PSV[(nv - 1) % 3]

            def a_bank():
                nonlocal na
                na += 1
                if na > 3:
                    pe.wait_ge(a_free, na - 3)
                return PSA[(na - 1) % 3]

            def unit(k=1):
                nonlocal nu
                got = []
                for _ in range(k):
                    pe.wait_ge(ld[nu % NS], 16 * (nu // NS + 1))
                    ncols, src = pre[nu]
                    got.append(slot_view(nu, ncols, src))
                    nu += 1
                return got

            ident = c("ident")

            def turn(src):
                for kp in range(KD // 2):
                    bank = v_bank() if kp % 2 == 0 else a_bank()
                    for kk in range(2):
                        for b in range(NB):
                            k = 2 * kp + kk
                            mm = pe.transpose(bank[:, kk * T + b * P:kk * T + b * P + P],
                                              src[:, b, k * P:(k + 1) * P], ident)
                    mm.then_inc(v_ready if kp % 2 == 0 else a_ready, 1)

            pe.wait_ge(s_const, 16)
            pe.wait_ge(s_rows, 16 * len(ROWS))
            bank = v_bank()
            pe.transpose(bank[:, 0:N_ROWS], rows[0:N_ROWS, :], ident[0:N_ROWS, 0:N_ROWS]).then_inc(v_ready, 1)
            pe.wait_ge(hn_done, 1)
            turn(hn)
            pe.wait_ge(v_free, nv)
            pe.wait_ge(a_free, na)
            def cols_T(units):
                for pair in range(2):
                    bank = a_bank()
                    for cc in range(2):
                        for k in range(KD):
                            w = units[k // 4][:, k % 4, (2 * pair + cc) * P:(2 * pair + cc + 1) * P]
                            mm = pe.matmul(bank[:, cc * T:(cc + 1) * T], w, hT[:, k, :],
                                           start=(k == 0), stop=(k == KD - 1))
                    mm.then_inc(a_ready, 1)
                freed.extend([(a_ready, na)] * 2)

            def rows_nat(units, take, ready, ncols=512):
                for b in range(NB):
                    bank = take()
                    for k in range(KD):
                        per = KD // len(units)
                        mm = pe.matmul(bank[:, 0:ncols], hT[:, k, b * P:(b + 1) * P], units[k // per][:, k % per, :],
                                       start=(k == 0), stop=(k == KD - 1))
                    mm.then_inc(ready, 1)
                freed.extend([(ready, nv if ready is v_ready else na)] * len(units))

            for n in range(3):
                cols_T(unit(2))
            rows_nat(unit(1), v_bank, v_ready, 8)
            rows_nat(unit(2), a_bank, a_ready)
            pe.wait_ge(g_ready, 1)
            bank = v_bank()
            for b in range(NB):
                mm = pe.matmul(bank[:, 4 * b:4 * b + 4], c("upto"), gl[:, b, :], start=True, stop=True)
            mm.then_inc(v_ready, 1)
            rows_nat(unit(2), v_bank, v_ready)
            cols_T(unit(2))
            cols_T(unit(2))
            pe.wait_ge(G_ready, 1)
            for b in range(NB):
                bank = v_bank()
                pe.matmul(bank[:], c("ones"), grows[:, b, :],
                          start=True, stop=True).then_inc(v_ready, 1)
            for n in range(4):
                pe.wait_ge(sqg_done, n // 2 + 1)
                bank = a_bank()
                pe.matmul(bank[:], c("ones"), sq[:, 2 * n:2 * n + 2, :], start=True, stop=True).then_inc(a_ready, 1)
            pe.wait_ge(silu_done, 3)
            pe.wait_ge(qkn_done, 2)
            for b in range(NB):
                bank = v_bank()
                for h in range(GH):
                    mm = pe.transpose(bank[:, h * P:(h + 1) * P], g[:, 8 + h, b * P:(b + 1) * P], ident)
                mm.then_inc(v_ready, 1)
            bank = v_bank()
            for h in range(GH):
                mm = pe.transpose(bank[:, h * P:(h + 1) * P], g[:, 4 + h, 0:P], ident)
            mm.then_inc(v_ready, 1)
            for b in range(NB):
                bank = v_bank()
                for h in range(GH):
                    kt = g[:, 4 + h, b * P:(b + 1) * P]
                    mm = pe.matmul(bank[:, h * P:(h + 1) * P], kt, kt, start=True, stop=True)
                mm.then_inc(v_ready, 1)
                at["BT"] = nv
                bank = v_bank()
                for h in range(GH):
                    mm = pe.matmul(bank[:, h * P:(h + 1) * P], g[:, 4 + h, b * P:(b + 1) * P],
                                   g[:, h, b * P:(b + 1) * P], start=True, stop=True)
                mm.then_inc(v_ready, 1)
            def level_w(n):
                pe.wait_ge(btm_done, n + 1)
                if n == 0:
                    pe.wait_ge(xy0, 2)
                else:
                    pe.wait_ge(a_free, na)
                for b in range(NB):
                    bank = v_bank()
                    for h in range(GH):
                        mm = pe.matmul(bank[:, h * P:(h + 1) * P], BTm[:, n % 2, b, h * P:(h + 1) * P], X[:, b, h, :],
                                       start=True, stop=True)
                    mm.then_inc(v_ready, 1)
                at["W", n] = nv

            def level_xy(n, w_at):
                pe.wait_ge(v_free, w_at)
                for b in range(NB):
                    if n < LEVELS - 1:
                        bank = a_bank()
                        for h in range(GH):
                            mm = pe.matmul(bank[:, h * P:(h + 1) * P], Y[:, b, h, :], Wm[:, b, h, :],
                                           start=True, stop=True)
                        mm.then_inc(a_ready, 1)
                    bank = a_bank()
                    for h in range(GH):
                        mm = pe.matmul(bank[:, h * P:(h + 1) * P], Wm[:, b, h, :], Y[:, b, h, :],
                                       start=True, stop=True)
                    mm.then_inc(a_ready, 1)

            def moba_scores(h):
                if h == 0:
                    pe.wait_ge(a_free, qk_at)
                q0 = MD * (h % 2)
                bank = v_bank()
                for b in range(NB):
                    n = (b + 1) * P
                    mm = pe.matmul(bank[:, b * P:b * P + n], qk[q0:q0 + MD, h // 2, b * P:(b + 1) * P],
                                   qk[q0:q0 + MD, 4 + h // 2, 0:n], start=True, stop=True)
                mm.then_inc(v_ready, 1)

            def moba_turn(h):
                pe.wait_ge(mn_done, h + 1)
                bank = v_bank()
                pe.transpose(bank[:, 0:P], mE[:, h % 2, 0:P], ident)
                pe.transpose(bank[:, P:2 * P], mE[:, h % 2, P:2 * P], ident)
                pe.transpose(bank[:, 2 * P:3 * P], mE[:, h % 2, 2 * P:3 * P], ident).then_inc(v_ready, 1)
                at["E", h] = nv
                return nv

            def moba_values(h, p_at):
                pe.wait_ge(v_free, p_at)
                q0 = MD * (h % 2)
                if h % 2 == 0 and h > 0:
                    pe.wait_ge(mv_free, h // 2)
                bank = PSX[0]
                vs = [v_nat[:, m, h * MD:(h + 1) * MD] for m in range(NB)]
                pe.matmul(bank[q0:q0 + MD, 0:P], vs[0], mP[:, h % 2, 0:P], start=True, stop=True)
                pe.matmul(bank[q0:q0 + MD, P:T], vs[0], mP[:, h % 2, P:T], start=True, stop=False)
                mm = pe.matmul(bank[q0:q0 + MD, P:T], vs[1], mP[:, h % 2, T:T + P], start=False, stop=True)
                mm.then_inc(mv_done, 1)

            def mod_tile(n):
                if n == 0:
                    pe.wait_ge(csil_done, 1)
                units = unit(2)
                bank = PSX[1]
                if n > 0:
                    pe.wait_ge(x_free, n)
                for r in range(2):
                    for j in range(4):
                        k = 4 * r + j
                        mm = pe.matmul(bank[32 * j:32 * j + 32, :], csil[:, k, :], units[r][:, j, :],
                                       start=(r == 0), stop=(r == 1 and j > 0))
                mm = pe.matmul(bank[0:32, :], c("pick")[0:NMOD, 32 * n:32 * n + 32], bmod[:], start=False, stop=True)
                mm.then_inc(x_ready, 1)
                freed.extend([(x_ready, n + 1)] * 2)
                pe.wait_ge(x_free, n + 1)
                bank = v_bank()
                for cc in range(4):
                    mm = pe.matmul(bank[:, 2 * cc:2 * cc + 2], mp[:, n % 2, cc * P:(cc + 1) * P], c("sum2"),
                                   start=True, stop=True)
                mm.then_inc(v_ready, 1)
                if n in (4, 5, 10, 11):
                    bank = v_bank()
                    pe.matmul(bank[:], c("sumrow"), mp[:, n % 2, :], start=True, stop=True).then_inc(v_ready, 1)
                at["mod", n] = nv

            qk_at = na
            prev_p = None
            for n in range(LEVELS + 1):
                if n < LEVELS:
                    level_w(n)
                    w_at = nv
                moba_scores(n)
                if n < LEVELS:
                    level_xy(n, w_at)
                if n > 0:
                    moba_values(n - 1, prev_p)
                prev_p = moba_turn(n)
                mod_tile(n)
            moba_values(MH - 1, prev_p)
            pe.wait_ge(a_free, na)
            bank = v_bank()
            for h in range(GH):
                mm = pe.matmul(bank[:, h * P:(h + 1) * P], Y[:, 0, h, :], bv[:, 0, h, :], start=True, stop=True)
            mm.then_inc(v_ready, 1)
            pe.wait_ge(v_free, nv)
            bank = v_bank()
            for h in range(GH):
                mm = pe.matmul(bank[:, h * P:(h + 1) * P], kdec[:, h, :], u[:, 0, h, :], start=True, stop=True)
            mm.then_inc(v_ready, 1)
            s_at = nv
            bank = v_bank()
            for h in range(GH):
                mm = pe.matmul(bank[:, h * P:(h + 1) * P], PT[:, 0, h, :], u[:, 0, h, :], start=True, stop=True)
            mm.then_inc(v_ready, 1)
            pe.wait_ge(v_free, s_at)
            bank = v_bank()
            for h in range(GH):
                mm = pe.matmul(bank[:, h * P:(h + 1) * P], g[:, 4 + h, P:T], S1[:, h, :], start=True, stop=True)
            mm.then_inc(v_ready, 1)
            ks_at = nv
            bank = v_bank()
            for h in range(GH):
                mm = pe.matmul(bank[:, h * P:(h + 1) * P], g[:, h, P:T], S1[:, h, :], start=True, stop=True)
            mm.then_inc(v_ready, 1)
            mod_tile(8)
            pe.wait_ge(v_free, ks_at)
            bank = v_bank()
            for h in range(GH):
                mm = pe.matmul(bank[:, h * P:(h + 1) * P], Y[:, 1, h, :], R[:, h, :], start=True, stop=True)
            mm.then_inc(v_ready, 1)
            pe.wait_ge(v_free, nv)
            bank = v_bank()
            for h in range(GH):
                mm = pe.matmul(bank[:, h * P:(h + 1) * P], PT[:, 1, h, :], u[:, 1, h, :], start=True, stop=True)
            mm.then_inc(v_ready, 1)
            for n in range(9, NMOD):
                mod_tile(n)
            pe.wait_ge(o_done, 1)
            for hp in range(2):
                bank = v_bank()
                for hh in range(2):
                    for b in range(NB):
                        mm = pe.transpose(bank[:, hh * T + b * P:hh * T + b * P + P], o[:, b, 2 * hp + hh, :], ident)
                mm.then_inc(v_ready, 1)
            pe.wait_ge(v_free, nv)
            pe.wait_ge(mv_free, MH // 2)
            for half in range(2):
                units = unit(2)
                for b in range(NB):
                    bank = v_bank()
                    for k in range(KD):
                        mm = pe.matmul(bank[:], mixT[:, k, b * P:(b + 1) * P], units[k // 4][:, k % 4, :],
                                       start=(k == 0), stop=(k == KD - 1))
                    mm.then_inc(v_ready, 1)
                freed.extend([(v_ready, nv)] * 2)
            at["x1"] = nv
            pe.wait_ge(hn_done, 2)
            turn(h2)
            pe.wait_ge(v_free, nv)
            pe.wait_ge(a_free, na)
            pe.wait_ge(s_wr, 32)
            bank = v_bank()
            for b in range(NB):
                for k in range(KD):
                    mm = pe.matmul(bank[:, b * NR:(b + 1) * NR], h2T[:, k, b * P:(b + 1) * P], wr[:, k, :],
                                   start=(k == 0), stop=(k == KD - 1))
            mm.then_inc(v_ready, 1)
            sel = rt[:, 0:NB * NE].rearrange("p (b e) -> p b e", b=NB)
            pe.wait_ge(sel_done, 1)
            bank = v_bank()
            pe.matmul(bank[:, 0:NE], c("before"), sel[:, 0, :], start=True, stop=True)
            pe.matmul(bank[:, NE:2 * NE], c("ones"), sel[:, 0, :], start=True, stop=False)
            pe.matmul(bank[:, NE:2 * NE], c("before"), sel[:, 1, :], start=False, stop=True)
            pe.matmul(bank[:, 2 * NE:3 * NE], c("ones"), sel[:, 0, :], start=True, stop=False)
            pe.matmul(bank[:, 2 * NE:3 * NE], c("ones"), sel[:, 1, :], start=False, stop=True).then_inc(v_ready, 1)
            pe.wait_ge(v_free, nv)
            pe.wait_ge(n_ready, 1)
            trips = value_trips(pe)
            mXT, mCT, mG, mHT, mY, mSc = PSA[0:2], PSV[0], PSV[1], PSV[2], (PSA[2], PSX[0]), (PSX[1], PSV[0])
            for ahead in (m_gp, m_ctp, m_sp):
                pe.sem_inc(ahead, 1)
            with pe.Fori(0, trips) as t:
                pe.wait_ge(m_pd, t + 1)
                pe.wait_ge(m_xt, 2 * t + 1)
                for half in range(2):
                    for kk in range(4):
                        k = 4 * half + kk
                        for b in range(NB):
                            mm = pe.matmul(mXT[half][:, kk * P:(kk + 1) * P], h2[:, b, k * P:(k + 1) * P],
                                           Pd[:, b, :, :].rearrange("p e s -> p (e s)"), start=(b == 0), stop=(b == 1))
                    mm.then_inc(m_xtp, 1)
                pe.wait_ge(m_s, 4 * t + 1)
                for b in range(NB):
                    mm = pe.transpose(mCT[:, b * P:(b + 1) * P], PdC[:, b, :, :].rearrange("p e s -> p (e s)"), ident)
                mm.then_inc(m_ctp, 1)
                pe.wait_ge(m_xt, 2 * t + 3)
                pe.wait_ge(m_hid, t + 1)
                for n in range(KD):
                    pe.wait_ge(mld[n], 32 * t + 32)
                    w = mview(n).rearrange("p (e n) -> p e n", e=EPG)
                    for e in range(EPG):
                        mm = pe.matmul(mG[32 * e:32 * e + 32, :], XT[:, n, 32 * e:32 * e + 32], w[:, e, :],
                                       start=(n == 0), stop=(n == KD - 1))
                    mm.then_inc(m_used if n < KD - 1 else m_gp, 1)
                pe.wait_ge(m_hid, t + 2)
                pe.wait_ge(m_ht, t + 1)
                for fc in range(2):
                    mm = pe.transpose(mHT[:, fc * P:(fc + 1) * P], hid[:, fc * P:(fc + 1) * P], ident)
                mm.then_inc(m_htp, 1)
                pe.wait_ge(m_ht, t + 2)
                pe.wait_ge(m_y, 2 * t + 1)
                for half in range(2):
                    for fc in range(2):
                        n = KD + 2 * half + fc
                        pe.wait_ge(mld[n], 32 * t + 32)
                        w = mview(n).rearrange("p (e n) -> p e n", e=EPG)
                        for e in range(EPG):
                            mm = pe.matmul(mY[half][32 * e:32 * e + 32, :], hidT[:, fc * P + 32 * e:fc * P + 32 * e + 32],
                                           w[:, e, :], start=(fc == 0), stop=(fc == 1))
                        mm.then_inc(m_used if fc == 0 else m_yp, 1)
                pe.wait_ge(m_ct, t + 1)
                for half in range(2):
                    pe.wait_ge(m_y, 2 * t + 2 + half)
                    for b in range(NB):
                        n = 2 * half + b
                        if n >= 2:
                            pe.wait_ge(m_s, 4 * t + n)
                        pe.matmul(mSc[b][:], CT[:, b * P:(b + 1) * P], Ysb[:, half, :],
                                  start=True, stop=True).then_inc(m_sp, 1)
            pe.wait_ge(m_s, 4 * trips + 1)
            def unit2(n):
                pe.wait_ge(ld2[n % NS], 16 * (n // NS + 1))
                ncols, src = post[n]
                return slot_view(NPRE + n, ncols, src)

            nu2 = 0

            pe.wait_ge(hn_done, 3)
            turn(hnc)
            pe.wait_ge(hn_done, 4)
            turn(hnx)
            pe.wait_ge(v_free, nv)
            pe.wait_ge(a_free, na)
            for n, (k, ncols, with_ctx) in enumerate(((1, 256, True), (2, 512, False), (2, 512, True), (2, 512, False),
                                                      (2, 512, True))):
                units = [unit2(nu2 + m) for m in range(k)]
                nu2 += k
                per = KD // k
                todo = [(hTx, b) for b in range(NB)] + ([(hTc, b) for b in range(NB)] if with_ctx else [])
                for m, (lhs, b) in enumerate(todo):
                    bank = a_bank()
                    for kk in range(KD):
                        mm = pe.matmul(bank[:, 0:ncols], lhs[:, kk, b * P:(b + 1) * P], units[kk // per][:, kk % per, :],
                                       start=(kk == 0), stop=(kk == KD - 1))
                    mm.then_inc(a_ready, 1)
                    at["proj2", n, m] = na
                freed2.extend([(a_ready, na)] * k)
            done = 0

            def turn_heads(src_of, heads, dst_chunks):
                nonlocal done
                for cp in range(0, len(heads), 2):
                    bank = v_bank()
                    for m, cc in enumerate(heads[cp:cp + 2]):
                        for b in range(NB):
                            mm = pe.transpose(bank[:, m * T + b * P:m * T + b * P + P], src_of(b, cc), ident)
                    mm.then_inc(v_ready, 1)

            pe.wait_ge(qk2_done, 1)
            turn_heads(lambda b, cc: pA[:, b, 512:640], [0], None)
            pe.wait_ge(qk2_done, 2)
            turn_heads(lambda b, cc: cA[:, b, 0:128], [0], None)
            pe.wait_ge(qk2_done, 3)
            turn_heads(lambda b, cc: pA[:, b, cc * P:(cc + 1) * P], [0, 1, 2, 3], None)
            pe.wait_ge(qk2_done, 4)
            turn_heads(lambda b, cc: pB[:, b, 512 + cc * P:512 + (cc + 1) * P], [0, 1, 2, 3], None)
            pe.wait_ge(qk2_done, 5)
            turn_heads(lambda b, cc: cB[:, b, cc * P:(cc + 1) * P], [0, 1, 2, 3], None)
            pe.wait_ge(qk2_done, 6)
            turn_heads(lambda b, cc: pB[:, b, cc * P:(cc + 1) * P], [0, 1, 2, 3], None)
            pe.wait_ge(v_free, nv)
            pe.wait_ge(a_free, na)
            pe.wait_ge(s_bias, NB)
            tiles = [(kind, b, h) for kind in range(2) for b in range(NB) for h in range(8)]

            def scores2(kind, b, h):
                bank = a_bank()
                if kind == 0:
                    r0, ch, kch = HD * (h // 4), h % 4, 0
                    qT, kT, kcT, add = qaT, kaT, kcaT, c("window")[:, b * T:(b + 1) * T]
                else:
                    r0, ch, kch = HD * (h % 2), h // 2, h // 2
                    qT, kT, kcT, add = qbT, kbT, kcbT, bias[:, b, h, :]
                q = qT[r0:r0 + HD, ch, b * P:(b + 1) * P]
                pe.matmul(bank[:, 0:T], q, kT[r0:r0 + HD, kch, :], start=True, stop=False)
                pe.matmul(bank[:, 0:T], ident if kind == 0 else c("flip"), add, start=False, stop=True)
                pe.matmul(bank[:, T:2 * T], q, kcT[r0:r0 + HD, kch, :], start=True, stop=True).then_inc(a_ready, 1)

            def turn2(n):
                pe.wait_ge(a_free, a0 + n + 1)
                bank = v_bank()
                for m in range(4):
                    mm = pe.transpose(bank[:, m * P:(m + 1) * P], E2[:, n % 2, m * P:(m + 1) * P], ident)
                mm.then_inc(v_ready, 1)
                at["E2", n] = nv
                return nv

            def values2(n, kind, b, h, p_at):
                pe.wait_ge(v_free, p_at)
                if h == 0 and n >= 16:
                    pe.wait_ge(o2_free, n // 8 - 1)
                bank = PSX[n // 8 % 2]
                if kind == 0:
                    vs = [pA[:, m, 640 + HD * (h // 4):640 + HD * (h // 4) + HD] for m in range(2)]
                    vs += [cA[:, m, 128 + HD * (h // 4):128 + HD * (h // 4) + HD] for m in range(2)]
                else:
                    vs = [pB[:, m, 1024 + h * HD:1024 + (h + 1) * HD] for m in range(2)]
                    vs += [cB[:, m, 512 + h * HD:512 + (h + 1) * HD] for m in range(2)]
                for m in range(4):
                    mm = pe.matmul(bank[:, h * HD:(h + 1) * HD], PT2[:, n % 2, m * P:(m + 1) * P], vs[m],
                                   start=(m == 0), stop=(m == 3))
                mm.then_inc(o2_done, 1)

            at_p = {}
            a0 = na
            at["a0"] = a0
            for n in range(len(tiles) + 2):
                if n < len(tiles):
                    scores2(*tiles[n])
                if 1 <= n <= len(tiles):
                    at_p[n - 1] = turn2(n - 1)
                if n >= 2:
                    values2(n - 2, *tiles[n - 2], at_p[n - 2])
            pe.wait_ge(o2_free, 4)
            pe.wait_ge(hn_done, 5)
            turn(onat)
            pe.wait_ge(v_free, nv)
            pe.wait_ge(a_free, na)
            for half in range(2):
                units = [unit2(nu2), unit2(nu2 + 1)]
                nu2 += 2
                for b in range(NB):
                    bank = v_bank()
                    for k in range(KD):
                        mm = pe.matmul(bank[:], oT[:, k, b * P:(b + 1) * P], units[k // 4][:, k % 4, :],
                                       start=(k == 0), stop=(k == KD - 1))
                    mm.then_inc(v_ready, 1)
                freed2.extend([(v_ready, nv)] * 2)
            pe.wait_ge(v_free, nv)
            pe.wait_ge(hn_done, 6)
            turn(hnx)
            pe.wait_ge(v_free, nv)
            pe.wait_ge(a_free, na)
            acc = (PSX[0], PSX[1], PSV[2], PSA[2])
            GU = ((PSV[0], PSA[0]), (PSV[1], PSA[1]))

            def up(n):
                wg, wu = unit2(nu2 + 3 * n), unit2(nu2 + 3 * n + 1)
                if n >= 2:
                    pe.wait_ge(fh_done, n - 1)
                for m, (w, bank) in enumerate(((wg, GU[n % 2][0]), (wu, GU[n % 2][1]))):
                    for fc in range(2):
                        for k in range(KD):
                            mm = pe.matmul(bank[:, fc * T:(fc + 1) * T], w[:, k, fc * P:(fc + 1) * P], h3T[:, k, :],
                                           start=(k == 0), stop=(k == KD - 1))
                    mm.then_inc(fg_ready, 1)
                freed2.extend([(fg_ready, 2 * n + 1), (fg_ready, 2 * n + 2), (down_done, n + 1)])

            def down(n):
                wd = unit2(nu2 + 3 * n + 2)
                pe.wait_ge(fh_done, n + 1)
                for b in range(NB):
                    for half in range(2):
                        for fc in range(2):
                            mm = pe.matmul(acc[2 * b + half][:], fhid[:, n % 2, fc * T + b * P:fc * T + b * P + P],
                                           wd[:, fc, half * 512:half * 512 + 512],
                                           start=(n == 0 and fc == 0), stop=(n == FP - 1 and fc == 1))
                    if n == FP - 1:
                        mm.then_inc(fd_done, 1)
                if n < FP - 1:
                    mm.then_inc(down_done, 1)

            up(0)
            for n in range(FP):
                if n + 1 < FP:
                    up(n + 1)
                down(n)

        @block.sync
        def _(sp):
            for n, (ncols, src) in enumerate(pre):
                if n >= NS:
                    sp.wait_ge(*freed[n - NS])
                sp.dma_start(slot_view(n, ncols, src), src).then_inc(ld[n % NS], 16)
            for n in range(MU):
                if n < NS:
                    sp.wait_ge(*freed[NPRE - NS + n])
                elif n == NS:
                    sp.wait_ge(v_free, at["x1"])
                load_expert_unit(sp, n, 0)
            sp.wait_ge(n_ready, 1)
            trips = value_trips(sp)

            def expert_slot_free(n, t):
                if n == KD - 1:
                    sp.wait_ge(m_gp, t + 1)
                elif n in (KD + 1, KD + 3):
                    sp.wait_ge(m_yp, 2 * t - 1 if n == KD + 1 else 2 * t)
                else:
                    k = n + 1 if n < KD else (8 if n == KD else 9)
                    sp.wait_ge(m_used, 9 * t + (k - 9))

            first_expert = sp.alloc_register("first_expert")
            with sp.Fori(1, trips) as t:
                sp.reg_mov(first_expert, (t & (PASSES - 1)) * EPG)
                e0 = sp.snap(first_expert, min_val=0, max_val=NE - EPG)
                for n in range(MU):
                    expert_slot_free(n, t)
                    load_expert_unit(sp, n, e0)
            for n, (ncols, src) in enumerate(post):
                if n - NS >= len(freed2):
                    return
                if n < NS:
                    sp.wait_ge(m_gp, trips + 1)
                else:
                    sp.wait_ge(*freed2[n - NS])
                sp.dma_start(slot_view(NPRE + n, ncols, src), src).then_inc(ld2[n % NS], 16)
            sp.wait_ge(y_done, NB)
            sp.dma_start(out.rearrange("a (b p) d -> p (a b) d", p=P), xres[:]).then_inc(s_out, 16)
            sp.wait_ge(s_out, 16)

        @block.scalar
        def _(act):
            na = 0
            nch = 0

            def link(ins):
                nonlocal nch
                nch += 1
                ins.then_inc(act_chain, 1)
                act.wait_ge(act_chain, nch)

            def a_take():
                nonlocal na
                na += 1
                act.wait_ge(a_ready, na)
                return PSA[(na - 1) % 3]

            act.dma_start(C[:], i["consts"]).then_inc(s_const, 16)
            act.dma_start(xres[:], i["x"].rearrange("a (b p) d -> p (a b) d", p=P)).then_inc(s_x, 16)
            v = lambda name: i[name]
            for name, src in (("attn", v("attn_norm").rearrange("l (c p) -> (l c) p", p=P)),
                              ("norm1", v("norm1_g_2").rearrange("l (c p) -> (l c) p", p=P)),
                              ("norm2", v("norm2_g_2").rearrange("l (c p) -> (l c) p", p=P)),
                              ("on_a", v("on_a_2").rearrange("l (c p) -> (l c) p", p=P)),
                              ("on_b", v("on_b_2").rearrange("l (c p) -> (l c) p", p=P)),
                              ("conv", v("conv_w").rearrange("l i (c p) -> (l i c) p", p=P)),
                              ("gdn", v("gdn_norm")),
                              ("c", v("c_2").rearrange("l (c p) -> (l c) p", p=P)),
                              ("c_ctx", v("c_ctx_2").rearrange("(c p) -> c p", p=P))):
                r0 = ROWS[name]
                act.dma_start(rows[r0:r0 + src.shape[0], :], src).then_inc(s_rows, 16)
            act.dma_start(head4[:, 0, :], v("A_log").broadcast_to((P, 4))).then_inc(s_small, 16)
            act.dma_start(head4[:, 1, :], v("dt_bias").broadcast_to((P, 4))).then_inc(s_small, 16)
            for n, name in enumerate(("qn_a_2", "kn_a_2", "qn_b_2", "kn_b_2")):
                act.dma_start(qkn[:, n, :], v(name).broadcast_to((P, HD))).then_inc(s_small, 16)
            act.dma_start(sink[:], v("sink_a_2").broadcast_to((P, AH))).then_inc(s_small, 16)
            act.dma_start(bmod[:], v("b_mod_2").rearrange("l (n c) -> (l n) c", n=NMOD)).then_inc(s_small, 16)
            act.dma_start(wr[:, :, 0:NG], v("w_group").rearrange("l (k p) g -> p (l k) g", p=P)).then_inc(s_wr, 16)
            act.dma_start(wr[:, :, NG:NR], v("w_router").rearrange("l (k p) g -> p (l k) g", p=P)).then_inc(s_wr, 16)

            def squares(src, dst):
                for b in range(NB):
                    act.activation(dst[:, b, :], src[:, b, :], ACT.Square, accum_out=ss[:, b:b + 1]).then_inc(sq_done, 1)

            def turned(dst, scale=None, shift=None):
                for kp in (1, 3):
                    bank = a_take()
                    for kk in range(2):
                        k = 2 * kp + kk
                        b_ = bank[:, kk * T:(kk + 1) * T]
                        if scale is None:
                            ins = act.activation(dst[:, k, :], b_, ACT.Copy)
                        elif shift is None:
                            ins = act.activation(dst[:, k, :], b_, ACT.Copy, scale=scale[:, k:k + 1])
                        else:
                            ins = act.activation(dst[:, k, :], b_, ACT.Identity, scale=scale[:, k:k + 1],
                                                 bias=shift[:, k:k + 1])
                    ins.then_inc(a_free, 1)

            act.wait_ge(s_x, 16)
            squares(xres, hn)
            act.wait_ge(v_free, 1)
            turned(hT, vc[:, ROWS["attn"]:ROWS["attn"] + KD])
            act.wait_ge(s_const, 16)
            act.wait_ge(csil_ready, 1)
            act.activation(csil[:, :, 0], vc[:, ROWS["c"]:ROWS["c"] + KD], ACT.Silu)
            act.activation(csil[:, :, 1], vc[:, ROWS["c_ctx"]:ROWS["c_ctx"] + KD], ACT.Silu).then_inc(csil_done, 1)
            act.wait_ge(pad_done, 1)
            for n in range(6):
                bank = a_take()
                act.activation(convin[:, 2 * n:2 * n + 2, 3:], bank[:].rearrange("p (c t) -> p c t", c=2),
                               ACT.Copy).then_inc(a_free, 1)
            for b in range(NB):
                bank = a_take()
                act.activation(z[:, b, :], bank[:], ACT.Silu).then_inc(a_free, 1)
            act.wait_ge(sp_req, 1)
            link(act.activation(gt[:, 1, :, :], gt[:, 1, :, :], ACT.Exp, scale=-1.0))
            act.activation(gt[:, 1, :, :], gt[:, 1, :, :], ACT.Ln, bias=c("ones")[:, 0:1])
            act.activation(beta[:], gab[:, :, 4:8], ACT.Sigmoid)
            act.activation(alog[:], head4[:, 0, :], ACT.Exp).then_inc(sp_done, 1)
            for n in range(4):
                bank = a_take()
                act.activation(qk[:, 2 * n:2 * n + 2, :], bank[:].rearrange("p (c t) -> p c t", c=2),
                               ACT.Copy).then_inc(a_free, 1)
            for n in range(3):
                act.wait_ge(conv_done, n + 1)
                act.activation(g[:, 4 * n:4 * n + 4, :], g[:, 4 * n:4 * n + 4, :], ACT.Silu).then_inc(silu_done, 1)
            for n in range(2):
                act.wait_ge(silu_done, n + 1)
                act.activation(sq[:, 4 * n:4 * n + 4, :], g[:, 4 * n:4 * n + 4, :], ACT.Square).then_inc(sqg_done, 1)
            act.wait_ge(g_ready, 2)
            act.activation(gam[:], Gc[:], ACT.Exp).then_inc(gexp_done, 1)
            act.wait_ge(DU_raw, 1)
            act.activation(kd[:], kd_arg[:], ACT.Exp).then_inc(gexp_done, 1)
            act.activation(DU[:], DU[:], ACT.Exp).then_inc(DU_done, 1)
            for n in range(4):
                bank = a_take()
                act.activation(sq[:, 2 * n:2 * n + 2, :], bank[:].rearrange("p (c t) -> p c t", c=2), ACT.Sqrt,
                               scale=(float(GD) if n < 2 else 1.0),
                               bias=(c("epsq") if n < 2 else c("epsk"))).then_inc(a_free, 1)
            def level_xy(n):
                for b in range(NB):
                    for dst in ([X] if n < LEVELS - 1 else []) + [Y]:
                        bank = a_take()
                        act.activation(dst[:, b, :, :], bank[:].rearrange("p (h j) -> p h j", h=GH),
                                       ACT.Copy).then_inc(a_free, 1)

            def moba_exp(h):
                act.wait_ge(ms_ready, h + 1)
                if h >= 2:
                    act.wait_ge(v_ready, at["E", h - 2])
                for b in range(NB):
                    s0, n = b * P, (b + 1) * P
                    ins = act.activation(mE[:, h % 2, s0:s0 + n], mS[:, h % 2, s0:s0 + n], ACT.Exp,
                                         bias=mmax[:, 2 * (h % 2) + b:2 * (h % 2) + b + 1],
                                         accum_out=msum[:, 2 * (h % 2) + b:2 * (h % 2) + b + 1])
                ins.then_inc(me_done, 1)

            def x_moba(pair):
                act.wait_ge(mv_done, 2 * pair + 2)
                act.activation(mixT[:, pair, :], PSX[0][:, 0:T], ACT.Copy).then_inc(mv_free, 1)

            def x_mod(n):
                act.wait_ge(x_ready, n + 1)
                if n >= 2:
                    act.wait_ge(v_ready, at["mod", n - 2])
                act.activation(mp[:, n % 2, :], PSX[1][:], ACT.Copy).then_inc(x_free, 1)

            for n in range(LEVELS + 1):
                moba_exp(n)
                if n < LEVELS:
                    level_xy(n)
                if n > 0 and n % 2 == 0:
                    x_moba(n // 2 - 1)
                x_mod(n)
            x_moba(3)
            for n in range(8, NMOD):
                x_mod(n)
            act.wait_ge(v_free, at["x1"])
            act.dma_start(ffn_bc, v("ffn_norm").broadcast_to((P, D))).then_inc(s_ffn_bc, 16)
            act.dma_start(fin_bc, v("final_norm").unsqueeze(0).broadcast_to((P, D))).then_inc(s_fin_bc, 16)
            squares(xres, h2)
            turned(h2T)
            act.wait_ge(rt_exp, 1)
            lg = rt[:, 64:136].rearrange("p (b n) -> p b n", b=NB)
            gp = rt[:, 136:144].rearrange("p (b n) -> p b n", b=NB)
            ing = rt[:, 144:160].rearrange("p (b n) -> p b n", b=NB)
            act.activation(gp[:], gp[:], ACT.Exp)
            act.activation(ing[:], ing[:], ACT.Exp).then_inc(rt_exped, 1)
            act.wait_ge(n_ready, 1)
            trips = value_trips(act)
            mXT, mCT, mG, mY = PSA[0:2], PSV[0], PSV[1], (PSA[2], PSX[0])
            for ahead in (m_xt, m_y):
                act.sem_inc(ahead, 1)
            with act.Fori(0, trips) as t:
                act.wait_ge(m_gp, t + 1)
                for half in range(2):
                    act.wait_ge(m_xtp, 2 * t + 1 + half)
                    act.activation(XT[:, 4 * half:4 * half + 4, :], mXT[half][:].rearrange("p (k s) -> p k s", k=4),
                                   ACT.Copy).then_inc(m_xt, 1)
                act.wait_ge(m_ctp, t + 2)
                act.wait_ge(m_sp, 4 * t + 1)
                act.activation(CT[:], mCT[:, 0:NB * P], ACT.Copy).then_inc(m_ct, 1)
                act.wait_ge(m_gp, t + 2)
                act.wait_ge(m_hid, t + 1)
                act.activation(sg[:], mG[:, 0:FF], ACT.Silu).then_inc(m_sg, 1)
                for half in range(2):
                    act.wait_ge(m_yp, 2 * t + 1 + half)
                    act.activation(Ysb[:, half, :], mY[half][:], ACT.Copy).then_inc(m_y, 1)
            act.wait_ge(m_s, 4 * trips + 1)
            act.dma_start(ctx_raw[:], v("ctx_2").rearrange("a (b p) d -> p (a b) d", p=P)).then_inc(s_ctx, 16)
            act.wait_ge(s_pad2, 16)
            for b in range(NB):
                for r2 in range(2):
                    src = bass.AP(tensor=rpb_pad.tensor, offset=(7 - 2 * b - r2) * GRID,
                                  ap=[[1, GRID], [1024, BH], [1, T]])
                    act.dma_start(bias[64 * r2:64 * r2 + 64, b, :, :], src).then_inc(s_toep, 16)
            squares(xres, hnx)
            act.wait_ge(s_ctx, 16)
            for b in range(NB):
                act.activation(hnc[:, b, :], ctx_raw[:, b, :], ACT.Square, accum_out=ss5[:, b:b + 1]).then_inc(sq_done, 1)
            act.wait_ge(xo_done, NB)
            squares(xres, hnx)
            turned(hTc, modA[:, 1, :], modT[:, 0:KD, 1])
            turned(hTx, modA[:, 0, :], modT[:, 0:KD, 0])
            for n, (dst, ncols) in enumerate([(pA[:, b, 512:768], 256) for b in range(NB)] + [(cA[:, b, :], 256) for b in range(NB)]
                               + [(pA[:, b, 0:512], 512) for b in range(NB)]
                               + [(pB[:, b, 512:1024], 512) for b in range(NB)]
                               + [(cB[:, b, 0:512], 512) for b in range(NB)]
                               + [(pB[:, b, 0:512], 512) for b in range(NB)]
                               + [(pB[:, b, 1024:1536], 512) for b in range(NB)]
                               + [(cB[:, b, 512:1024], 512) for b in range(NB)]):
                bank = a_take()
                src = bank[:, 0:ncols]
                if dst.shape[1] == 512 and n in (4, 5):
                    dst = dst.rearrange("p (c v d) -> p v c d", c=4, v=2)
                    src = src.rearrange("p (v c d) -> p v c d", c=4, v=2)
                act.activation(dst, src, ACT.Copy).then_inc(a_free, 1)
            for n in range(32):
                na += 1
                act.wait_ge(mx_done, n + 1)
                if n >= 2:
                    act.wait_ge(v_ready, at["E2", n - 2])
                act.activation(E2[:, n % 2, :], PSA[(na - 1) % 3][:], ACT.Exp, bias=nm2[:, n:n + 1],
                               accum_out=rs2[:, n:n + 1]).then_inc(a_free, 1)
            act.wait_ge(sk_req, 1)
            act.activation(den[:, 0:16], den[:, 0:16], ACT.Exp).then_inc(sk_done, 1)
            for b in range(NB):
                for kind in range(2):
                    act.wait_ge(on_done, 2 * b + kind + 1)
                    act.activation(oT.rearrange("p k t -> p (k t)")[:, (2 * b + kind) * 512:(2 * b + kind + 1) * 512], onat[:, b, 512 * kind:512 * kind + 512],
                                   ACT.Square, accum_out=ss5[:, 2 * b + kind:2 * b + kind + 1]).then_inc(sq_done, 1)
            turned(oT, vc[:, ROWS["on_a"]:ROWS["on_a"] + KD])
            act.wait_ge(x3_done, 1)
            squares(xres, hnx)
            turned(h3T, modA[:, 2, :], modT[:, 24:32, 0])
            G = (PSV[0], PSV[1])
            for n in range(FP):
                act.wait_ge(fg_ready, 2 * n + 1)
                if n >= 2:
                    act.wait_ge(fh_done, n - 1)
                act.activation(fsg[:, n % 2, :], G[n % 2][:], ACT.Silu).then_inc(fsg_done, 1)

        @block.vector
        def _(dve):
            nv = nch = nrs = nsq = nqk = 0
            vec = nc.vector

            def link(ins):
                nonlocal nch
                nch += 1
                ins.then_inc(dve_chain, 1)
                dve.wait_ge(dve_chain, nch)

            def v_take():
                nonlocal nv
                nv += 1
                dve.wait_ge(v_ready, nv)
                return PSV[(nv - 1) % 3]

            def rsqrt(src, dst, n, scale=None):
                nonlocal nrs
                vec.tensor_scalar(dst, src, 1.0 / n, EPS, ALU.mult, ALU.add).then_inc(rs_req, 1)
                nrs += 1
                dve.wait_ge(rs_done, nrs)
                if scale is not None:
                    link(vec.tensor_scalar(dst, dst, scale, None, ALU.mult))

            def turned(dst, scale=None, shift=None):
                for kp in (0, 2):
                    bank = v_take()
                    for kk in range(2):
                        k = 2 * kp + kk
                        b_ = bank[:, kk * T:(kk + 1) * T]
                        if scale is None:
                            ins = vec.tensor_copy(dst[:, k, :], b_)
                        elif shift is None:
                            ins = vec.tensor_scalar(dst[:, k, :], b_, scale[:, k:k + 1], None, ALU.mult)
                        else:
                            ins = vec.tensor_scalar(dst[:, k, :], b_, scale[:, k:k + 1], shift[:, k:k + 1],
                                                    ALU.mult, ALU.add)
                    ins.then_inc(v_free, 1)

            def normed(src, dst, gain=None, own=False):
                nonlocal nsq
                nsq += 2
                dve.wait_ge(sq_done, nsq)
                rsqrt(ss, rstd, D)
                for b in range(NB):
                    if gain is None:
                        ins = vec.tensor_scalar(dst[:, b, :], src[:, b, :], rstd[:, b:b + 1], None, ALU.mult)
                    else:
                        ins = vec.scalar_tensor_tensor(dst[:, b, :], src[:, b, :], rstd[:, b:b + 1], gain,
                                                       ALU.mult, ALU.mult)
                    if own:
                        ins.then_inc(xo_done, 1)
                if not own:
                    ins.then_inc(hn_done, 1)

            def heads(v, n=GH):
                return v.rearrange("p (h j) -> p h j", h=n)

            def spread(v, n):
                return v.unsqueeze(2).broadcast_to((P, v.shape[1], n))

            bank = v_take()
            vec.tensor_copy(vc[:], bank[:, 0:N_ROWS]).then_inc(v_free, 1)
            normed(xres, hn)
            dve.wait_ge(v_free, 1)
            turned(hT, vc[:, ROWS["attn"]:ROWS["attn"] + KD])
            dve.wait_ge(pad_done, 1)

            def conv(n):
                dve.wait_ge(a_free, 2 + 2 * (n + 1))
                for cc in range(4 * n, 4 * n + 4):
                    w = [vc[:, ROWS["conv"] + r * GQKV + cc:ROWS["conv"] + r * GQKV + cc + 1] for r in range(TAPS)]
                    link(vec.tensor_scalar(g[:, cc, :], convin[:, cc, 0:T], w[0], None, ALU.mult))
                    for r in range(1, TAPS):
                        ins = vec.scalar_tensor_tensor(g[:, cc, :], convin[:, cc, r:r + T], w[r], g[:, cc, :],
                                                       ALU.mult, ALU.add)
                        if r < TAPS - 1 or cc < 4 * n + 3:
                            link(ins)
                ins.then_inc(conv_done, 1)

            conv(0)
            bank = v_take()
            for b in range(NB):
                ins = vec.tensor_copy(gab[:, b, :], bank[:, 8 * b:8 * b + 8]) if False else None
            vec.tensor_copy(gab[:, 0, :], bank[:, 0:8]).then_inc(v_free, 1)
            bank = v_take()
            vec.tensor_copy(gab[:, 1, :], bank[:, 0:8]).then_inc(v_free, 1)
            dve.wait_ge(v_free, nv)
            dve.wait_ge(s_small, 16 * 8)
            dtb = head4[:, 1, :].unsqueeze(1).broadcast_to((P, NB, 4))
            link(vec.tensor_tensor(gt[:, 0], gab[:, :, 0:4], dtb, ALU.add))
            link(vec.scalar_tensor_tensor(gt[:, 1], gt[:, 0], -1.0, gt[:, 0], ALU.mult, ALU.max))
            vec.tensor_scalar(gt[:, 2], gt[:, 0], 0.0, None, ALU.max).then_inc(sp_req, 1)
            dve.wait_ge(sp_req, 1)
            dve.wait_ge(sp_done, 1)
            link(vec.tensor_tensor(gt[:, 0], gt[:, 1], gt[:, 2], ALU.add))
            vec.scalar_tensor_tensor(gl[:], gt[:, 0], -1.0, alog.unsqueeze(1).broadcast_to((P, NB, 4)),
                                     ALU.mult, ALU.mult).then_inc(g_ready, 1)
            dve.wait_ge(g_ready, 1)
            for b in range(NB):
                for h in range(GH):
                    ins = vec.tensor_scalar(grows[:, b, h * P:(h + 1) * P], c("upto"), gl[:, b, h:h + 1], None, ALU.mult)
            ins.then_inc(G_ready, 1)
            conv(1)
            bank = v_take()
            vec.tensor_copy(Gc[:], bank[:, 0:8].rearrange("p (b n) -> p b n", b=NB)).then_inc(v_free, 1)
            dve.wait_ge(v_free, nv)
            vec.tensor_scalar(nbeta[:], beta[:], -1.0, None, ALU.mult).then_inc(g_ready, 1)
            conv(2)
            for b in range(NB):
                bank = v_take()
                vec.tensor_copy(v_nat[:, b, :], bank[:]).then_inc(v_free, 1)
            for b in range(NB):
                bank = v_take()
                if b == 0:
                    dve.wait_ge(g_ready, 2)
                    last = heads(bank[:])[:, :, P - 1]
                    link(vec.tensor_tensor(kd_arg, last, Gc[:, 0, :], ALU.subtract))
                    dve.wait_ge(conv_done, 3)
                for h in range(GH):
                    ins = vec.scalar_tensor_tensor(DU[:, b, h, :], bank[:, h * P:(h + 1) * P], Gc[:, b, h:h + 1],
                                                   c("future"), ALU.subtract, ALU.subtract)
                ins.then_inc(v_free, 1)
            dve.wait_ge(gexp_done, 1)
            vec.scalar_tensor_tensor(bgam, beta[:, 1, :], -1.0, gam[:, 1, :], ALU.mult, ALU.mult).then_inc(DU_raw, 1)
            for n in range(2):
                dve.wait_ge(a_free, 14 + 2 * (n + 1))
                dve.wait_ge(silu_done, n + 1)
                link(vec.reciprocal(sq[:, 4 * n:4 * n + 4, :], sq[:, 4 * n:4 * n + 4, :]))
                vec.tensor_tensor(g[:, 4 * n:4 * n + 4, :], g[:, 4 * n:4 * n + 4, :], sq[:, 4 * n:4 * n + 4, :],
                                  ALU.mult).then_inc(qkn_done, 1)
            for b in range(NB):
                bank = v_take()
                vec.tensor_tensor(bv[:, b], heads(bank[:]), spread(beta[:, b, :], P), ALU.mult).then_inc(v_free, 1)
            bank = v_take()
            dve.wait_ge(gexp_done, 2)
            vec.tensor_tensor(kdec[:], heads(bank[:]), spread(kd, P), ALU.mult).then_inc(v_free, 1)
            dve.wait_ge(DU_done, 1)
            for b in range(NB):
                bank = v_take()
                vec.tensor_tensor(heads(BT[:, b, :]), heads(bank[:]), DU[:, b], ALU.mult).then_inc(v_free, 1)
                bank = v_take()
                vec.tensor_tensor(PT[:, b], heads(bank[:]), DU[:, b], ALU.mult).then_inc(v_free, 1)
            def level_w():
                for b in range(NB):
                    bank = v_take()
                    for h in range(GH):
                        ins = vec.scalar_tensor_tensor(Wm[:, b, h, :], bank[:, h * P:(h + 1) * P],
                                                       nbeta[:, b, h:h + 1], c("ident"), ALU.mult, ALU.add)
                    ins.then_inc(v_free, 1)

            def moba_max(h):
                bank = v_take()
                if h >= 2:
                    dve.wait_ge(me_done, h - 1)
                vec.scalar_tensor_tensor(mS[:, h % 2, :], bank[:, 0:384], MD ** -0.5, c("causal"),
                                         ALU.mult, ALU.add).then_inc(v_free, 1)
                dve.wait_ge(v_free, nv)
                for b in range(NB):
                    s0, n = b * P, (b + 1) * P
                    ins = vec.tensor_reduce(mmax[:, 2 * (h % 2) + b:2 * (h % 2) + b + 1], mS[:, h % 2, s0:s0 + n],
                                            AX, ALU.max, negate=True)
                ins.then_inc(ms_ready, 1)

            def moba_norm(h):
                dve.wait_ge(me_done, h + 1)
                link(vec.reciprocal(minv[:, 2 * (h % 2):2 * (h % 2) + 2], msum[:, 2 * (h % 2):2 * (h % 2) + 2]))
                for b in range(NB):
                    s0, n = b * P, (b + 1) * P
                    ins = vec.tensor_scalar(mE[:, h % 2, s0:s0 + n], mE[:, h % 2, s0:s0 + n],
                                            minv[:, 2 * (h % 2) + b:2 * (h % 2) + b + 1], None, ALU.mult)
                ins.then_inc(mn_done, 1)

            def moba_turned(h):
                bank = v_take()
                if h >= 2:
                    dve.wait_ge(mv_done, h - 1)
                vec.tensor_copy(mP[:, h % 2, :], bank[:, 0:384]).then_inc(v_free, 1)

            def mod_cols(n):
                bank = v_take()
                vec.tensor_copy(modT[:, 4 * n:4 * n + 4, :],
                                bank[:, 0:8].rearrange("p (k r) -> p k r", k=4)).then_inc(v_free, 1)
                if n in (4, 5, 10, 11):
                    which, half = n // 10, n % 2
                    bank = v_take()
                    vec.tensor_copy(gbc[:, which, half * 512:half * 512 + 512], bank[:]).then_inc(v_free, 1)

            for n in range(LEVELS + 1):
                if n < LEVELS:
                    level_w()
                moba_max(n)
                moba_norm(n)
                moba_turned(n)
                mod_cols(n)
            bank = v_take()
            vec.tensor_copy(u[:, 0], heads(bank[:])).then_inc(v_free, 1)
            bank = v_take()
            vec.tensor_copy(S1[:], heads(bank[:])).then_inc(v_free, 1)
            bank = v_take()
            vec.tensor_copy(o[:, 0], heads(bank[:])).then_inc(v_free, 1)
            bank = v_take()
            for h in range(GH):
                ins = vec.scalar_tensor_tensor(R[:, h, :], bank[:, h * P:(h + 1) * P], bgam[:, h:h + 1], bv[:, 1, h, :],
                                               ALU.mult, ALU.add)
            ins.then_inc(v_free, 1)
            bank = v_take()
            vec.tensor_tensor(o[:, 1], heads(bank[:]), spread(gam[:, 1, :], P), ALU.mult).then_inc(v_free, 1)
            mod_cols(8)
            bank = v_take()
            vec.tensor_copy(u[:, 1], heads(bank[:])).then_inc(v_free, 1)
            bank = v_take()
            dve.wait_ge(v_free, nv - 1)
            vec.tensor_tensor(o[:, 1], o[:, 1], heads(bank[:]), ALU.add).then_inc(v_free, 1)
            dve.wait_ge(v_free, nv)
            link(vec.tensor_tensor(Wm[:], o[:], o[:], ALU.mult))
            link(vec.tensor_reduce(ssg, Wm.rearrange("p b h j -> p (b h) j"), AX, ALU.add))
            rsqrt(ssg, rsg, GD)
            ov = o.rearrange("p b h j -> p (b h) j")
            link(vec.tensor_tensor(ov, ov, spread(rsg, P), ALU.mult))
            dve.wait_ge(a_free, 10)
            vec.tensor_tensor(ov, ov, z.rearrange("p b (h j) -> p (b h) j", h=GH), ALU.mult).then_inc(o_done, 1)
            for n in range(9, NMOD):
                mod_cols(n)
            dve.wait_ge(v_free, nv)
            for n, (r, name, c0) in enumerate(((0, "norm1", 8), (1, "norm1", 8), (0, "norm2", 32))):
                vec.scalar_tensor_tensor(modA[:, n, :], modT[:, c0:c0 + KD, r], 1.0,
                                         vc[:, ROWS[name]:ROWS[name] + KD], ALU.add, ALU.mult)
            for hp in range(2):
                bank = v_take()
                vec.tensor_scalar(mixT[:, 4 + 2 * hp:6 + 2 * hp, :], bank[:].rearrange("p (h t) -> p h t", h=2),
                                  vc[:, ROWS["gdn"]:ROWS["gdn"] + 1], None, ALU.mult).then_inc(v_free, 1)
            for half in range(2):
                for b in range(NB):
                    bank = v_take()
                    xv = xres[:, b, half * 512:half * 512 + 512]
                    vec.tensor_tensor(xv, xv, bank[:], ALU.add).then_inc(v_free, 1)
            dve.wait_ge(v_free, nv)
            dve.wait_ge(s_ffn_bc, 16)
            normed(xres, h2, gain=ffn_bc)
            turned(h2T)
            def f(a, *d):
                v_ = rt[:, a:a + int(np.prod(d))]
                if len(d) == 1:
                    return v_
                nm = "abc"[:len(d)]
                return v_.rearrange(f"p ({' '.join(nm)}) -> p {' '.join(nm)}", **dict(zip(nm[1:], d[1:])))

            def over(v, n):
                return v.unsqueeze(2).broadcast_to((P, NB, n))

            sel, lg, gp, ing = f(0, NB, NG, EG), f(64, NB, NR), f(136, NB, NG), f(144, NB, EG)
            gm, gw, gmw, goh = f(160, NB), f(162, NB, NG), f(170, NB), f(172, NB, NG)
            gsum, picked, im = f(180, NB), f(192, NB, NG, EG), f(256, NB)
            m1, w1, wm1, oh1 = f(258, NB), f(260, NB, EG), f(276, NB), f(278, NB, EG)
            rem, m2, w2, wm2, oh2 = f(294, NB, EG), f(310, NB), f(312, NB, EG), f(328, NB), f(330, NB, EG)
            dn, wi, s8, comb = f(346, NB), f(348, NB, EG), f(364, NB, EG), f(380, NB, NG, EG)
            pos, cmax = f(444, NB, NE), f(508, 1)
            tie_g = c("tie")[:, 0:NG].unsqueeze(1).broadcast_to((P, NB, NG))
            tie_e = c("tie")[:, NG:NG + EG].unsqueeze(1).broadcast_to((P, NB, EG))
            bank = v_take()
            vec.tensor_copy(lg[:], bank[:, 0:NB * NR].rearrange("p (b n) -> p b n", b=NB)).then_inc(v_free, 1)
            dve.wait_ge(v_free, nv)
            link(vec.tensor_reduce(gm, lg[:, :, 0:NG], AX, ALU.max))
            link(vec.tensor_tensor(gp[:], lg[:, :, 0:NG], over(gm, NG), ALU.subtract))
            link(vec.tensor_tensor(gw[:], lg[:, :, 0:NG], over(gm, NG), ALU.is_equal))
            link(vec.tensor_tensor(gw[:], gw[:], tie_g, ALU.mult))
            link(vec.tensor_reduce(gmw, gw[:], AX, ALU.max))
            link(vec.tensor_tensor(goh[:], gw[:], over(gmw, NG), ALU.is_equal))
            el = lg[:, :, NG:NR].rearrange("p b (g e) -> p b g e", g=NG)
            link(vec.tensor_tensor(picked[:], el, goh.unsqueeze(3).broadcast_to((P, NB, NG, EG)), ALU.mult))
            link(vec.tensor_reduce(ing[:], picked.rearrange("p b g e -> p b e g"), AX, ALU.add))
            link(vec.tensor_reduce(im, ing[:], AX, ALU.max))
            vec.tensor_tensor(ing[:], ing[:], over(im, EG), ALU.subtract).then_inc(rt_exp, 1)
            dve.wait_ge(rt_exped, 1)
            link(vec.tensor_reduce(gsum, gp[:], AX, ALU.add))
            for m, src, w_, wm, oh in ((m1, ing, w1, wm1, oh1), (m2, rem, w2, wm2, oh2)):
                if src is rem:
                    link(vec.scalar_tensor_tensor(rem[:], oh1[:], -2.0, ing[:], ALU.mult, ALU.add))
                link(vec.tensor_reduce(m, src[:], AX, ALU.max))
                link(vec.tensor_tensor(w_[:], src[:], over(m, EG), ALU.is_equal))
                link(vec.tensor_tensor(w_[:], w_[:], tie_e, ALU.mult))
                link(vec.tensor_reduce(wm, w_[:], AX, ALU.max))
                link(vec.tensor_tensor(oh[:], w_[:], over(wm, EG), ALU.is_equal))
            link(vec.tensor_tensor(dn, m1, m2, ALU.add))
            link(vec.tensor_tensor(dn, dn, gsum, ALU.mult))
            link(vec.reciprocal(dn, dn))
            link(vec.tensor_tensor(m1, m1, dn, ALU.mult))
            link(vec.tensor_tensor(m2, m2, dn, ALU.mult))
            link(vec.tensor_tensor(wi[:], oh1[:], over(m1, EG), ALU.mult))
            link(vec.tensor_tensor(w2[:], oh2[:], over(m2, EG), ALU.mult))
            link(vec.tensor_tensor(wi[:], wi[:], w2[:], ALU.add))
            link(vec.tensor_tensor(s8[:], oh1[:], oh2[:], ALU.add))
            g4 = goh.unsqueeze(3).broadcast_to((P, NB, NG, EG))
            link(vec.tensor_tensor(comb[:], g4, wi.unsqueeze(2).broadcast_to((P, NB, NG, EG)), ALU.mult))
            vec.tensor_tensor(sel[:], g4, s8.unsqueeze(2).broadcast_to((P, NB, NG, EG)), ALU.mult).then_inc(sel_done, 1)
            dve.wait_ge(sel_done, 1)
            bank = v_take()
            self_ = sel.rearrange("p b g e -> p b (g e)")
            link(vec.scalar_tensor_tensor(pos[:], bank[:, 0:2 * NE].rearrange("p (b e) -> p b e", b=NB), 1.0, self_,
                                          ALU.add, ALU.mult))
            vec.tensor_reduce(cmax, bank[:, 2 * NE:3 * NE], AX, ALU.max).then_inc(v_free, 1)
            dve.wait_ge(v_free, nv)
            for r in range(ROUNDS):
                vec.tensor_scalar(posall[:, :, r * NE:(r + 1) * NE], pos[:], -1.0 - SLOTS * r, None, ALU.add)
                vec.tensor_copy(comball[:, :, r * NE:(r + 1) * NE], comb.rearrange("p b g e -> p b (g e)"))
            link(vec.tensor_scalar(trips_i[:, 0:1], cmax, float(SLOTS - 1), None, ALU.add))
            link(vec.tensor_scalar(trips_i[:, 0:1], trips_i[:, 0:1], SLOTS.bit_length() - 1, None, ALU.arith_shift_right))
            vec.tensor_scalar(trips_i[:, 1:2], trips_i[:, 0:1], PASSES.bit_length() - 1, None,
                              ALU.logical_shift_left).then_inc(n_ready, 1)
            dve.wait_ge(n_ready, 1)
            trips = value_trips(dve)
            mG, mHT, mSc = PSV[1], PSV[2], (PSX[1], PSV[0])
            for ahead in (m_hid, m_ht, m_s):
                dve.sem_inc(ahead, 1)
            with dve.Fori(0, trips) as t:
                dve.wait_ge(m_ctp, t + 1)
                now = posall[:, :, bass.ds(t * EPG, EPG)].unsqueeze(3).broadcast_to((P, NB, EPG, SLOTS))
                weight = comball[:, :, bass.ds(t * EPG, EPG)].unsqueeze(3).broadcast_to((P, NB, EPG, SLOTS))
                slots = c("slots").rearrange("p (e s) -> p e s", e=EPG).unsqueeze(1).broadcast_to((P, NB, EPG, SLOTS))
                vec.tensor_tensor(Pd[:], now, slots, ALU.is_equal).then_inc(m_pc, 1)
                dve.wait_ge(m_pc, t + 1)
                vec.tensor_tensor(PdC[:], weight, Pd[:], ALU.mult).then_inc(m_pd, 1)
                dve.wait_ge(m_sg, t + 1)
                vec.tensor_tensor(hid[:], sg[:], mG[:, FF:2 * FF], ALU.mult).then_inc(m_hid, 1)
                dve.wait_ge(m_htp, t + 1)
                vec.tensor_copy(hidT[:], mHT[:, 0:FF]).then_inc(m_ht, 1)
                for half in range(2):
                    for b in range(NB):
                        n = 2 * half + b
                        dve.wait_ge(m_sp, 4 * t + n + 2)
                        dve.wait_ge(m_s, 4 * t + n + 1)
                        xv = xres[:, b, half * 512:half * 512 + 512]
                        vec.tensor_tensor(xv, xv, mSc[b][:], ALU.add).then_inc(m_s, 1)
            dve.wait_ge(m_s, 4 * trips + 1)
            dve.wait_ge(s_fin_bc, 16)
            normed(xres, xres, gain=fin_bc, own=True)
            nsq += 2
            dve.wait_ge(sq_done, nsq)
            rsqrt(ss5[:, 0:2], rs5[:, 0:2], D)
            for b in range(NB):
                ins = vec.tensor_scalar(hnc[:, b, :], ctx_raw[:, b, :], rs5[:, b:b + 1], None, ALU.mult)
            ins.then_inc(hn_done, 1)
            dve.wait_ge(xo_done, NB)
            normed(xres, hnx)
            turned(hTc, modA[:, 1, :], modT[:, 0:KD, 1])
            turned(hTx, modA[:, 0, :], modT[:, 0:KD, 0])
            dve.wait_ge(v_free, nv)
            for n in range(2):
                gain = qkn[:, n, :]
                vec.tensor_tensor(tabs[:, 2 * n], c("cos").rearrange("p (b d) -> p b d", b=NB),
                                  gain.unsqueeze(1).broadcast_to((P, NB, HD)), ALU.mult)
                for w_ in range(2):
                    def part(v_, w__):
                        return v_.rearrange("p (u w s) -> p u w s", u=2, w=2)[:, :, w__, :]
                    for b in range(NB):
                        ins = vec.tensor_tensor(part(tabs[:, 2 * n + 1, b, :], w_), part(c("sin")[:, b * HD:(b + 1) * HD], w_),
                                                part(gain, 1 - w_), ALU.mult)
            link(ins)

            def qk_norm(views, a_tiles, gain, rope, scale=None):
                nonlocal nqk
                nh = views[0].shape[1] // HD
                for b in range(NB):
                    dve.wait_ge(a_free, a_tiles[b])
                    xv = views[b].rearrange("p (h d) -> p h d", h=nh)
                    tt = t0[:, 0:nh * HD].rearrange("p (h d) -> p h d", h=nh)
                    link(vec.tensor_tensor(tt, xv, xv, ALU.mult))
                    link(vec.tensor_reduce(ssn[:, b * nh:(b + 1) * nh], tt, AX, ALU.add))
                rsqrt(ssn[:, 0:2 * nh], rsn[:, 0:2 * nh], HD, scale)
                for b in range(NB):
                    xv = views[b].rearrange("p (h d) -> p h d", h=nh)
                    tt = t0[:, 0:nh * HD].rearrange("p (h d) -> p h d", h=nh)
                    ta = t1[:, 0:nh * HD].rearrange("p (h d) -> p h d", h=nh)
                    link(vec.tensor_tensor(xv, xv, spread(rsn[:, b * nh:(b + 1) * nh], HD), ALU.mult))
                    if not rope:
                        ins = vec.tensor_tensor(xv, xv, qkn[:, gain, :].unsqueeze(1).broadcast_to((P, nh, HD)), ALU.mult)
                    else:
                        link(vec.tensor_tensor(tt, xv, tabs[:, 2 * gain, b, :].unsqueeze(1).broadcast_to((P, nh, HD)),
                                               ALU.mult))
                        for u_ in range(2):
                            for w_ in range(2):
                                a_, o_ = 32 * u_ + 16 * w_, 32 * u_ + 16 * (1 - w_)
                                sn = tabs[:, 2 * gain + 1, b, a_:a_ + 16].unsqueeze(1).broadcast_to((P, nh, 16))
                                ins = vec.tensor_tensor(ta[:, :, a_:a_ + 16], xv[:, :, o_:o_ + 16], sn, ALU.mult)
                        link(ins)
                        ins = vec.tensor_tensor(xv, tt, ta, ALU.add)
                    if b == 0:
                        link(ins)
                ins.then_inc(qk2_done, 1)

            X0 = [(0, 0), (0, 1)]
            qk_norm([pA[:, b, 512:640] for b in range(NB)], [at["proj2", 0, b] for b in range(NB)], 1, True)
            dve.wait_ge(qk2_done, 1)
            qk_norm([cA[:, b, 0:128] for b in range(NB)], [at["proj2", 0, 2 + b] for b in range(NB)], 1, False)
            dve.wait_ge(qk2_done, 2)
            qk_norm([pA[:, b, 0:512] for b in range(NB)], [at["proj2", 1, b] for b in range(NB)], 0, True, 0.125)
            dve.wait_ge(qk2_done, 3)
            qk_norm([pB[:, b, 512:1024] for b in range(NB)], [at["proj2", 2, b] for b in range(NB)], 3, False)
            dve.wait_ge(qk2_done, 4)
            qk_norm([cB[:, b, 0:512] for b in range(NB)], [at["proj2", 2, 2 + b] for b in range(NB)], 3, False)
            dve.wait_ge(qk2_done, 5)
            qk_norm([pB[:, b, 0:512] for b in range(NB)], [at["proj2", 3, b] for b in range(NB)], 2, False, 0.125)
            for dst, chunks in ((kaT, 1), (kcaT, 1), (qaT, 4), (kbT, 4), (kcbT, 4), (qbT, 4)):
                for cp in range(0, chunks, 2):
                    w_ = min(2, chunks - cp)
                    bank = v_take()
                    vec.tensor_copy(dst[:, cp:cp + w_, :],
                                    bank[:, 0:w_ * T].rearrange("p (k t) -> p k t", k=w_)).then_inc(v_free, 1)
            a0 = at["a0"]
            for n in range(34):
                if n < 32:
                    kind, b, h = n // 16, n // 8 % 2, n % 8
                    dve.wait_ge(a_ready, a0 + n + 1)
                    src = PSA[(a0 + n) % 3][:]
                    if kind == 0:
                        link(vec.tensor_reduce(mxt[:, n % 2:n % 2 + 1], src, AX, ALU.max))
                        vec.tensor_scalar(nm2[:, n:n + 1], mxt[:, n % 2:n % 2 + 1], sink[:, h:h + 1], -1.0,
                                          ALU.max, ALU.mult).then_inc(mx_done, 1)
                    else:
                        vec.tensor_reduce(nm2[:, n:n + 1], src, AX, ALU.max, negate=True).then_inc(mx_done, 1)
                if 1 <= n <= 32:
                    bank = v_take()
                    if n >= 3:
                        dve.wait_ge(o2_done, n - 2)
                    vec.tensor_copy(PT2[:, (n - 1) % 2, :], bank[:]).then_inc(v_free, 1)
                if n >= 2 and (n - 2) % 8 == 7:
                    k = (n - 2) // 8
                    dve.wait_ge(o2_done, 8 * (k + 1))
                    vec.tensor_copy(onat[:, k % 2, 512 * (k // 2):512 * (k // 2) + 512], PSX[k % 2][:]).then_inc(o2_free, 1)
            dve.wait_ge(mx_done, 32)
            dve.wait_ge(a_free, a0 + 32)
            vec.tensor_tensor(den[:, 0:16].rearrange("p (b h) -> p b h", b=NB), nm2[:, 0:16].rearrange("p (b h) -> p b h", b=NB),
                              sink[:].unsqueeze(1).broadcast_to((P, NB, AH)), ALU.add).then_inc(sk_req, 1)
            dve.wait_ge(sk_done, 1)
            link(vec.tensor_tensor(den[:, 0:16], den[:, 0:16], rs2[:, 0:16], ALU.add))
            link(vec.tensor_copy(den[:, 16:32], rs2[:, 16:32]))
            link(vec.reciprocal(den, den))
            dve.wait_ge(o2_free, 4)
            for b in range(NB):
                for kind in range(2):
                    ov = onat[:, b, 512 * kind:512 * kind + 512].rearrange("p (h d) -> p h d", h=8)
                    n = kind * 16 + b * 8
                    vec.tensor_tensor(ov, ov, spread(den[:, n:n + 8], HD), ALU.mult).then_inc(on_done, 1)
            nsq += 4
            dve.wait_ge(sq_done, nsq)
            rsqrt(ss5, rs5, 512)
            dve.wait_ge(on_done, 4)
            for b in range(NB):
                for kind in range(2):
                    ov = onat[:, b, 512 * kind:512 * kind + 512]
                    ins = vec.tensor_scalar(ov, ov, rs5[:, 2 * b + kind:2 * b + kind + 1], None, ALU.mult)
            ins.then_inc(hn_done, 1)
            turned(oT, vc[:, ROWS["on_a"]:ROWS["on_a"] + KD])
            for half in range(2):
                for b in range(NB):
                    bank = v_take()
                    xv = xres[:, b, half * 512:half * 512 + 512]
                    vec.tensor_tensor(t0, bank[:], gbc[:, 0, half * 512:half * 512 + 512], ALU.mult).then_inc(v_free, 1)
                    dve.wait_ge(v_free, nv)
                    link(vec.tensor_tensor(xv, xv, t0, ALU.add))
            vec.memset(t1[:, 0:1], 0.0).then_inc(x3_done, 1)
            normed(xres, hnx)
            turned(h3T, modA[:, 2, :], modT[:, 24:32, 0])
            U = (PSA[0], PSA[1])
            for n in range(FP):
                dve.wait_ge(fg_ready, 2 * n + 2)
                dve.wait_ge(fsg_done, n + 1)
                if n >= 2:
                    dve.wait_ge(down_done, n - 1)
                vec.tensor_tensor(fhid[:, n % 2, :], fsg[:, n % 2, :], U[n % 2][:], ALU.mult).then_inc(fh_done, 1)
            acc = (PSX[0], PSX[1], PSV[2], PSA[2])
            for b in range(NB):
                dve.wait_ge(fd_done, b + 1)
                if b > 0:
                    dve.wait_ge(y_done, b)
                for half in range(2):
                    xv = xres[:, b, half * 512:half * 512 + 512]
                    link(vec.tensor_tensor(t0, acc[2 * b + half][:], gbc[:, 1, half * 512:half * 512 + 512], ALU.mult))
                    ins = vec.tensor_tensor(xv, xv, t0, ALU.add)
                    if half == 0:
                        link(ins)
                ins.then_inc(y_done, 1)

        @block.gpsimd
        def _(pool):
            npc = nrs = 0
            pl = nc.gpsimd

            def power(dst):
                nonlocal nrs
                nrs += 1
                pool.wait_ge(rs_req, nrs)
                pl.tensor_tensor(dst, dst, c("neghalf")[:, 0:dst.shape[1]], ALU.pow).then_inc(rs_done, 1)

            pl.memset(csil[:], 0.0).then_inc(csil_ready, 1)
            pl.memset(convin[:, :, 0:TAPS - 1], 0.0).then_inc(pad_done, 1)
            pl.memset(padr[0:BH, :], 0.0).then_inc(s_pad0, 1)
            pool.wait_ge(s_pad0, 1)
            pool.dma_start(padr[0:BH, 48:48 + 15 * 64].rearrange("h (r c) -> h r c", c=64)[:, :, 0:31],
                           i["rpb_b_2"].rearrange("l h r c -> (l h) r c")).then_inc(s_pad1, 16)
            pool.wait_ge(s_pad1, 16)
            pool.dma_start(rpb_pad, padr[0:BH, :]).then_inc(s_pad2, 16)
            pool.wait_ge(s_const, 16)
            power(rstd)
            pool.wait_ge(qkn_done, 2)
            start = c("ident").unsqueeze(1).broadcast_to((P, NB * GH, P))
            for dst in (X, Y):
                pl.tensor_copy(dst.rearrange("p b h j -> p (b h) j"), start).then_inc(xy0, 1)
            for n in range(LEVELS):
                if n == 0:
                    pool.wait_ge(v_free, at["BT"])
                    pool.wait_ge(a_ready, 14)
                if n >= 2:
                    pool.wait_ge(v_ready, at["W", n - 2])
                mask = c(f"level{n}").unsqueeze(1).broadcast_to((P, NB * GH, P))
                pl.tensor_tensor(BTm[:, n % 2].rearrange("p b (h j) -> p (b h) j", h=GH),
                                 BT.rearrange("p b (h j) -> p (b h) j", h=GH), mask, ALU.mult).then_inc(btm_done, 1)
            power(rsg)
            power(rstd)
            power(rstd)
            power(rs5[:, 0:2])
            power(rstd)
            pool.wait_ge(s_toep, 64)
            for b in range(NB):
                mask = c("columns")[:, b * T:(b + 1) * T].unsqueeze(1).broadcast_to((P, BH, T))
                pl.tensor_tensor(bias[:, b], bias[:, b], mask, ALU.add).then_inc(s_bias, 1)
            for nh in (2, 2, 8, 8, 8, 8):
                power(rsn[:, 0:2 * nh])
            power(rs5)
            power(rstd)


_INS = ['x', 'attn_norm', 'w_in', 'conv_w', 'A_log', 'dt_bias', 'gdn_norm', 'w_out', 'ffn_norm', 'w_group',
        'w_router', 'w_gate', 'w_up', 'w_down', 'final_norm', 'c_2', 'ctx_2', 'c_ctx_2', 'w_mod_2', 'b_mod_2',
        'norm1_g_2', 'w_in_2', 'qn_a_2', 'kn_a_2', 'sink_a_2', 'qn_b_2', 'kn_b_2', 'rpb_b_2', 'on_a_2', 'on_b_2',
        'w_out_2', 'norm2_g_2', 'w_gate_2', 'w_up_2', 'w_down_2']


def kernel(**inputs):
    import concourse.bacc as _bacc
    from concourse.bass_utils import run_bass_kernel_spmd as _run

    nc = _bacc.Bacc("TRN2", target_bir_lowering=False, num_devices=1)
    consts, where = constants()
    arrays, aps = {}, {}
    for name in _INS + ["consts"]:
        a = consts if name == "consts" else np.ascontiguousarray(inputs[name])
        arrays[f"in_{name}_dram"] = a
        aps[name] = nc.dram_tensor(f"in_{name}_dram", a.shape, mybir.dt.from_np(a.dtype), kind="ExternalInput").ap()
    out = nc.dram_tensor("out_dram", (1, T, D), F32, kind="ExternalOutput").ap()
    two_blocks(nc, consts, where, aps, out)
    r = _run(nc, [arrays], core_ids=[0])
    return r.results[0]["out_dram"]
```

```python
from contextlib import ExitStack

import concourse.bass as bass
import numpy as np
from concourse import mybir

F32 = mybir.dt.float32
F32R = mybir.dt.float32r
I32 = mybir.dt.int32
ALU = mybir.AluOpType
ACT = mybir.ActivationFunctionType
AX = mybir.AxisListType.X

P = 128
T = 256
NB = T // P
D = 1024
KD = D // P
EPS = 1e-6
FIRST = 144
BIG = 1e30

MH, MD = 8, 64
GH, GD = 4, 128
TAPS = 4
GQKV = 3 * GH
W_IN = 3592
NG, EG, NE, FF = 4, 8, 32, 256
NR = NG + NE
SLOTS = 32
EPG = P // SLOTS
ROUNDS = T // SLOTS
PASSES = NE // EPG

GRID = 64
AH, BH, HD = 8, 8, 64
CTX = 256
IN2 = 2304
FFN = 2816
NMOD = 6 * D // 512

SLOT = 2048
NS = 8
MU = 12

LEVELS = 7

OUTPUTS_AT, SINK_AT, DIVIDE_AT, SQUARES_AT, NORM_AT = 19, 20, 22, 24, 26

MOD_AT = {"rows": (0, 1), "norms": (2, 3, 4, 5, 6), "chunk": (7,), "tail": (8, 9), "mixed": (10, 11)}


def constants():
    cols, at = [], {}

    def put(name, a):
        full = np.zeros((P, a.shape[1]), np.float32)
        full[:a.shape[0]] = a
        at[name] = (sum(c.shape[1] for c in cols), a.shape[1])
        cols.append(full)

    i = np.arange(P)
    put("ident", np.eye(P))
    put("neghalf", np.full((P, 16), -0.5))
    put("upto", (i[:, None] <= i[None, :]).astype(np.float64))
    put("before", (i[:, None] < i[None, :]).astype(np.float64))
    put("ones", np.ones((P, P)))
    put("future", np.where(i[None, :] < i[:, None], BIG, 0.0))
    key = np.arange(T)
    put("causal", np.concatenate([np.where(i[None, :] > i[:, None], -BIG, 0.0),
                                  np.where(key[None, :] > P + i[:, None], -BIG, 0.0)], 1))
    for n in range(LEVELS):
        b = 1 << n
        put(f"level{n}", ((i[:, None] // (2 * b) == i[None, :] // (2 * b)) & (i[:, None] // b % 2 == 0)
                          & (i[None, :] // b % 2 == 1)).astype(np.float64))
    put("slots", np.tile(np.tile(np.arange(SLOTS), EPG)[None], (P, 1)))
    put("sum2", np.stack([(i % 32 == 0), (i % 32 == 1)], 1).astype(np.float64))
    put("sumrow", np.tile((i % 32 == 0)[:, None], (1, P)).astype(np.float64))
    q = np.arange(T)
    near = np.where(np.abs(key[None] - q[:, None]) <= 128, 0.0, -BIG)
    put("window", near.reshape(NB, P, T).transpose(1, 0, 2).reshape(P, NB * T))
    qc, kc = q % GRID, key % GRID
    cs = np.clip(qc - 8, 0, GRID - 16)
    ok = (kc[None] >= cs[:, None]) & (kc[None] < cs[:, None] + 16)
    ok = ok.reshape(T // GRID, GRID, T)[:, ::-1].reshape(T, T)
    flip = np.kron(np.eye(P // GRID), np.eye(GRID)[::-1])
    put("flip", flip)
    put("columns", np.where(ok, 0.0, -BIG).reshape(NB, P, T).transpose(1, 0, 2).reshape(P, NB * T))
    inv = (1.0 / (np.float32(10000.0) ** (np.arange(16, dtype=np.float32) / np.float32(16)))).astype(np.float32)
    ang = lambda pos: pos.astype(np.float32)[:, None] * inv[None]
    r, c = ang(q // GRID), ang(q % GRID)
    cos = np.concatenate([np.cos(r), np.cos(r), np.cos(c), np.cos(c)], 1)
    sin = np.concatenate([-np.sin(r), np.sin(r), -np.sin(c), np.sin(c)], 1)
    put("cos", cos.reshape(NB, P, HD).transpose(1, 0, 2).reshape(P, NB * HD))
    put("sin", sin.reshape(NB, P, HD).transpose(1, 0, 2).reshape(P, NB * HD))
    put("tie", np.tile(np.concatenate([np.arange(NG, 0, -1), np.arange(EG, 0, -1)])[None], (P, 1)))
    put("epsq", np.full((P, 1), GD * EPS))
    put("epsk", np.full((P, 1), EPS))
    return np.ascontiguousarray(np.concatenate(cols, 1).astype(np.float32)), at


ROWS = {}
_n = 0
for _name, _k in (("attn", 8), ("norm1", 8), ("norm2", 8), ("on_a", 4), ("on_b", 4), ("conv", TAPS * GQKV),
                  ("gdn", 1), ("c", 8), ("c_ctx", 8)):
    ROWS[_name] = _n
    _n += _k
N_ROWS = _n


def two_blocks(nc, consts, where, i, out):
    with ExitStack() as ctx:
        def sb(name, shape, dt=F32):
            return ctx.enter_context(nc.sbuf_tensor(name, shape, dt))

        def sem(name):
            return ctx.enter_context(nc.semaphore(name))

        C = sb("consts", [P, consts.shape[1]])

        def c(name):
            a, n = where[name]
            return C[:, a:a + n]

        ring = sb("ring", [P, NS, SLOT])
        xres = sb("residual", [P, NB, D])
        parts, end = {}, 0
        with ExitStack() as place:
            for name, first, shape in (("hidden_parts", 2048, [P, 2, 2, 512]), ("unit_parts0", 8192, [P, 2, SLOT]),
                                       ("unit_parts1", 13824, [P, 2, SLOT]), ("column_parts", 17920, [P, 2, KD, T]),
                                       ("unit_parts2", 22016, [P, 2, SLOT])):
                if first > end:
                    place.enter_context(nc.sbuf_tensor(f"before_{name}", [P, first - end], F32))
                parts[name] = place.enter_context(nc.sbuf_tensor(name, shape, F32R))
                end = first + int(np.prod(shape[1:]))
        hid_parts, col_parts = parts["hidden_parts"], parts["column_parts"]
        unit_parts = [parts[f"unit_parts{n}"] for n in range(3)]
        arena = sb("arena", [P, 28836])
        vc = sb("vec_cols", [P, N_ROWS])
        modT = sb("mod_cols", [P, 48, 2])
        modA = sb("mod_gains", [P, 3, KD])
        wr = sb("w_route", [P, KD, NR])
        qkn = sb("qk_gains", [P, 4, HD])
        head4 = sb("per_head4", [P, 2, 4])
        sink = sb("sinks", [P, AH])
        brow = sb("bmod_rows", [6 * KD, P])
        bcol = sb("bmod_cols", [P, 6 * KD])
        col = sb("small", [P, 512])

        def ar(a, *dims):
            n = int(np.prod(dims))
            v = arena[:, a:a + n]
            if len(dims) == 1:
                return v
            names = "abcd"[:len(dims)]
            return v.rearrange(f"p ({' '.join(names)}) -> p {' '.join(names)}", **dict(zip(names[1:], dims[1:])))

        hn, hT = ar(0, NB, D), ar(2048, KD, T)
        Wm, u = ar(0, NB, GH, P), ar(1024, NB, GH, P)
        BTm = ar(2048, 2, NB, 512)
        qk, v_nat, z = ar(4096, 8, T), ar(6144, NB, 512), ar(7168, NB, 512)
        g = ar(8192, GQKV, T)
        convin = ar(11264, GQKV, T + 3)
        bv, DU, PT = ar(11264, NB, GH, P), ar(12288, NB, GH, P), ar(13312, NB, GH, P)
        sq = ar(14372, 8, T)
        X, Y = ar(14372, NB, GH, P), ar(15396, NB, GH, P)
        BT = ar(16420, NB, 512)
        kdec, S1, R = ar(17444, GH, P), ar(17956, GH, P), ar(18468, GH, P)
        o = ar(18980, NB, GH, P)
        mS, mE, mP = ar(20004, 2, 384), ar(20772, 2, 384), ar(21540, 2, 384)
        mixT = ar(22308, 8, T)
        mp = ar(24356, 2, 512)
        csil = ar(25380, KD, 32)
        rows = ar(25636, P)
        padr = ar(25764, 1024)
        gbc = ar(26788, 2, D)
        xslot = ar(0, 4, SLOT)
        h2, h2T = ar(8192, NB, D), ar(10240, KD, T)
        XT = ar(12288, KD, P)
        sg, hid, hidT, CT = ar(13312, FF), ar(13568, FF), ar(13824, FF), ar(14080, NB * P)
        Pd, PdC = ar(14336, NB, EPG, SLOTS), ar(14592, NB, EPG, SLOTS)
        Ysb = ar(14848, 2, 512)
        posall, comball = ar(15872, NB, ROUNDS * NE), ar(16384, NB, ROUNDS * NE)
        ffn_bc, fin_bc = ar(16896, D), ar(17920, D)
        rt = ar(18944, 1024)
        sqc = ar(14372, NB, D)
        hnc, hTc = ar(20004, NB, D), ar(22180, KD, T)
        cA = ar(24228, NB, 256)
        cB = ar(24740, NB, 1024)
        hTx = ar(0, KD, T)
        E2, PT2 = ar(20004, 4, 512), ar(22052, 4, 512)
        sqo = ar(14336, 2, 512)
        oT, h3T = ar(2048, KD, T), ar(0, KD, T)
        hnx = ar(4096, NB, D)
        onat = ar(4096, NB, D)
        pA = ar(8192, NB, 768)
        pB = ar(9728, NB, 1536)
        qaT, kaT, qbT, kbT = ar(15360, 4, T), ar(16384, 1, T), ar(16640, 4, T), ar(17664, 4, T)
        kcaT, kcbT = ar(18688, 1, T), ar(18944, 4, T)
        bias = (ar(6144, BH, T), ar(2048, BH, T))
        t0, t1 = ar(12800, 512), ar(13312, 512)
        fhid, fsg = ar(6144, 2, 512), ar(7168, 2, 512)

        tabs = ar(13824, 4, NB, HD)
        grows = ar(17444, NB, 512)
        PSV = [ctx.enter_context(nc.psum_tensor(f"psv{n}", [P, 512], F32)) for n in range(3)]
        PSA = [ctx.enter_context(nc.psum_tensor(f"psa{n}", [P, 512], F32)) for n in range(3)]
        PSX = [ctx.enter_context(nc.psum_tensor(f"psx{n}", [P, 512], F32)) for n in range(2)]

        rpb_pad = nc.dram_tensor("rpb_pad", (BH, 1024), F32, kind="Internal").ap()

        s_ident, s_const, s_gain, s_gate, s_rows, s_small, s_wr = map(sem, ("s_ident", "s_const", "s_gain", "s_gate", "s_rows", "s_small", "s_wr"))
        s_x = [sem(f"s_x{b}") for b in range(NB)]
        s_ctx, s_fin_bc, s_ffn_bc, s_out = map(sem, ("s_ctx", "s_fin_bc", "s_ffn_bc", "s_out"))
        s_pad0, s_pad1, s_pad2, s_toep, s_bias = map(sem, ("s_pad0", "s_pad1", "s_pad2", "s_toep", "s_bias"))
        v_ready, v_free, a_ready, a_free = map(sem, ("v_ready", "v_free", "a_ready", "a_free"))
        x_ready, x_free = sem("x_ready"), sem("x_free")
        rs_req, rs_done, dve_chain, act_chain, pool_chain = map(
            sem, ("rs_req", "rs_done", "dve_chain", "act_chain", "pool_chain"))
        m_used, m_pc = sem("m_used"), sem("m_pc")
        ld = [sem(f"ld{n}") for n in range(NS)]
        mld = [sem(f"mld{n}") for n in range(MU)]
        ld2 = [sem(f"ldb{n}") for n in range(NS)]
        sq_done, hn_done, pad_done, silu_done, conv_done, sqg_done, qkn_done = map(
            sem, ("sq_done", "hn_done", "pad_done", "silu_done", "conv_done", "sqg_done", "qkn_done"))
        g_ready, G_ready, gexp_done, DU_raw, DU_done, csil_ready, csil_done, sp_req, sp_done = map(
            sem, ("g_ready", "G_ready", "gexp_done", "DU_raw", "DU_done", "csil_ready", "csil_done", "sp_req",
                  "sp_done"))
        xy0, btm_done, mv_done, mv_free = map(sem, ("xy0", "btm_done", "mv_done", "mv_free"))
        ms_ready, me_done, mn_done, o_done, xo_done, x3_done = map(
            sem, ("ms_ready", "me_done", "mn_done", "o_done", "xo_done", "x3_done"))
        rt_exp, rt_exped, sel_done, n_ready = map(
            sem, ("rt_exp", "rt_exped", "sel_done", "n_ready"))
        m_pd, m_xtp, m_xt, m_ctp, m_ct, m_gp, m_sg, m_hid, m_htp, m_ht, m_yp, m_y, m_sp, m_s = map(
            sem, ("m_pd", "m_xtp", "m_xt", "m_ctp", "m_ct", "m_gp", "m_sg", "m_hid", "m_htp", "m_ht", "m_yp",
                  "m_y", "m_sp", "m_s"))
        s2_done, e2_done, t2_done, p2_done, on_sq = map(sem, ("s2_done", "e2_done", "t2_done", "p2_done", "on_sq"))
        hi_done, lo_done, h3_split = map(sem, ("hi_done", "lo_done", "h3_split"))
        qk2_done, mx_done, sk_req, sk_done, o2_done, o2_free, on_done = map(
            sem, ("qk2_done", "mx_done", "sk_req", "sk_done", "o2_done", "o2_free", "on_done"))
        fg_ready, down_done, fsg_done, fh_done, fd_done, y_done = map(
            sem, ("fg_ready", "down_done", "fsg_done", "fh_done", "fd_done", "y_done"))

        ss = col[:, 0:2]
        ms = col[:, 2:4]
        rstd = col[:, 4:6]
        gab = col[:, 8:24].rearrange("p (b n) -> p b n", b=NB)
        beta = col[:, 24:32].rearrange("p (b n) -> p b n", b=NB)
        gl = col[:, 32:40].rearrange("p (b n) -> p b n", b=NB)
        Gc = col[:, 40:48].rearrange("p (b n) -> p b n", b=NB)
        gam = col[:, 48:56].rearrange("p (b n) -> p b n", b=NB)
        bgam = col[:, 56:60]
        nbeta = col[:, 60:68].rearrange("p (b n) -> p b n", b=NB)
        kd_arg, kd = col[:, 68:72], col[:, 72:76]
        gt = col[:, 76:100].rearrange("p (n b k) -> p n b k", n=3, b=NB)
        alog = col[:, 100:104]
        mmax = col[:, 104:108]
        msum = col[:, 108:112]
        minv = col[:, 112:116]
        ssg = col[:, 116:124]
        msg = col[:, 124:132]
        rsg = col[:, 132:140]
        nm2 = col[:, 144:176]
        rs2 = col[:, 176:208]
        den = col[:, 208:240]
        ssn = col[:, 240:304]
        msn = col[:, 304:368]
        rsn = col[:, 368:432]
        mxt = col[:, 432:434]
        ss5, ms5, rs5 = col[:, 440:444], col[:, 444:448], col[:, 448:452]
        nrm2 = col[:, 456:460]
        trips_f, trips_i = col[:, 464:468], sb("trips", [P, 2], I32)


        def slot_of(n):
            return ring[:, n % NS, :]

        pre = []

        def unit512(lst, w, c0, ncols=512):
            kk = SLOT // ncols
            for k0 in range(0, KD, kk):
                lst.append((ncols, w[k0 * P:(k0 + kk) * P, c0:c0 + ncols].rearrange("(k p) n -> p k n", p=P)))

        w_in = i["w_in"].rearrange("l d n -> (l d) n")
        w_mod = i["w_mod_2"].rearrange("l d n -> (l d) n")
        w_out = i["w_out"].rearrange("l d n -> (l d) n")
        for c0 in (1536, 2048, 2560):
            unit512(pre, w_in, c0)
        pre.append((8, w_in[:, 3584:3592].rearrange("(k p) n -> p k n", p=P)))
        for c0 in (3072, 1024, 0, 512):
            unit512(pre, w_in, c0)
        for n in range(MOD_AT["mixed"][0]):
            unit512(pre, w_mod, n * 512)
        for n in range(2):
            unit512(pre, w_out, n * 512)
        for n in MOD_AT["mixed"]:
            unit512(pre, w_mod, n * 512)
        w_in2 = i["w_in_2"].rearrange("l d n -> (l d) n")
        unit512(pre, w_in2, 512, 256)
        unit512(pre, w_in2, 1280)
        NPRE = len(pre)
        mslot = [(NPRE + n) % NS if n < NS else n for n in range(MU)]

        def mod_bank(n):
            return PSX[1] if n == MOD_AT["chunk"][0] else PSX[n % 2]

        def mview(n):
            return ring[:, mslot[n], :] if n < NS else xslot[:, n - NS, :]

        w_gate = i["w_gate"].rearrange("l g e d f -> (l g e) d f")
        w_up = i["w_up"].rearrange("l g e d f -> (l g e) d f")
        w_down = i["w_down"].rearrange("l g e f d -> (l g e) f d")

        def load_expert_unit(sp, n, e0):
            v = mview(n).rearrange("p (e n) -> p e n", e=EPG)
            if n < KD:
                for w, c0 in ((w_gate, 0), (w_up, FF)):
                    src = w[bass.ds(e0, EPG), n * P:(n + 1) * P, :].rearrange("e p f -> p e f")
                    sp.dma_start(v[:, :, c0:c0 + FF], src).then_inc(mld[n], 16)
            else:
                half, fc = divmod(n - KD, 2)
                src = w_down[bass.ds(e0, EPG), fc * P:(fc + 1) * P, half * 512:half * 512 + 512]
                sp.dma_start(v, src.rearrange("e p d -> p e d")).then_inc(mld[n], 32)

        post = []
        w_out2 = i["w_out_2"].rearrange("l d n -> (l d) n")
        wg2 = i["w_gate_2"].rearrange("l d n -> (l d) n")
        wu2 = i["w_up_2"].rearrange("l d n -> (l d) n")
        wd2 = i["w_down_2"].rearrange("l d n -> (l d) n")
        unit512(post, w_in2, 1792)
        unit512(post, w_in2, 512, 256)
        for c0 in (0, 1280, 768, 1792):
            unit512(post, w_in2, c0)
        for n in range(2):
            unit512(post, w_out2, n * 512)
        FP = FFN // 256
        for n in range(FP):
            unit512(post, wg2, n * 256, 256)
            unit512(post, wu2, n * 256, 256)
            post.append((D, wd2[n * 256:(n + 1) * 256, :].rearrange("(k p) n -> p k n", p=P)))

        def slot_view(n, ncols, src):
            k = src.shape[1]
            return ring[:, n % NS, 0:k * ncols].rearrange("p (k n) -> p k n", k=k)

        def value_trips(eng):
            return eng.value_load(trips_i[0:1, 1:2], min_val=PASSES, max_val=PASSES * ROUNDS)

        tiles2 = [(b, kind, h) for b in range(NB) for kind in range(2)
                  for h in ((0, 4, 1, 5, 2, 6, 3, 7) if kind == 0 else range(8))]
        SB, TB = (PSA[0], PSA[1], PSA[2], PSV[2]), (PSV[0], PSV[1])
        NT = len(tiles2)

        def stat(n):
            b, kind, h = tiles2[n]
            return kind * 16 + b * 8 + h

        mlp = [(0, 0), (1, 0)]
        for n in range(FP):
            mlp += [(m, n + 1) for m in range(2) if n + 1 < FP] + [(2, n)]

        def mlp_used(q):
            kind, n = mlp[q]
            return (down_done, n + 1) if kind == 2 else (fg_ready, 2 * n + 1 + kind)

        def mlp_behind(n):
            return [q for q in range(3 * n + 2 if n else 3, 3 * n + 5) if q < len(mlp)]

        block = ctx.enter_context(nc.Block())
        at = {}
        freed, freed2 = [], []

        @block.tensor
        def _(pe):
            def split_product(o, l, r, first, last):
                pe.matmul(o, l[0], r[0], start=first, stop=False)
                pe.matmul(o, l[1], r[0], start=False, stop=False)
                return pe.matmul(o, l[0], r[1], start=False, stop=last)

            nv = na = nu = 0

            def v_bank():
                nonlocal nv
                nv += 1
                if nv > 3:
                    pe.wait_ge(v_free, nv - 3)
                return PSV[(nv - 1) % 3]

            def a_bank():
                nonlocal na
                na += 1
                if na > 3:
                    pe.wait_ge(a_free, na - 3)
                return PSA[(na - 1) % 3]

            def unit(k=1):
                nonlocal nu
                got = []
                for _ in range(k):
                    pe.wait_ge(ld[nu % NS], 16 * (nu // NS + 1))
                    ncols, src = pre[nu]
                    got.append(slot_view(nu, ncols, src))
                    nu += 1
                return got

            ident = c("ident")

            def turn(src):
                for kp in range(KD // 2):
                    bank = v_bank() if kp % 2 == 0 else a_bank()
                    for kk in range(2):
                        for b in range(NB):
                            k = 2 * kp + kk
                            mm = pe.transpose(bank[:, kk * T + b * P:kk * T + b * P + P],
                                              src[:, b, k * P:(k + 1) * P], ident)
                    mm.then_inc(v_ready if kp % 2 == 0 else a_ready, 1)

            pe.wait_ge(s_ident, 16)
            pe.wait_ge(s_gain, 16)
            bank = v_bank()
            pe.transpose(bank[:, 0:KD], rows[0:KD, :], ident[0:KD, 0:KD]).then_inc(v_ready, 1)
            pe.wait_ge(hn_done, 1)
            turn(hn)
            pe.wait_ge(v_free, nv)
            pe.wait_ge(a_free, na)
            def cols_T(units):
                for pair in range(2):
                    bank = a_bank()
                    for cc in range(2):
                        for k in range(KD):
                            w = units[k // 4][:, k % 4, (2 * pair + cc) * P:(2 * pair + cc + 1) * P]
                            mm = pe.matmul(bank[:, cc * T:(cc + 1) * T], w, hT[:, k, :],
                                           start=(k == 0), stop=(k == KD - 1))
                    mm.then_inc(a_ready, 1)
                freed.extend([(a_ready, na)] * 2)

            def rows_nat(units, take, ready, ncols=512):
                for b in range(NB):
                    bank = take()
                    for k in range(KD):
                        per = KD // len(units)
                        mm = pe.matmul(bank[:, 0:ncols], hT[:, k, b * P:(b + 1) * P], units[k // per][:, k % per, :],
                                       start=(k == 0), stop=(k == KD - 1))
                    mm.then_inc(ready, 1)
                freed.extend([(ready, nv if ready is v_ready else na)] * len(units))

            def mod_products(n):
                if n == 0:
                    pe.wait_ge(csil_done, 1)
                if n == MOD_AT["tail"][0]:
                    pe.wait_ge(mv_free, MH // 2)
                units = unit(2)
                bank = mod_bank(n)
                before = [m for m in range(n) if mod_bank(m) is bank]
                if before:
                    pe.wait_ge(x_free, before[-1] + 1)
                for r in range(2):
                    for j in range(4):
                        k = 4 * r + j
                        mm = pe.matmul(bank[32 * j:32 * j + 32, :], csil[:, k, :], units[r][:, j, :],
                                       start=(r == 0), stop=(r == 1))
                mm.then_inc(x_ready, 1)
                freed.extend([(x_ready, n + 1)] * 2)

            def mod_sums(n):
                pe.wait_ge(x_free, n + 1)
                bank = v_bank()
                for cc in range(4):
                    mm = pe.matmul(bank[:, 2 * cc:2 * cc + 2], mp[:, n % 2, cc * P:(cc + 1) * P], c("sum2"),
                                   start=True, stop=True)
                mm.then_inc(v_ready, 1)
                if n in (4, 5, 10, 11):
                    bank = v_bank()
                    pe.matmul(bank[:], c("sumrow"), mp[:, n % 2, :], start=True, stop=True).then_inc(v_ready, 1)
                at["mod", n] = nv

            def mod_tiles(where):
                tiles = MOD_AT[where]
                for m, n in enumerate(tiles):
                    mod_products(n)
                    if m > 0:
                        mod_sums(n - 1)
                mod_sums(tiles[-1])

            for n in range(3):
                cols_T(unit(2))
                if n == 0:
                    pe.wait_ge(s_rows, 16 * len(ROWS))
                    bank = v_bank()
                    pe.transpose(bank[:, 0:N_ROWS], rows[0:N_ROWS, :], ident[0:N_ROWS, 0:N_ROWS])
                    pe.transpose(bank[:, N_ROWS:N_ROWS + 6 * KD], brow[:],
                                 ident[0:6 * KD, 0:6 * KD]).then_inc(v_ready, 1)
            rows_nat(unit(1), v_bank, v_ready, 8)
            rows_nat(unit(2), a_bank, a_ready)
            rows_nat(unit(2), v_bank, v_ready)
            pe.wait_ge(s_const, 16)
            pe.wait_ge(g_ready, 1)
            bank = v_bank()
            for b in range(NB):
                mm = pe.matmul(bank[:, 4 * b:4 * b + 4], c("upto"), gl[:, b, :], start=True, stop=True)
            mm.then_inc(v_ready, 1)
            cols_T(unit(2))
            cols_T(unit(2))
            qk_at = na
            pe.wait_ge(G_ready, 1)
            for b in range(NB):
                bank = v_bank()
                pe.matmul(bank[:], c("ones"), grows[:, b, :],
                          start=True, stop=True).then_inc(v_ready, 1)
            mod_tiles("rows")
            for n in range(4):
                pe.wait_ge(sqg_done, n // 2 + 1)
                bank = a_bank()
                pe.matmul(bank[:], c("ones"), sq[:, 2 * n:2 * n + 2, :], start=True, stop=True).then_inc(a_ready, 1)
            mod_tiles("norms")
            pe.wait_ge(silu_done, 3)
            pe.wait_ge(qkn_done, 2)
            for b in range(NB):
                bank = v_bank()
                for h in range(GH):
                    mm = pe.transpose(bank[:, h * P:(h + 1) * P], g[:, 8 + h, b * P:(b + 1) * P], ident)
                mm.then_inc(v_ready, 1)
            bank = v_bank()
            for h in range(GH):
                mm = pe.transpose(bank[:, h * P:(h + 1) * P], g[:, 4 + h, 0:P], ident)
            mm.then_inc(v_ready, 1)
            for b in range(NB):
                bank = v_bank()
                for h in range(GH):
                    kt = g[:, 4 + h, b * P:(b + 1) * P]
                    mm = pe.matmul(bank[:, h * P:(h + 1) * P], kt, kt, start=True, stop=True)
                mm.then_inc(v_ready, 1)
                at["BT"] = nv
                bank = v_bank()
                for h in range(GH):
                    mm = pe.matmul(bank[:, h * P:(h + 1) * P], g[:, 4 + h, b * P:(b + 1) * P],
                                   g[:, h, b * P:(b + 1) * P], start=True, stop=True)
                mm.then_inc(v_ready, 1)
            def level_w(n):
                pe.wait_ge(btm_done, n + 1)
                if n == 0:
                    pe.wait_ge(xy0, 2)
                else:
                    pe.wait_ge(a_free, na)
                for b in range(NB):
                    bank = v_bank()
                    for h in range(GH):
                        mm = pe.matmul(bank[:, h * P:(h + 1) * P], BTm[:, n % 2, b, h * P:(h + 1) * P], X[:, b, h, :],
                                       start=True, stop=True)
                    mm.then_inc(v_ready, 1)
                at["W", n] = nv

            def level_xy(n, w_at):
                pe.wait_ge(v_free, w_at)
                for b in range(NB):
                    if n < LEVELS - 1:
                        bank = a_bank()
                        for h in range(GH):
                            mm = pe.matmul(bank[:, h * P:(h + 1) * P], Y[:, b, h, :], Wm[:, b, h, :],
                                           start=True, stop=True)
                        mm.then_inc(a_ready, 1)
                    bank = a_bank()
                    for h in range(GH):
                        mm = pe.matmul(bank[:, h * P:(h + 1) * P], Wm[:, b, h, :], Y[:, b, h, :],
                                       start=True, stop=True)
                    mm.then_inc(a_ready, 1)

            def moba_scores(h):
                if h == 0:
                    pe.wait_ge(a_free, qk_at)
                q0 = MD * (h % 2)
                bank = v_bank()
                for b in range(NB):
                    n = (b + 1) * P
                    mm = pe.matmul(bank[:, b * P:b * P + n], qk[q0:q0 + MD, h // 2, b * P:(b + 1) * P],
                                   qk[q0:q0 + MD, 4 + h // 2, 0:n], start=True, stop=True)
                mm.then_inc(v_ready, 1)

            def moba_turn(h):
                pe.wait_ge(mn_done, h + 1)
                bank = v_bank()
                pe.transpose(bank[:, 0:P], mE[:, h % 2, 0:P], ident)
                pe.transpose(bank[:, P:2 * P], mE[:, h % 2, P:2 * P], ident)
                pe.transpose(bank[:, 2 * P:3 * P], mE[:, h % 2, 2 * P:3 * P], ident).then_inc(v_ready, 1)
                at["E", h] = nv
                return nv

            def moba_values(h, p_at):
                pe.wait_ge(v_free, p_at)
                q0 = MD * (h % 2)
                if h == 0:
                    pe.wait_ge(x_free, MOD_AT["norms"][-1] + 1)
                elif h % 2 == 0:
                    pe.wait_ge(mv_free, h // 2)
                bank = PSX[0]
                vs = [v_nat[:, m, h * MD:(h + 1) * MD] for m in range(NB)]
                pe.matmul(bank[q0:q0 + MD, 0:P], vs[0], mP[:, h % 2, 0:P], start=True, stop=True)
                pe.matmul(bank[q0:q0 + MD, P:T], vs[0], mP[:, h % 2, P:T], start=True, stop=False)
                mm = pe.matmul(bank[q0:q0 + MD, P:T], vs[1], mP[:, h % 2, T:T + P], start=False, stop=True)
                mm.then_inc(mv_done, 1)

            prev_p = None
            for n in range(LEVELS + 1):
                if n < LEVELS:
                    level_w(n)
                    w_at = nv
                moba_scores(n)
                if n > 0:
                    moba_values(n - 1, prev_p)
                if n < LEVELS:
                    level_xy(n, w_at)
                prev_p = moba_turn(n)
            moba_values(MH - 1, prev_p)
            pe.wait_ge(a_free, na)
            bank = v_bank()
            for h in range(GH):
                mm = pe.matmul(bank[:, h * P:(h + 1) * P], Y[:, 0, h, :], bv[:, 0, h, :], start=True, stop=True)
            mm.then_inc(v_ready, 1)
            pe.wait_ge(v_free, nv)
            bank = v_bank()
            for h in range(GH):
                mm = pe.matmul(bank[:, h * P:(h + 1) * P], kdec[:, h, :], u[:, 0, h, :], start=True, stop=True)
            mm.then_inc(v_ready, 1)
            s_at = nv
            bank = v_bank()
            for h in range(GH):
                mm = pe.matmul(bank[:, h * P:(h + 1) * P], PT[:, 0, h, :], u[:, 0, h, :], start=True, stop=True)
            mm.then_inc(v_ready, 1)
            pe.wait_ge(v_free, s_at)
            bank = v_bank()
            for h in range(GH):
                mm = pe.matmul(bank[:, h * P:(h + 1) * P], g[:, 4 + h, P:T], S1[:, h, :], start=True, stop=True)
            mm.then_inc(v_ready, 1)
            ks_at = nv
            bank = v_bank()
            for h in range(GH):
                mm = pe.matmul(bank[:, h * P:(h + 1) * P], g[:, h, P:T], S1[:, h, :], start=True, stop=True)
            mm.then_inc(v_ready, 1)
            mod_tiles("chunk")
            pe.wait_ge(v_free, ks_at)
            bank = v_bank()
            for h in range(GH):
                mm = pe.matmul(bank[:, h * P:(h + 1) * P], Y[:, 1, h, :], R[:, h, :], start=True, stop=True)
            mm.then_inc(v_ready, 1)
            at["Y"] = nv
            pe.wait_ge(v_free, nv)
            bank = v_bank()
            for h in range(GH):
                mm = pe.matmul(bank[:, h * P:(h + 1) * P], PT[:, 1, h, :], u[:, 1, h, :], start=True, stop=True)
            mm.then_inc(v_ready, 1)
            mod_tiles("tail")
            pe.wait_ge(o_done, 1)
            for hp in range(2):
                bank = v_bank()
                for hh in range(2):
                    for b in range(NB):
                        mm = pe.transpose(bank[:, hh * T + b * P:hh * T + b * P + P], o[:, b, 2 * hp + hh, :], ident)
                mm.then_inc(v_ready, 1)
            pe.wait_ge(v_free, nv)
            pe.wait_ge(mv_free, MH // 2)
            for half in range(2):
                units = unit(2)
                for b in range(NB):
                    bank = v_bank()
                    for k in range(KD):
                        mm = pe.matmul(bank[:], mixT[:, k, b * P:(b + 1) * P], units[k // 4][:, k % 4, :],
                                       start=(k == 0), stop=(k == KD - 1))
                    mm.then_inc(v_ready, 1)
                freed.extend([(v_ready, nv)] * 2)
            at["x1"] = nv
            def ctx_cols(n, units, ncols, blocks=range(NB)):
                for b in blocks:
                    bank = a_bank()
                    for k in range(KD):
                        per = KD // len(units)
                        mm = pe.matmul(bank[:, 0:ncols], hTc[:, k, b * P:(b + 1) * P], units[k // per][:, k % per, :],
                                       start=(k == 0), stop=(k == KD - 1))
                    mm.then_inc(a_ready, 1)
                    at["ctx", n, b] = na
                if b == NB - 1:
                    freed.extend([(a_ready, na)] * len(units))

            pe.wait_ge(hn_done, 2)
            turn(hnc)
            hc_at = nv
            mod_tiles("mixed")
            pe.wait_ge(v_free, hc_at)
            pe.wait_ge(a_free, na)
            ctx_cols(0, unit(1), 256)
            pe.wait_ge(hn_done, 3)
            turn(h2)
            pe.wait_ge(v_free, nv)
            pe.wait_ge(a_free, na)
            pe.wait_ge(s_wr, 32)
            bank = v_bank()
            for b in range(NB):
                for k in range(KD):
                    mm = pe.matmul(bank[:, b * NR:(b + 1) * NR], h2T[:, k, b * P:(b + 1) * P], wr[:, k, :],
                                   start=(k == 0), stop=(k == KD - 1))
            mm.then_inc(v_ready, 1)
            kb_units = unit(2)
            ctx_cols(1, kb_units, 512, (0,))
            sel = rt[:, 0:NB * NE].rearrange("p (b e) -> p b e", b=NB)
            pe.wait_ge(sel_done, 1)
            bank = v_bank()
            pe.matmul(bank[:, 0:NE], c("before"), sel[:, 0, :], start=True, stop=True)
            pe.matmul(bank[:, NE:2 * NE], c("ones"), sel[:, 0, :], start=True, stop=False)
            pe.matmul(bank[:, NE:2 * NE], c("before"), sel[:, 1, :], start=False, stop=True)
            pe.matmul(bank[:, 2 * NE:3 * NE], c("ones"), sel[:, 0, :], start=True, stop=False)
            pe.matmul(bank[:, 2 * NE:3 * NE], c("ones"), sel[:, 1, :], start=False, stop=True).then_inc(v_ready, 1)
            ctx_cols(1, kb_units, 512, (1,))
            pe.wait_ge(v_free, nv)
            pe.wait_ge(a_free, na)
            pe.wait_ge(n_ready, 1)
            trips = value_trips(pe)
            mXT, mCT, mG, mHT, mY, mSc = PSA[0:2], PSV[0], PSV[1], PSV[2], (PSA[2], PSX[0]), (PSX[1], PSV[0])
            for ahead in (m_gp, m_ctp, m_sp):
                pe.sem_inc(ahead, 1)
            with pe.Fori(0, trips) as t:
                pe.wait_ge(m_pd, t + 1)
                pe.wait_ge(m_xt, 2 * t + 1)
                for half in range(2):
                    for kk in range(4):
                        k = 4 * half + kk
                        for b in range(NB):
                            mm = pe.matmul(mXT[half][:, kk * P:(kk + 1) * P], h2[:, b, k * P:(k + 1) * P],
                                           Pd[:, b, :, :].rearrange("p e s -> p (e s)"), start=(b == 0), stop=(b == 1))
                    mm.then_inc(m_xtp, 1)
                pe.wait_ge(m_s, 4 * t + 1)
                for b in range(NB):
                    mm = pe.transpose(mCT[:, b * P:(b + 1) * P], PdC[:, b, :, :].rearrange("p e s -> p (e s)"), ident)
                mm.then_inc(m_ctp, 1)
                pe.wait_ge(m_xt, 2 * t + 3)
                pe.wait_ge(m_hid, t + 1)
                for n in range(KD):
                    pe.wait_ge(mld[n], 32 * t + 32)
                    w = mview(n).rearrange("p (e n) -> p e n", e=EPG)
                    for e in range(EPG):
                        mm = pe.matmul(mG[32 * e:32 * e + 32, :], XT[:, n, 32 * e:32 * e + 32], w[:, e, :],
                                       start=(n == 0), stop=(n == KD - 1))
                    mm.then_inc(m_used if n < KD - 1 else m_gp, 1)
                pe.wait_ge(m_hid, t + 2)
                pe.wait_ge(m_ht, t + 1)
                for fc in range(2):
                    mm = pe.transpose(mHT[:, fc * P:(fc + 1) * P], hid[:, fc * P:(fc + 1) * P], ident)
                mm.then_inc(m_htp, 1)
                pe.wait_ge(m_ht, t + 2)
                pe.wait_ge(m_y, 2 * t + 1)
                for half in range(2):
                    for fc in range(2):
                        n = KD + 2 * half + fc
                        pe.wait_ge(mld[n], 32 * t + 32)
                        w = mview(n).rearrange("p (e n) -> p e n", e=EPG)
                        for e in range(EPG):
                            mm = pe.matmul(mY[half][32 * e:32 * e + 32, :], hidT[:, fc * P + 32 * e:fc * P + 32 * e + 32],
                                           w[:, e, :], start=(fc == 0), stop=(fc == 1))
                        mm.then_inc(m_used if fc == 0 else m_yp, 1)
                pe.wait_ge(m_ct, t + 1)
                for half in range(2):
                    pe.wait_ge(m_y, 2 * t + 2 + half)
                    for b in range(NB):
                        n = 2 * half + b
                        if n >= 2:
                            pe.wait_ge(m_s, 4 * t + n)
                        pe.matmul(mSc[b][:], CT[:, b * P:(b + 1) * P], Ysb[:, half, :],
                                  start=True, stop=True).then_inc(m_sp, 1)
            pe.wait_ge(m_s, 4 * trips + 1)
            def unit2(n):
                pe.wait_ge(ld2[n % NS], 16 * (n // NS + 1))
                ncols, src = post[n]
                return slot_view(NPRE + n, ncols, src)

            nu2 = 0

            def cols2(lhs, units, ncols):
                per = KD // len(units)
                for b in range(NB):
                    bank = a_bank()
                    for k in range(KD):
                        mm = pe.matmul(bank[:, 0:ncols], lhs[:, k, b * P:(b + 1) * P], units[k // per][:, k % per, :],
                                       start=(k == 0), stop=(k == KD - 1))
                    mm.then_inc(a_ready, 1)

            cols2(hTc, [unit2(0), unit2(1)], 512)
            freed2.extend([(a_ready, na)] * 2)
            nu2 = 2
            pe.wait_ge(hn_done, 4)
            turn(hnx)
            pe.wait_ge(v_free, nv)
            pe.wait_ge(a_free, na)
            for n, (k, ncols) in enumerate(((1, 256), (2, 512), (2, 512), (2, 512), (2, 512))):
                cols2(hTx, [unit2(nu2 + m) for m in range(k)], ncols)
                for b in range(NB):
                    at["proj2", n, b] = na - NB + 1 + b
                nu2 += k
                freed2.extend([(a_ready, na)] * k)
            done = 0

            def turn_heads(src_of, heads, dst_chunks):
                nonlocal done
                for cp in range(0, len(heads), 2):
                    bank = v_bank()
                    for m, cc in enumerate(heads[cp:cp + 2]):
                        for b in range(NB):
                            mm = pe.transpose(bank[:, m * T + b * P:m * T + b * P + P], src_of(b, cc), ident)
                    mm.then_inc(v_ready, 1)

            pe.wait_ge(qk2_done, 1)
            turn_heads(lambda b, cc: pA[:, b, 512:640], [0], None)
            pe.wait_ge(qk2_done, 2)
            turn_heads(lambda b, cc: cA[:, b, 0:128], [0], None)
            pe.wait_ge(qk2_done, 3)
            turn_heads(lambda b, cc: pA[:, b, cc * P:(cc + 1) * P], [0, 1, 2, 3], None)
            pe.wait_ge(qk2_done, 4)
            turn_heads(lambda b, cc: pB[:, b, 512 + cc * P:512 + (cc + 1) * P], [0, 1, 2, 3], None)
            pe.wait_ge(qk2_done, 5)
            turn_heads(lambda b, cc: cB[:, b, cc * P:(cc + 1) * P], [0, 1, 2, 3], None)
            pe.wait_ge(qk2_done, 6)
            turn_heads(lambda b, cc: pB[:, b, cc * P:(cc + 1) * P], [0, 1, 2, 3], None)
            pe.wait_ge(v_free, nv)
            pe.wait_ge(a_free, na)
            pe.wait_ge(s_bias, NB)

            def scores2(p):
                steps = []
                for n in (2 * p, 2 * p + 1):
                    if n >= 4:
                        pe.wait_ge(e2_done, n - 3)
                    b, kind, h = tiles2[n]
                    bank = SB[n % 4]
                    if kind == 0:
                        r0, ch, kch, qT, kT, kcT = HD * (h // 4), h % 4, 0, qaT, kaT, kcaT
                        plain, masked = (0, P) if b == 0 else (P, 0)
                    else:
                        r0, ch, kch, qT, kT, kcT = HD * (h % 2), h // 2, h // 2, qbT, kbT, kcbT
                    q = qT[r0:r0 + HD, ch, b * P:(b + 1) * P]
                    keys, ckeys = kT[r0:r0 + HD, kch, :], kcT[r0:r0 + HD, kch, :]
                    if kind == 0:
                        st = [(bank[:, plain:plain + P], q, keys[:, plain:plain + P], True, True),
                              (bank[:, masked:masked + P], q, keys[:, masked:masked + P], True, False),
                              (bank[:, masked:masked + P], ident, c("window")[:, b * T + masked:b * T + masked + P],
                               False, True)]
                    else:
                        st = [(bank[:, 0:T], q, keys, True, False),
                              (bank[:, 0:T], c("flip"), bias[b][:, h, :], False, True)]
                    steps.append(st + [(bank[:, T:2 * T], q, ckeys, True, True)])
                for two in zip(*steps):
                    for o_, l_, r_, first, last in two:
                        mm = pe.matmul(o_, l_, r_, start=first, stop=last)
                        if two[0] is steps[0][-1]:
                            mm.then_inc(s2_done, 1)

            def turn2(n):
                pe.wait_ge(e2_done, n + 1)
                if n >= 2:
                    pe.wait_ge(p2_done, n - 1)
                for m in range(4):
                    mm = pe.transpose(TB[n % 2][:, m * P:(m + 1) * P], E2[:, n % 4, m * P:(m + 1) * P], ident)
                mm.then_inc(t2_done, 1)

            def values2(n):
                pe.wait_ge(p2_done, n + 1)
                b, kind, h = tiles2[n]
                if n % 8 == 0 and n >= 16:
                    pe.wait_ge(o2_free, n // 8 - 1)
                bank = PSX[n // 8 % 2]
                if kind == 0:
                    vs = [pA[:, m, 640 + HD * (h // 4):640 + HD * (h // 4) + HD] for m in range(2)]
                    vs += [cA[:, m, 128 + HD * (h // 4):128 + HD * (h // 4) + HD] for m in range(2)]
                else:
                    vs = [pB[:, m, 1024 + h * HD:1024 + (h + 1) * HD] for m in range(2)]
                    vs += [cB[:, m, 512 + h * HD:512 + (h + 1) * HD] for m in range(2)]
                for m in range(4):
                    mm = pe.matmul(bank[:, h * HD:(h + 1) * HD], PT2[:, n % 4, m * P:(m + 1) * P], vs[m],
                                   start=(m == 0), stop=(m == 3))
                mm.then_inc(o2_done, 1)

            for p in range(NT // 2 + 2):
                if p < NT // 2:
                    scores2(p)
                if 1 <= p <= NT // 2:
                    turn2(2 * p - 2)
                    turn2(2 * p - 1)
                if p >= 2:
                    values2(2 * p - 4)
                    values2(2 * p - 3)
            def turn_block(src, b):
                for take, ready, k0 in ((v_bank, v_ready, 0), (a_bank, a_ready, 4)):
                    bank = take()
                    for kk in range(4):
                        mm = pe.transpose(bank[:, kk * P:(kk + 1) * P], src[:, b, (k0 + kk) * P:(k0 + kk + 1) * P], ident)
                    mm.then_inc(ready, 1)

            out_units = [unit2(nu2 + m) for m in range(4)]
            nu2 += 4
            def project_out(b, half):
                bank = v_bank()
                for k in range(KD):
                    mm = pe.matmul(bank[:], oT[:, k, b * P:(b + 1) * P], out_units[2 * half + k // 4][:, k % 4, :],
                                   start=(k == 0), stop=(k == KD - 1))
                mm.then_inc(v_ready, 1)

            pe.wait_ge(hn_done, 5)
            turn_block(onat, 0)
            pe.wait_ge(v_free, nv)
            pe.wait_ge(a_free, na)
            project_out(0, 0)
            pe.wait_ge(hn_done, 6)
            turn_block(onat, 1)
            o1_at = nv
            project_out(0, 1)
            pe.wait_ge(v_free, o1_at)
            pe.wait_ge(a_free, na)
            project_out(1, 0)
            freed2.extend([(v_ready, nv)] * 2)
            pe.wait_ge(hn_done, 7)
            turn_block(hnx, 0)
            h0_at = nv
            at["h", 0] = na
            project_out(1, 1)
            freed2.extend([(v_ready, nv)] * 2)
            pe.wait_ge(v_free, h0_at)
            pe.wait_ge(a_free, na)
            pe.wait_ge(o2_free, 4)
            fv = [PSV[(nv + m) % 3] for m in range(3)]
            fa = [PSA[(na + m) % 3] for m in range(3)]
            at["ffn"] = fv, fa
            acc = (PSX[0], PSX[1], fv[2], fa[2])
            at["mlp"] = nu2
            GU = ((fv[1], fa[1]), (fv[0], fa[0]))

            def mlp_unit(kind, n):
                q = mlp.index((kind, n))
                pe.wait_ge(lo_done, q + 1)
                return [unit_parts[q % 3][:, m, :].rearrange("p (k n) -> p k n", k=2 if kind == 2 else KD)
                        for m in range(2)]

            def hidden(w, bank, fc, t_0, t_1):
                for k in range(KD):
                    mm = split_product(bank[:, fc * T + t_0:fc * T + t_1], [w_[:, k, fc * P:(fc + 1) * P] for w_ in w],
                                       [col_parts[:, m, k, t_0:t_1] for m in range(2)], k == 0, k == KD - 1)
                return mm

            def up(n):
                if n >= 2:
                    pe.wait_ge(fh_done, n - 1)
                for kind in range(2):
                    w = mlp_unit(kind, n)
                    for fc in range(2):
                        mm = hidden(w, GU[n % 2][kind], fc, 0, T)
                    mm.then_inc(fg_ready, 1)

            def up_first():
                for b in range(NB):
                    pe.wait_ge(h3_split, b + 1)
                    for kind in range(2):
                        w = mlp_unit(kind, 0)
                        for fc in range(2):
                            mm = hidden(w, GU[0][kind], fc, b * P, (b + 1) * P)
                        if b == NB - 1:
                            mm.then_inc(fg_ready, 1)
                        elif kind == 0:
                            pe.wait_ge(hn_done, 8)
                            turn_block(hnx, 1)
                            at["h", 1] = na
                    if b == 0:
                        pe.wait_ge(v_free, nv)
                        pe.wait_ge(a_free, na)

            def down(n):
                wd = mlp_unit(2, n)
                pe.wait_ge(fh_done, n + 1)
                for b in range(NB):
                    for half in range(2):
                        for fc in range(2):
                            t_, c_ = fc * T + b * P, half * 512
                            mm = split_product(acc[2 * b + half][:], [hid_parts[:, n % 2, m, t_:t_ + P] for m in range(2)],
                                               [w_[:, fc, c_:c_ + 512] for w_ in wd],
                                               n == 0 and fc == 0, n == FP - 1 and fc == 1)
                        if n == FP - 1:
                            mm.then_inc(fd_done, 1)
                if n < FP - 1:
                    mm.then_inc(down_done, 1)

            for n in range(FP):
                freed2.extend([(lo_done, mlp.index((kind, n)) + 1) for kind in range(3)])
            up_first()
            for n in range(FP):
                if n + 1 < FP:
                    up(n + 1)
                down(n)

        @block.sync
        def _(sp):
            for b in range(NB):
                sp.dma_start(xres[:, b, :], i["x"][0, b * P:(b + 1) * P, :]).then_inc(s_x[b], 16)
            v = lambda name: i[name]

            def stream(first, end):
                for n in range(first, end):
                    ncols, src = pre[n]
                    if n >= NS:
                        sp.wait_ge(*freed[n - NS])
                    sp.dma_start(slot_view(n, ncols, src), src).then_inc(ld[n % NS], 16)

            for name, src in (("attn", v("attn_norm").rearrange("l (c p) -> (l c) p", p=P)),
                              ("norm1", v("norm1_g_2").rearrange("l (c p) -> (l c) p", p=P)),
                              ("norm2", v("norm2_g_2").rearrange("l (c p) -> (l c) p", p=P)),
                              ("on_a", v("on_a_2").rearrange("l (c p) -> (l c) p", p=P)),
                              ("on_b", v("on_b_2").rearrange("l (c p) -> (l c) p", p=P)),
                              ("conv", v("conv_w").rearrange("l i (c p) -> (l i c) p", p=P)),
                              ("gdn", v("gdn_norm")),
                              ("c", v("c_2").rearrange("l (c p) -> (l c) p", p=P)),
                              ("c_ctx", v("c_ctx_2").rearrange("(c p) -> c p", p=P))):
                r0 = ROWS[name]
                sp.dma_start(rows[r0:r0 + src.shape[0], :], src).then_inc(s_gain if name == "attn" else s_rows, 16)
                if name == "attn":
                    stream(0, 2)
            sp.dma_start(brow[:], v("b_mod_2").rearrange("l (n c) -> (l n) c", c=P)).then_inc(s_rows, 16)
            stream(2, 4)
            sp.dma_start(C[:, FIRST:], i["consts"][:, FIRST:]).then_inc(s_const, 16)
            sp.dma_start(head4[:, 0, :], v("A_log").broadcast_to((P, 4))).then_inc(s_small, 16)
            sp.dma_start(head4[:, 1, :], v("dt_bias").broadcast_to((P, 4))).then_inc(s_small, 16)
            for n, name in enumerate(("qn_a_2", "kn_a_2", "qn_b_2", "kn_b_2")):
                sp.dma_start(qkn[:, n, :], v(name).broadcast_to((P, HD))).then_inc(s_small, 16)
            sp.dma_start(sink[:], v("sink_a_2").broadcast_to((P, AH))).then_inc(s_small, 16)
            for which in range(2):
                c0 = (2 + 3 * which) * D
                sp.dma_start(gbc[:, which, :], v("b_mod_2")[:, c0:c0 + D].broadcast_to((P, D))).then_inc(s_gate, 16)
            sp.dma_start(wr[:, :, 0:NG], v("w_group").rearrange("l (k p) g -> p (l k) g", p=P)).then_inc(s_wr, 16)
            sp.dma_start(wr[:, :, NG:NR], v("w_router").rearrange("l (k p) g -> p (l k) g", p=P)).then_inc(s_wr, 16)

            stream(4, NPRE)
            for n in (*range(NS - 2), *range(NS, MU), NS - 2, NS - 1):
                if n < NS:
                    sp.wait_ge(*freed[NPRE - NS + n])
                elif n == NS:
                    sp.wait_ge(v_free, at["x1"])
                load_expert_unit(sp, n, 0)
            sp.wait_ge(n_ready, 1)
            trips = value_trips(sp)

            def expert_slot_free(n, t):
                if n == KD - 1:
                    sp.wait_ge(m_gp, t + 1)
                elif n in (KD + 1, KD + 3):
                    sp.wait_ge(m_yp, 2 * t - 1 if n == KD + 1 else 2 * t)
                else:
                    k = n + 1 if n < KD else (8 if n == KD else 9)
                    sp.wait_ge(m_used, 9 * t + (k - 9))

            first_expert = sp.alloc_register("first_expert")
            with sp.Fori(1, trips) as t:
                sp.reg_mov(first_expert, (t & (PASSES - 1)) * EPG)
                e0 = sp.snap(first_expert, min_val=0, max_val=NE - EPG)
                for n in range(MU):
                    expert_slot_free(n, t)
                    load_expert_unit(sp, n, e0)
            for n, (ncols, src) in enumerate(post):
                if n - NS >= len(freed2):
                    return
                if n < NS:
                    sp.wait_ge(m_gp, trips + 1)
                else:
                    sp.wait_ge(*freed2[n - NS])
                sp.dma_start(slot_view(NPRE + n, ncols, src), src).then_inc(ld2[n % NS], 16)
            for m in range(2 * NB):
                b, half = divmod(m, 2)
                sp.wait_ge(y_done, m + 1)
                sp.dma_start(out[0, b * P:(b + 1) * P, half * 512:half * 512 + 512],
                             xres[:, b, half * 512:half * 512 + 512]).then_inc(s_out, 16)
            sp.wait_ge(s_out, 16 * 2 * NB)

        @block.scalar
        def _(act):
            na = 0
            nch = 0

            def link(ins):
                nonlocal nch
                nch += 1
                ins.then_inc(act_chain, 1)
                act.wait_ge(act_chain, nch)

            def a_take():
                nonlocal na
                na += 1
                act.wait_ge(a_ready, na)
                return PSA[(na - 1) % 3]

            v = lambda name: i[name]
            act.dma_start(C[:, 0:FIRST], i["consts"][:, 0:FIRST]).then_inc(s_ident, 16)
            def squares(src, dst):
                for b in range(NB):
                    act.activation(dst[:, b, :], src[:, b, :], ACT.Square, accum_out=ss[:, b:b + 1]).then_inc(sq_done, 1)

            def turned(dst, scale=None, shift=None):
                for kp in (1, 3):
                    bank = a_take()
                    for kk in range(2):
                        k = 2 * kp + kk
                        b_ = bank[:, kk * T:(kk + 1) * T]
                        if scale is None:
                            ins = act.activation(dst[:, k, :], b_, ACT.Copy)
                        elif shift is None:
                            ins = act.activation(dst[:, k, :], b_, ACT.Copy, scale=scale[:, k:k + 1])
                        else:
                            ins = act.activation(dst[:, k, :], b_, ACT.Identity, scale=scale[:, k:k + 1],
                                                 bias=shift[:, k:k + 1])
                    ins.then_inc(a_free, 1)

            for b in range(NB):
                act.wait_ge(s_x[b], 16)
                act.activation(hn[:, b, :], xres[:, b, :], ACT.Square, accum_out=ss[:, b:b + 1]).then_inc(sq_done, 1)
            act.wait_ge(v_free, 1)
            turned(hT, vc[:, ROWS["attn"]:ROWS["attn"] + KD])
            act.wait_ge(s_const, 16)
            act.wait_ge(csil_ready, 1)
            act.wait_ge(v_free, 4)
            act.activation(csil[:, :, 0], vc[:, ROWS["c"]:ROWS["c"] + KD], ACT.Silu)
            act.activation(csil[:, :, 1], vc[:, ROWS["c_ctx"]:ROWS["c_ctx"] + KD], ACT.Silu).then_inc(csil_done, 1)
            act.wait_ge(pad_done, 1)
            for n in range(6):
                bank = a_take()
                act.activation(convin[:, 2 * n:2 * n + 2, 3:], bank[:].rearrange("p (c t) -> p c t", c=2),
                               ACT.Copy).then_inc(a_free, 1)
            for b in range(NB):
                bank = a_take()
                act.activation(z[:, b, :], bank[:], ACT.Silu).then_inc(a_free, 1)
            act.wait_ge(sp_req, 1)
            link(act.activation(gt[:, 1, :, :], gt[:, 1, :, :], ACT.Exp, scale=-1.0))
            act.activation(gt[:, 1, :, :], gt[:, 1, :, :], ACT.Ln, bias=c("ones")[:, 0:1])
            act.activation(beta[:], gab[:, :, 4:8], ACT.Sigmoid)
            act.activation(alog[:], head4[:, 0, :], ACT.Exp).then_inc(sp_done, 1)
            for n in range(4):
                bank = a_take()
                act.activation(qk[:, 2 * n:2 * n + 2, :], bank[:].rearrange("p (c t) -> p c t", c=2),
                               ACT.Copy).then_inc(a_free, 1)
            for n in range(3):
                act.wait_ge(conv_done, n + 1)
                act.activation(g[:, 4 * n:4 * n + 4, :], g[:, 4 * n:4 * n + 4, :], ACT.Silu).then_inc(silu_done, 1)
            for n in range(2):
                act.wait_ge(silu_done, n + 1)
                act.activation(sq[:, 4 * n:4 * n + 4, :], g[:, 4 * n:4 * n + 4, :], ACT.Square).then_inc(sqg_done, 1)
            def x_mod(n):
                act.wait_ge(x_ready, n + 1)
                if n >= 2:
                    act.wait_ge(v_ready, at["mod", n - 2])
                act.activation(mp[:, n % 2, :], mod_bank(n)[:], ACT.Copy).then_inc(x_free, 1)

            act.wait_ge(g_ready, 2)
            act.activation(gam[:], Gc[:], ACT.Exp).then_inc(gexp_done, 1)
            for n in MOD_AT["rows"]:
                x_mod(n)
            act.wait_ge(DU_raw, 1)
            act.activation(kd[:], kd_arg[:], ACT.Exp).then_inc(gexp_done, 1)
            act.activation(DU[:], DU[:], ACT.Exp).then_inc(DU_done, 1)
            for n in range(4):
                bank = a_take()
                act.activation(sq[:, 2 * n:2 * n + 2, :], bank[:].rearrange("p (c t) -> p c t", c=2), ACT.Sqrt,
                               scale=(float(GD) if n < 2 else 1.0),
                               bias=(c("epsq") if n < 2 else c("epsk"))).then_inc(a_free, 1)
            for n in MOD_AT["norms"]:
                x_mod(n)
            def level_xy(n):
                for b in range(NB):
                    for dst in ([X] if n < LEVELS - 1 else []) + [Y]:
                        bank = a_take()
                        act.activation(dst[:, b, :, :], bank[:].rearrange("p (h j) -> p h j", h=GH),
                                       ACT.Copy).then_inc(a_free, 1)

            def moba_exp(h):
                act.wait_ge(ms_ready, h + 1)
                if h >= 2:
                    act.wait_ge(v_ready, at["E", h - 2])
                for b in range(NB):
                    s0, n = b * P, (b + 1) * P
                    ins = act.activation(mE[:, h % 2, s0:s0 + n], mS[:, h % 2, s0:s0 + n], ACT.Exp,
                                         bias=mmax[:, 2 * (h % 2) + b:2 * (h % 2) + b + 1],
                                         accum_out=msum[:, 2 * (h % 2) + b:2 * (h % 2) + b + 1])
                ins.then_inc(me_done, 1)

            def x_moba(pair):
                act.wait_ge(mv_done, 2 * pair + 2)
                act.activation(mixT[:, pair, :], PSX[0][:, 0:T], ACT.Copy).then_inc(mv_free, 1)

            for n in range(LEVELS + 1):
                moba_exp(n)
                if n < LEVELS:
                    level_xy(n)
                if n > 0 and n % 2 == 0:
                    x_moba(n // 2 - 1)
            x_moba(3)
            act.wait_ge(me_done, MH)
            act.wait_ge(v_ready, at["E", MH - 1])
            act.dma_start(hnc[:], v("ctx_2").rearrange("a (b p) d -> p (a b) d", p=P)).then_inc(s_ctx, 16)
            for n in MOD_AT["chunk"] + MOD_AT["tail"]:
                x_mod(n)
            act.wait_ge(s_ctx, 16)
            act.wait_ge(v_ready, at["Y"])
            for b in range(NB):
                act.activation(sqc[:, b, :], hnc[:, b, :], ACT.Square, accum_out=ss5[:, b:b + 1]).then_inc(sq_done, 1)
            act.wait_ge(v_free, at["x1"])
            act.dma_start(ffn_bc, v("ffn_norm").broadcast_to((P, D))).then_inc(s_ffn_bc, 16)
            act.dma_start(fin_bc, v("final_norm").unsqueeze(0).broadcast_to((P, D))).then_inc(s_fin_bc, 16)
            squares(xres, h2)
            turned(hTc, modA[:, 1, :], modT[:, 0:KD, 1])
            for n in MOD_AT["mixed"]:
                x_mod(n)
            act.wait_ge(s_pad2, 16)
            def a_out(dsts):
                for dst in dsts:
                    bank = a_take()
                    act.activation(dst, bank[:, 0:dst.shape[1]], ACT.Copy).then_inc(a_free, 1)

            a_out([cA[:, b, :] for b in range(NB)])
            turned(h2T)
            act.wait_ge(rt_exp, 1)
            lg = rt[:, 64:136].rearrange("p (b n) -> p b n", b=NB)
            gp = rt[:, 136:144].rearrange("p (b n) -> p b n", b=NB)
            ing = rt[:, 144:160].rearrange("p (b n) -> p b n", b=NB)
            act.activation(gp[:], gp[:], ACT.Exp)
            act.activation(ing[:], ing[:], ACT.Exp).then_inc(rt_exped, 1)
            a_out([cB[:, b, 0:512] for b in range(NB)])
            act.wait_ge(n_ready, 1)
            trips = value_trips(act)
            mXT, mCT, mG, mY = PSA[0:2], PSV[0], PSV[1], (PSA[2], PSX[0])
            for ahead in (m_xt, m_y):
                act.sem_inc(ahead, 1)
            with act.Fori(0, trips) as t:
                act.wait_ge(m_gp, t + 1)
                for half in range(2):
                    act.wait_ge(m_xtp, 2 * t + 1 + half)
                    act.activation(XT[:, 4 * half:4 * half + 4, :], mXT[half][:].rearrange("p (k s) -> p k s", k=4),
                                   ACT.Copy).then_inc(m_xt, 1)
                act.wait_ge(m_ctp, t + 2)
                act.wait_ge(m_sp, 4 * t + 1)
                act.activation(CT[:], mCT[:, 0:NB * P], ACT.Copy).then_inc(m_ct, 1)
                act.wait_ge(m_gp, t + 2)
                act.wait_ge(m_hid, t + 1)
                act.activation(sg[:], mG[:, 0:FF], ACT.Silu).then_inc(m_sg, 1)
                for half in range(2):
                    act.wait_ge(m_yp, 2 * t + 1 + half)
                    act.activation(Ysb[:, half, :], mY[half][:], ACT.Copy).then_inc(m_y, 1)
            act.wait_ge(m_s, 4 * trips + 1)
            act.wait_ge(s_pad2, 16)
            for b in range(NB):
                for r2 in range(2):
                    src = bass.AP(tensor=rpb_pad.tensor, offset=(7 - 2 * b - r2) * GRID,
                                  ap=[[1, GRID], [1024, BH], [1, T]])
                    act.dma_start(bias[b][GRID * r2:GRID * r2 + GRID], src).then_inc(s_toep, 16)
            squares(xres, hnx)
            act.wait_ge(xo_done, NB)
            squares(xres, hnx)
            a_out([cB[:, b, 512:1024] for b in range(NB)])
            turned(hTx, modA[:, 0, :], modT[:, 0:KD, 0])
            a_out([pA[:, b, 512:768] for b in range(NB)])
            for b in range(NB):
                bank = a_take()
                act.activation(pA[:, b, 0:512].rearrange("p (c v d) -> p v c d", c=4, v=2),
                               bank[:].rearrange("p (v c d) -> p v c d", c=4, v=2), ACT.Copy).then_inc(a_free, 1)
            a_out([pB[:, b, c0:c0 + 512] for c0 in (512, 0, 1024) for b in range(NB)])
            def turned_block(dst, b, scale, shift=None):
                bank = a_take()
                for kk in range(4):
                    k = 4 + kk
                    d_, b_ = dst[:, k, b * P:(b + 1) * P], bank[:, kk * P:(kk + 1) * P]
                    if shift is None:
                        ins = act.activation(d_, b_, ACT.Copy, scale=scale[:, k:k + 1])
                    else:
                        ins = act.activation(d_, b_, ACT.Identity, scale=scale[:, k:k + 1], bias=shift[:, k:k + 1])
                ins.then_inc(a_free, 1)

            def sink_exp(b):
                act.wait_ge(sk_req, b + 1)
                act.activation(den[:, 8 * b:8 * b + 8], den[:, 8 * b:8 * b + 8], ACT.Exp).then_inc(sk_done, 1)

            def head_squares(b):
                if b > 0:
                    act.wait_ge(on_sq, 2 * b)
                for kind in range(2):
                    act.wait_ge(on_done, 2 * b + kind + 1)
                    act.activation(sqo[:, kind, :], onat[:, b, 512 * kind:512 * kind + 512],
                                   ACT.Square, accum_out=ss5[:, 2 * b + kind:2 * b + kind + 1]).then_inc(on_sq, 1)

            for n in range(NT + 2):
                if n < NT:
                    act.wait_ge(mx_done, n + 1)
                    if n >= 4:
                        act.wait_ge(t2_done, n - 3)
                    act.activation(E2[:, n % 4, :], SB[n % 4][:], ACT.Exp, bias=nm2[:, stat(n):stat(n) + 1],
                                   accum_out=rs2[:, stat(n):stat(n) + 1]).then_inc(e2_done, 1)
                if n >= 2:
                    m = n - 2
                    act.wait_ge(t2_done, m + 1)
                    if m >= 4:
                        act.wait_ge(o2_done, m - 3)
                    act.activation(PT2[:, m % 4, :], TB[m % 2][:], ACT.Copy).then_inc(p2_done, 1)
                if n == SINK_AT:
                    sink_exp(0)
                if n == SQUARES_AT:
                    head_squares(0)
            def upper(q):
                kind, n = mlp[q]
                u_ = at["mlp"] + 3 * n + kind
                act.wait_ge(ld2[u_ % NS], 16 * (u_ // NS + 1))
                if q >= 3:
                    act.wait_ge(*mlp_used(q - 3))
                act.activation(unit_parts[q % 3][:, 0, :], slot_of(NPRE + u_), ACT.Copy).then_inc(hi_done, 1)

            sink_exp(1)
            turned_block(oT, 0, vc[:, ROWS["on_a"]:ROWS["on_a"] + KD])
            head_squares(1)
            turned_block(oT, 1, vc[:, ROWS["on_a"]:ROWS["on_a"] + KD])
            act.wait_ge(o2_done, NT)
            act.wait_ge(on_sq, 2 * NB)
            upper(0)
            for b in range(NB):
                act.wait_ge(x3_done, b + 1)
                act.activation(hnx[:, b, :], xres[:, b, :], ACT.Square, accum_out=ss[:, b:b + 1]).then_inc(sq_done, 1)
                turned_block(h3T, b, modA[:, 2, :], modT[:, 24:32, 0])
                upper(b + 1)
            G = (at["ffn"][0][1], at["ffn"][0][0])
            for n in range(FP):
                act.wait_ge(fg_ready, 2 * n + 1)
                if n >= 2:
                    act.wait_ge(fh_done, n - 1)
                act.activation(fsg[:, n % 2, :], G[n % 2][:], ACT.Silu).then_inc(fsg_done, 1)
                for q in mlp_behind(n):
                    upper(q)

        @block.vector
        def _(dve):
            nv = nch = nrs = nsq = nqk = 0
            vec = nc.vector

            def link(ins):
                nonlocal nch
                nch += 1
                ins.then_inc(dve_chain, 1)
                dve.wait_ge(dve_chain, nch)

            def v_take():
                nonlocal nv
                nv += 1
                dve.wait_ge(v_ready, nv)
                return PSV[(nv - 1) % 3]

            def rsqrt(src, dst, n, scale=None):
                nonlocal nrs
                vec.tensor_scalar(dst, src, 1.0 / n, EPS, ALU.mult, ALU.add).then_inc(rs_req, 1)
                nrs += 1
                dve.wait_ge(rs_done, nrs)
                if scale is not None:
                    link(vec.tensor_scalar(dst, dst, scale, None, ALU.mult))

            def turned(dst, scale=None, shift=None):
                for kp in (0, 2):
                    bank = v_take()
                    for kk in range(2):
                        k = 2 * kp + kk
                        b_ = bank[:, kk * T:(kk + 1) * T]
                        if scale is None:
                            ins = vec.tensor_copy(dst[:, k, :], b_)
                        elif shift is None:
                            ins = vec.tensor_scalar(dst[:, k, :], b_, scale[:, k:k + 1], None, ALU.mult)
                        else:
                            ins = vec.tensor_scalar(dst[:, k, :], b_, scale[:, k:k + 1], shift[:, k:k + 1],
                                                    ALU.mult, ALU.add)
                    ins.then_inc(v_free, 1)

            def normed(src, dst, gain=None, own=False):
                nonlocal nsq
                nsq += 2
                dve.wait_ge(sq_done, nsq)
                rsqrt(ss, rstd, D)
                for b in range(NB):
                    if gain is None:
                        ins = vec.tensor_scalar(dst[:, b, :], src[:, b, :], rstd[:, b:b + 1], None, ALU.mult)
                    else:
                        ins = vec.scalar_tensor_tensor(dst[:, b, :], src[:, b, :], rstd[:, b:b + 1], gain,
                                                       ALU.mult, ALU.mult)
                    if own:
                        ins.then_inc(xo_done, 1)
                if not own:
                    ins.then_inc(hn_done, 1)

            def heads(v, n=GH):
                return v.rearrange("p (h j) -> p h j", h=n)

            def spread(v, n):
                return v.unsqueeze(2).broadcast_to((P, v.shape[1], n))

            bank = v_take()
            vec.tensor_copy(vc[:, 0:KD], bank[:, 0:KD]).then_inc(v_free, 1)
            normed(xres, hn)
            dve.wait_ge(v_free, 1)
            turned(hT, vc[:, ROWS["attn"]:ROWS["attn"] + KD])
            dve.wait_ge(pad_done, 1)

            def conv(n):
                dve.wait_ge(a_free, 2 + 2 * (n + 1))
                for cc in range(4 * n, 4 * n + 4):
                    w = [vc[:, ROWS["conv"] + r * GQKV + cc:ROWS["conv"] + r * GQKV + cc + 1] for r in range(TAPS)]
                    link(vec.tensor_scalar(g[:, cc, :], convin[:, cc, 0:T], w[0], None, ALU.mult))
                    for r in range(1, TAPS):
                        ins = vec.scalar_tensor_tensor(g[:, cc, :], convin[:, cc, r:r + T], w[r], g[:, cc, :],
                                                       ALU.mult, ALU.add)
                        if r < TAPS - 1 or cc < 4 * n + 3:
                            link(ins)
                ins.then_inc(conv_done, 1)

            bank = v_take()
            vec.tensor_copy(vc[:, KD:], bank[:, KD:N_ROWS])
            vec.tensor_copy(bcol[:], bank[:, N_ROWS:N_ROWS + 6 * KD]).then_inc(v_free, 1)
            dve.wait_ge(v_free, nv)
            conv(0)
            bank = v_take()
            vec.tensor_copy(gab[:, 0, :], bank[:, 0:8]).then_inc(v_free, 1)
            bank = v_take()
            vec.tensor_copy(gab[:, 1, :], bank[:, 0:8]).then_inc(v_free, 1)
            dve.wait_ge(v_free, nv)
            dve.wait_ge(s_small, 16 * 7)
            dtb = head4[:, 1, :].unsqueeze(1).broadcast_to((P, NB, 4))
            link(vec.tensor_tensor(gt[:, 0], gab[:, :, 0:4], dtb, ALU.add))
            link(vec.scalar_tensor_tensor(gt[:, 1], gt[:, 0], -1.0, gt[:, 0], ALU.mult, ALU.max))
            vec.tensor_scalar(gt[:, 2], gt[:, 0], 0.0, None, ALU.max).then_inc(sp_req, 1)
            dve.wait_ge(sp_req, 1)
            dve.wait_ge(sp_done, 1)
            link(vec.tensor_tensor(gt[:, 0], gt[:, 1], gt[:, 2], ALU.add))
            vec.scalar_tensor_tensor(gl[:], gt[:, 0], -1.0, alog.unsqueeze(1).broadcast_to((P, NB, 4)),
                                     ALU.mult, ALU.mult).then_inc(g_ready, 1)
            dve.wait_ge(g_ready, 1)
            dve.wait_ge(s_const, 16)
            for b in range(NB):
                for h in range(GH):
                    ins = vec.tensor_scalar(grows[:, b, h * P:(h + 1) * P], c("upto"), gl[:, b, h:h + 1], None, ALU.mult)
            ins.then_inc(G_ready, 1)
            conv(1)
            conv(2)
            for b in range(NB):
                bank = v_take()
                vec.tensor_copy(v_nat[:, b, :], bank[:]).then_inc(v_free, 1)
            bank = v_take()
            vec.tensor_copy(Gc[:], bank[:, 0:8].rearrange("p (b n) -> p b n", b=NB)).then_inc(v_free, 1)
            dve.wait_ge(v_free, nv)
            vec.tensor_scalar(nbeta[:], beta[:], -1.0, None, ALU.mult).then_inc(g_ready, 1)
            def mod_cols(n):
                bank = v_take()
                vec.tensor_tensor(modT[:, 4 * n:4 * n + 4, :], bank[:, 0:8].rearrange("p (k r) -> p k r", k=4),
                                  bcol[:, 4 * n:4 * n + 4].unsqueeze(2).broadcast_to((P, 4, 2)),
                                  ALU.add).then_inc(v_free, 1)
                if n in (4, 5, 10, 11):
                    which, half = n // 10, n % 2
                    bank = v_take()
                    dve.wait_ge(s_gate, 32)
                    gv = gbc[:, which, half * 512:half * 512 + 512]
                    vec.tensor_tensor(gv, gv, bank[:], ALU.add).then_inc(v_free, 1)

            for b in range(NB):
                bank = v_take()
                if b == 0:
                    dve.wait_ge(g_ready, 2)
                    last = heads(bank[:])[:, :, P - 1]
                    link(vec.tensor_tensor(kd_arg, last, Gc[:, 0, :], ALU.subtract))
                    dve.wait_ge(conv_done, 3)
                for h in range(GH):
                    ins = vec.scalar_tensor_tensor(DU[:, b, h, :], bank[:, h * P:(h + 1) * P], Gc[:, b, h:h + 1],
                                                   c("future"), ALU.subtract, ALU.subtract)
                ins.then_inc(v_free, 1)
            for n in MOD_AT["rows"]:
                mod_cols(n)
            dve.wait_ge(gexp_done, 1)
            vec.scalar_tensor_tensor(bgam, beta[:, 1, :], -1.0, gam[:, 1, :], ALU.mult, ALU.mult).then_inc(DU_raw, 1)
            for n in range(2):
                dve.wait_ge(a_free, 14 + 2 * (n + 1))
                dve.wait_ge(silu_done, n + 1)
                link(vec.reciprocal(sq[:, 4 * n:4 * n + 4, :], sq[:, 4 * n:4 * n + 4, :]))
                vec.tensor_tensor(g[:, 4 * n:4 * n + 4, :], g[:, 4 * n:4 * n + 4, :], sq[:, 4 * n:4 * n + 4, :],
                                  ALU.mult).then_inc(qkn_done, 1)
                for m in MOD_AT["norms"][3 * n:3 * n + 3]:
                    mod_cols(m)
            for b in range(NB):
                bank = v_take()
                vec.tensor_tensor(bv[:, b], heads(bank[:]), spread(beta[:, b, :], P), ALU.mult).then_inc(v_free, 1)
            bank = v_take()
            dve.wait_ge(gexp_done, 2)
            vec.tensor_tensor(kdec[:], heads(bank[:]), spread(kd, P), ALU.mult).then_inc(v_free, 1)
            dve.wait_ge(DU_done, 1)
            for b in range(NB):
                bank = v_take()
                vec.tensor_tensor(heads(BT[:, b, :]), heads(bank[:]), DU[:, b], ALU.mult).then_inc(v_free, 1)
                bank = v_take()
                vec.tensor_tensor(PT[:, b], heads(bank[:]), DU[:, b], ALU.mult).then_inc(v_free, 1)
            def level_w():
                for b in range(NB):
                    bank = v_take()
                    for h in range(GH):
                        ins = vec.scalar_tensor_tensor(Wm[:, b, h, :], bank[:, h * P:(h + 1) * P],
                                                       nbeta[:, b, h:h + 1], c("ident"), ALU.mult, ALU.add)
                    ins.then_inc(v_free, 1)

            def moba_max(h):
                bank = v_take()
                if h >= 2:
                    dve.wait_ge(me_done, h - 1)
                vec.scalar_tensor_tensor(mS[:, h % 2, :], bank[:, 0:384], MD ** -0.5, c("causal"),
                                         ALU.mult, ALU.add).then_inc(v_free, 1)
                dve.wait_ge(v_free, nv)
                for b in range(NB):
                    s0, n = b * P, (b + 1) * P
                    ins = vec.tensor_reduce(mmax[:, 2 * (h % 2) + b:2 * (h % 2) + b + 1], mS[:, h % 2, s0:s0 + n],
                                            AX, ALU.max, negate=True)
                ins.then_inc(ms_ready, 1)

            def moba_norm(h):
                dve.wait_ge(me_done, h + 1)
                link(vec.reciprocal(minv[:, 2 * (h % 2):2 * (h % 2) + 2], msum[:, 2 * (h % 2):2 * (h % 2) + 2]))
                for b in range(NB):
                    s0, n = b * P, (b + 1) * P
                    ins = vec.tensor_scalar(mE[:, h % 2, s0:s0 + n], mE[:, h % 2, s0:s0 + n],
                                            minv[:, 2 * (h % 2) + b:2 * (h % 2) + b + 1], None, ALU.mult)
                ins.then_inc(mn_done, 1)

            def moba_turned(h):
                bank = v_take()
                if h >= 2:
                    dve.wait_ge(mv_done, h - 1)
                vec.tensor_copy(mP[:, h % 2, :], bank[:, 0:384]).then_inc(v_free, 1)

            for n in range(LEVELS + 1):
                if n < LEVELS:
                    level_w()
                moba_max(n)
                moba_norm(n)
                moba_turned(n)
            bank = v_take()
            vec.tensor_copy(u[:, 0], heads(bank[:])).then_inc(v_free, 1)
            bank = v_take()
            vec.tensor_copy(S1[:], heads(bank[:])).then_inc(v_free, 1)
            bank = v_take()
            vec.tensor_copy(o[:, 0], heads(bank[:])).then_inc(v_free, 1)
            bank = v_take()
            for h in range(GH):
                ins = vec.scalar_tensor_tensor(R[:, h, :], bank[:, h * P:(h + 1) * P], bgam[:, h:h + 1], bv[:, 1, h, :],
                                               ALU.mult, ALU.add)
            ins.then_inc(v_free, 1)
            bank = v_take()
            vec.tensor_tensor(o[:, 1], heads(bank[:]), spread(gam[:, 1, :], P), ALU.mult).then_inc(v_free, 1)
            for n in MOD_AT["chunk"]:
                mod_cols(n)
            bank = v_take()
            vec.tensor_copy(u[:, 1], heads(bank[:])).then_inc(v_free, 1)
            bank = v_take()
            dve.wait_ge(v_free, nv - 1)
            vec.tensor_tensor(o[:, 1], o[:, 1], heads(bank[:]), ALU.add).then_inc(v_free, 1)
            dve.wait_ge(v_free, nv)
            link(vec.tensor_tensor(Wm[:], o[:], o[:], ALU.mult))
            link(vec.tensor_reduce(ssg, Wm.rearrange("p b h j -> p (b h) j"), AX, ALU.add))
            rsqrt(ssg, rsg, GD)
            ov = o.rearrange("p b h j -> p (b h) j")
            link(vec.tensor_tensor(ov, ov, spread(rsg, P), ALU.mult))
            dve.wait_ge(a_free, 10)
            vec.tensor_tensor(ov, ov, z.rearrange("p b (h j) -> p (b h) j", h=GH), ALU.mult).then_inc(o_done, 1)
            for n in MOD_AT["tail"]:
                mod_cols(n)
            dve.wait_ge(v_free, nv)
            for n, (r, name, c0) in enumerate(((0, "norm1", 8), (1, "norm1", 8), (0, "norm2", 32))):
                vec.scalar_tensor_tensor(modA[:, n, :], modT[:, c0:c0 + KD, r], 1.0,
                                         vc[:, ROWS[name]:ROWS[name] + KD], ALU.add, ALU.mult)
            nsq += 2
            dve.wait_ge(sq_done, nsq)
            rsqrt(ss5[:, 0:2], rs5[:, 0:2], D)
            for b in range(NB):
                ins = vec.tensor_scalar(hnc[:, b, :], hnc[:, b, :], rs5[:, b:b + 1], None, ALU.mult)
            ins.then_inc(hn_done, 1)
            for hp in range(2):
                bank = v_take()
                vec.tensor_scalar(mixT[:, 4 + 2 * hp:6 + 2 * hp, :], bank[:].rearrange("p (h t) -> p h t", h=2),
                                  vc[:, ROWS["gdn"]:ROWS["gdn"] + 1], None, ALU.mult).then_inc(v_free, 1)
            for half in range(2):
                for b in range(NB):
                    bank = v_take()
                    xv = xres[:, b, half * 512:half * 512 + 512]
                    vec.tensor_tensor(xv, xv, bank[:], ALU.add).then_inc(v_free, 1)
            dve.wait_ge(v_free, nv)
            turned(hTc, modA[:, 1, :], modT[:, 0:KD, 1])
            dve.wait_ge(s_ffn_bc, 16)
            normed(xres, h2, gain=ffn_bc)
            for n in MOD_AT["mixed"]:
                mod_cols(n)
            turned(h2T)
            def f(a, *d):
                v_ = rt[:, a:a + int(np.prod(d))]
                if len(d) == 1:
                    return v_
                nm = "abc"[:len(d)]
                return v_.rearrange(f"p ({' '.join(nm)}) -> p {' '.join(nm)}", **dict(zip(nm[1:], d[1:])))

            def over(v, n):
                return v.unsqueeze(2).broadcast_to((P, NB, n))

            sel, lg, gp, ing = f(0, NB, NG, EG), f(64, NB, NR), f(136, NB, NG), f(144, NB, EG)
            gm, gw, gmw, goh = f(160, NB), f(162, NB, NG), f(170, NB), f(172, NB, NG)
            gsum, picked, im = f(180, NB), f(192, NB, NG, EG), f(256, NB)
            m1, w1, wm1, oh1 = f(258, NB), f(260, NB, EG), f(276, NB), f(278, NB, EG)
            rem, m2, w2, wm2, oh2 = f(294, NB, EG), f(310, NB), f(312, NB, EG), f(328, NB), f(330, NB, EG)
            dn, wi, s8, comb = f(346, NB), f(348, NB, EG), f(364, NB, EG), f(380, NB, NG, EG)
            pos, cmax = f(444, NB, NE), f(508, 1)
            tie_g = c("tie")[:, 0:NG].unsqueeze(1).broadcast_to((P, NB, NG))
            tie_e = c("tie")[:, NG:NG + EG].unsqueeze(1).broadcast_to((P, NB, EG))
            bank = v_take()
            vec.tensor_copy(lg[:], bank[:, 0:NB * NR].rearrange("p (b n) -> p b n", b=NB)).then_inc(v_free, 1)
            dve.wait_ge(v_free, nv)
            link(vec.tensor_reduce(gm, lg[:, :, 0:NG], AX, ALU.max))
            link(vec.tensor_tensor(gp[:], lg[:, :, 0:NG], over(gm, NG), ALU.subtract))
            link(vec.tensor_tensor(gw[:], lg[:, :, 0:NG], over(gm, NG), ALU.is_equal))
            link(vec.tensor_tensor(gw[:], gw[:], tie_g, ALU.mult))
            link(vec.tensor_reduce(gmw, gw[:], AX, ALU.max))
            link(vec.tensor_tensor(goh[:], gw[:], over(gmw, NG), ALU.is_equal))
            el = lg[:, :, NG:NR].rearrange("p b (g e) -> p b g e", g=NG)
            link(vec.tensor_tensor(picked[:], el, goh.unsqueeze(3).broadcast_to((P, NB, NG, EG)), ALU.mult))
            link(vec.tensor_reduce(ing[:], picked.rearrange("p b g e -> p b e g"), AX, ALU.add))
            link(vec.tensor_reduce(im, ing[:], AX, ALU.max))
            vec.tensor_tensor(ing[:], ing[:], over(im, EG), ALU.subtract).then_inc(rt_exp, 1)
            dve.wait_ge(rt_exped, 1)
            link(vec.tensor_reduce(gsum, gp[:], AX, ALU.add))
            for m, src, w_, wm, oh in ((m1, ing, w1, wm1, oh1), (m2, rem, w2, wm2, oh2)):
                if src is rem:
                    link(vec.scalar_tensor_tensor(rem[:], oh1[:], -2.0, ing[:], ALU.mult, ALU.add))
                link(vec.tensor_reduce(m, src[:], AX, ALU.max))
                link(vec.tensor_tensor(w_[:], src[:], over(m, EG), ALU.is_equal))
                link(vec.tensor_tensor(w_[:], w_[:], tie_e, ALU.mult))
                link(vec.tensor_reduce(wm, w_[:], AX, ALU.max))
                link(vec.tensor_tensor(oh[:], w_[:], over(wm, EG), ALU.is_equal))
            link(vec.tensor_tensor(dn, m1, m2, ALU.add))
            link(vec.tensor_tensor(dn, dn, gsum, ALU.mult))
            link(vec.reciprocal(dn, dn))
            link(vec.tensor_tensor(m1, m1, dn, ALU.mult))
            link(vec.tensor_tensor(m2, m2, dn, ALU.mult))
            link(vec.tensor_tensor(wi[:], oh1[:], over(m1, EG), ALU.mult))
            link(vec.tensor_tensor(w2[:], oh2[:], over(m2, EG), ALU.mult))
            link(vec.tensor_tensor(wi[:], wi[:], w2[:], ALU.add))
            link(vec.tensor_tensor(s8[:], oh1[:], oh2[:], ALU.add))
            g4 = goh.unsqueeze(3).broadcast_to((P, NB, NG, EG))
            link(vec.tensor_tensor(comb[:], g4, wi.unsqueeze(2).broadcast_to((P, NB, NG, EG)), ALU.mult))
            vec.tensor_tensor(sel[:], g4, s8.unsqueeze(2).broadcast_to((P, NB, NG, EG)), ALU.mult).then_inc(sel_done, 1)
            dve.wait_ge(sel_done, 1)
            bank = v_take()
            self_ = sel.rearrange("p b g e -> p b (g e)")
            link(vec.scalar_tensor_tensor(pos[:], bank[:, 0:2 * NE].rearrange("p (b e) -> p b e", b=NB), 1.0, self_,
                                          ALU.add, ALU.mult))
            vec.tensor_reduce(cmax, bank[:, 2 * NE:3 * NE], AX, ALU.max).then_inc(v_free, 1)
            dve.wait_ge(v_free, nv)
            for r in range(ROUNDS):
                vec.tensor_scalar(posall[:, :, r * NE:(r + 1) * NE], pos[:], -1.0 - SLOTS * r, None, ALU.add)
                vec.tensor_copy(comball[:, :, r * NE:(r + 1) * NE], comb.rearrange("p b g e -> p b (g e)"))
            link(vec.tensor_scalar(trips_i[:, 0:1], cmax, float(SLOTS - 1), None, ALU.add))
            link(vec.tensor_scalar(trips_i[:, 0:1], trips_i[:, 0:1], SLOTS.bit_length() - 1, None, ALU.arith_shift_right))
            vec.tensor_scalar(trips_i[:, 1:2], trips_i[:, 0:1], PASSES.bit_length() - 1, None,
                              ALU.logical_shift_left).then_inc(n_ready, 1)
            dve.wait_ge(n_ready, 1)
            trips = value_trips(dve)
            mG, mHT, mSc = PSV[1], PSV[2], (PSX[1], PSV[0])
            for ahead in (m_hid, m_ht, m_s):
                dve.sem_inc(ahead, 1)
            with dve.Fori(0, trips) as t:
                dve.wait_ge(m_ctp, t + 1)
                now = posall[:, :, bass.ds(t * EPG, EPG)].unsqueeze(3).broadcast_to((P, NB, EPG, SLOTS))
                weight = comball[:, :, bass.ds(t * EPG, EPG)].unsqueeze(3).broadcast_to((P, NB, EPG, SLOTS))
                slots = c("slots").rearrange("p (e s) -> p e s", e=EPG).unsqueeze(1).broadcast_to((P, NB, EPG, SLOTS))
                vec.tensor_tensor(Pd[:], now, slots, ALU.is_equal).then_inc(m_pc, 1)
                dve.wait_ge(m_pc, t + 1)
                vec.tensor_tensor(PdC[:], weight, Pd[:], ALU.mult).then_inc(m_pd, 1)
                dve.wait_ge(m_sg, t + 1)
                vec.tensor_tensor(hid[:], sg[:], mG[:, FF:2 * FF], ALU.mult).then_inc(m_hid, 1)
                dve.wait_ge(m_htp, t + 1)
                vec.tensor_copy(hidT[:], mHT[:, 0:FF]).then_inc(m_ht, 1)
                for half in range(2):
                    for b in range(NB):
                        n = 2 * half + b
                        dve.wait_ge(m_sp, 4 * t + n + 2)
                        dve.wait_ge(m_s, 4 * t + n + 1)
                        xv = xres[:, b, half * 512:half * 512 + 512]
                        vec.tensor_tensor(xv, xv, mSc[b][:], ALU.add).then_inc(m_s, 1)
            dve.wait_ge(m_s, 4 * trips + 1)
            dve.wait_ge(s_fin_bc, 16)
            normed(xres, xres, gain=fin_bc, own=True)
            dve.wait_ge(xo_done, NB)
            normed(xres, hnx)
            turned(hTx, modA[:, 0, :], modT[:, 0:KD, 0])
            dve.wait_ge(v_free, nv)
            for n in range(2):
                gain = qkn[:, n, :]
                vec.tensor_tensor(tabs[:, 2 * n], c("cos").rearrange("p (b d) -> p b d", b=NB),
                                  gain.unsqueeze(1).broadcast_to((P, NB, HD)), ALU.mult)
                for w_ in range(2):
                    def part(v_, w__):
                        return v_.rearrange("p (u w s) -> p u w s", u=2, w=2)[:, :, w__, :]
                    for b in range(NB):
                        ins = vec.tensor_tensor(part(tabs[:, 2 * n + 1, b, :], w_), part(c("sin")[:, b * HD:(b + 1) * HD], w_),
                                                part(gain, 1 - w_), ALU.mult)
            link(ins)

            def qk_norm(views, a_tiles, gain, rope, scale=None):
                nonlocal nqk
                nh = views[0].shape[1] // HD
                for b in range(NB):
                    dve.wait_ge(a_free, a_tiles[b])
                    xv = views[b].rearrange("p (h d) -> p h d", h=nh)
                    tt = t0[:, 0:nh * HD].rearrange("p (h d) -> p h d", h=nh)
                    link(vec.tensor_tensor(tt, xv, xv, ALU.mult))
                    link(vec.tensor_reduce(ssn[:, b * nh:(b + 1) * nh], tt, AX, ALU.add))
                rsqrt(ssn[:, 0:2 * nh], rsn[:, 0:2 * nh], HD, scale)
                for b in range(NB):
                    xv = views[b].rearrange("p (h d) -> p h d", h=nh)
                    tt = t0[:, 0:nh * HD].rearrange("p (h d) -> p h d", h=nh)
                    ta = t1[:, 0:nh * HD].rearrange("p (h d) -> p h d", h=nh)
                    link(vec.tensor_tensor(xv, xv, spread(rsn[:, b * nh:(b + 1) * nh], HD), ALU.mult))
                    if not rope:
                        ins = vec.tensor_tensor(xv, xv, qkn[:, gain, :].unsqueeze(1).broadcast_to((P, nh, HD)), ALU.mult)
                    else:
                        link(vec.tensor_tensor(tt, xv, tabs[:, 2 * gain, b, :].unsqueeze(1).broadcast_to((P, nh, HD)),
                                               ALU.mult))
                        for u_ in range(2):
                            for w_ in range(2):
                                a_, o_ = 32 * u_ + 16 * w_, 32 * u_ + 16 * (1 - w_)
                                sn = tabs[:, 2 * gain + 1, b, a_:a_ + 16].unsqueeze(1).broadcast_to((P, nh, 16))
                                ins = vec.tensor_tensor(ta[:, :, a_:a_ + 16], xv[:, :, o_:o_ + 16], sn, ALU.mult)
                        link(ins)
                        ins = vec.tensor_tensor(xv, tt, ta, ALU.add)
                    if b == 0:
                        link(ins)
                ins.then_inc(qk2_done, 1)

            X0 = [(0, 0), (0, 1)]
            qk_norm([pA[:, b, 512:640] for b in range(NB)], [at["proj2", 0, b] for b in range(NB)], 1, True)
            dve.wait_ge(qk2_done, 1)
            qk_norm([cA[:, b, 0:128] for b in range(NB)], [at["ctx", 0, b] for b in range(NB)], 1, False)
            dve.wait_ge(qk2_done, 2)
            qk_norm([pA[:, b, 0:512] for b in range(NB)], [at["proj2", 1, b] for b in range(NB)], 0, True, 0.125)
            dve.wait_ge(qk2_done, 3)
            qk_norm([pB[:, b, 512:1024] for b in range(NB)], [at["proj2", 2, b] for b in range(NB)], 3, False)
            dve.wait_ge(qk2_done, 4)
            qk_norm([cB[:, b, 0:512] for b in range(NB)], [at["ctx", 1, b] for b in range(NB)], 3, False)
            dve.wait_ge(qk2_done, 5)
            qk_norm([pB[:, b, 0:512] for b in range(NB)], [at["proj2", 3, b] for b in range(NB)], 2, False, 0.125)
            for dst, chunks in ((kaT, 1), (kcaT, 1), (qaT, 4), (kbT, 4), (kcbT, 4), (qbT, 4)):
                for cp in range(0, chunks, 2):
                    w_ = min(2, chunks - cp)
                    bank = v_take()
                    vec.tensor_copy(dst[:, cp:cp + w_, :],
                                    bank[:, 0:w_ * T].rearrange("p (k t) -> p k t", k=w_)).then_inc(v_free, 1)
            def turned_block(dst, b, scale, shift=None):
                bank = v_take()
                for k in range(4):
                    d_, b_ = dst[:, k, b * P:(b + 1) * P], bank[:, k * P:(k + 1) * P]
                    if shift is None:
                        ins = vec.tensor_scalar(d_, b_, scale[:, k:k + 1], None, ALU.mult)
                    else:
                        ins = vec.tensor_scalar(d_, b_, scale[:, k:k + 1], shift[:, k:k + 1], ALU.mult, ALU.add)
                ins.then_inc(v_free, 1)

            def outputs(k):
                dve.wait_ge(o2_done, 8 * (k + 1))
                vec.tensor_copy(onat[:, k // 2, 512 * (k % 2):512 * (k % 2) + 512], PSX[k % 2][:]).then_inc(o2_free, 1)

            def sink_arg(b):
                vec.tensor_tensor(den[:, 8 * b:8 * b + 8], nm2[:, 8 * b:8 * b + 8], sink[:], ALU.add).then_inc(sk_req, 1)

            def both(v, b):
                return v.rearrange("p (k b h) -> p b k h", k=2, b=NB)[:, b]

            def divide(b):
                dve.wait_ge(e2_done, 16 * (b + 1))
                dve.wait_ge(sk_done, b + 1)
                link(vec.tensor_tensor(den[:, 8 * b:8 * b + 8], den[:, 8 * b:8 * b + 8], rs2[:, 8 * b:8 * b + 8], ALU.add))
                link(vec.tensor_copy(den[:, 16 + 8 * b:24 + 8 * b], rs2[:, 16 + 8 * b:24 + 8 * b]))
                link(vec.reciprocal(both(den, b), both(den, b)))
                dve.wait_ge(o2_free, 2 * (b + 1))
                for kind in range(2):
                    ov = onat[:, b, 512 * kind:512 * kind + 512].rearrange("p (h d) -> p h d", h=8)
                    n = kind * 16 + b * 8
                    vec.tensor_tensor(ov, ov, spread(den[:, n:n + 8], HD), ALU.mult).then_inc(on_done, 1)

            def head_norm(b):
                dve.wait_ge(on_sq, 2 * (b + 1))
                rsqrt(ss5[:, 2 * b:2 * b + 2], rs5[:, 2 * b:2 * b + 2], 512)
                dve.wait_ge(on_done, 2 * (b + 1))
                for kind in range(2):
                    ov = onat[:, b, 512 * kind:512 * kind + 512]
                    ins = vec.tensor_scalar(ov, ov, rs5[:, 2 * b + kind:2 * b + kind + 1], None, ALU.mult)
                ins.then_inc(hn_done, 1)

            for n in range(NT + 4):
                if n < NT:
                    b, kind, h = tiles2[n]
                    j = stat(n)
                    dve.wait_ge(s2_done, n + 1)
                    src = SB[n % 4][:]
                    if kind == 0:
                        link(vec.tensor_reduce(mxt[:, n % 2:n % 2 + 1], src, AX, ALU.max))
                        vec.tensor_scalar(nm2[:, j:j + 1], mxt[:, n % 2:n % 2 + 1], sink[:, h:h + 1], -1.0,
                                          ALU.max, ALU.mult).then_inc(mx_done, 1)
                    else:
                        vec.tensor_reduce(nm2[:, j:j + 1], src, AX, ALU.max, negate=True).then_inc(mx_done, 1)
                if n % 8 == 3 and n > 8:
                    outputs(n // 8 - 1)
                if n == OUTPUTS_AT:
                    dve.wait_ge(mx_done, 16)
                    sink_arg(0)
                if n == DIVIDE_AT:
                    divide(0)
                if n == NORM_AT:
                    head_norm(0)
            dve.wait_ge(mx_done, NT)
            sink_arg(1)
            turned_block(oT, 0, vc[:, ROWS["on_a"]:ROWS["on_a"] + KD])
            divide(1)
            head_norm(1)

            def add_attention(b, half):
                bank = v_take()
                xv = xres[:, b, half * 512:half * 512 + 512]
                tm = (t0, t1)[half]
                if b > 0:
                    dve.wait_ge(x3_done, b)
                vec.tensor_tensor(tm, bank[:], gbc[:, 0, half * 512:half * 512 + 512], ALU.mult).then_inc(v_free, 1)
                dve.wait_ge(v_free, nv)
                ins = vec.tensor_tensor(xv, xv, tm, ALU.add)
                if half == 0:
                    link(ins)
                else:
                    ins.then_inc(x3_done, 1)

            def normed_block(b):
                nonlocal nsq
                nsq += 1
                dve.wait_ge(sq_done, nsq)
                rsqrt(ss[:, b:b + 1], rstd[:, b:b + 1], D)
                vec.tensor_scalar(hnx[:, b, :], xres[:, b, :], rstd[:, b:b + 1], None, ALU.mult).then_inc(hn_done, 1)

            def lower(q):
                dve.wait_ge(hi_done, q + 1)
                kind, n = mlp[q]
                hi, lo = (unit_parts[q % 3][:, m, :] for m in range(2))
                vec.tensor_tensor(lo, slot_of(NPRE + at["mlp"] + 3 * n + kind), hi, ALU.subtract).then_inc(lo_done, 1)

            def split_columns(b):
                dve.wait_ge(v_free, nv)
                dve.wait_ge(a_free, at["h", b])
                hi, lo = (col_parts[:, m, :, b * P:(b + 1) * P] for m in range(2))
                link(vec.tensor_copy(hi, h3T[:, :, b * P:(b + 1) * P]))
                vec.tensor_tensor(lo, h3T[:, :, b * P:(b + 1) * P], hi, ALU.subtract).then_inc(h3_split, 1)

            add_attention(0, 0)
            turned_block(oT, 1, vc[:, ROWS["on_a"]:ROWS["on_a"] + KD])
            add_attention(0, 1)
            normed_block(0)
            add_attention(1, 0)
            turned_block(h3T, 0, modA[:, 2, :], modT[:, 24:32, 0])
            split_columns(0)
            lower(0)
            add_attention(1, 1)
            normed_block(1)
            lower(1)
            turned_block(h3T, 1, modA[:, 2, :], modT[:, 24:32, 0])
            split_columns(1)
            lower(2)
            U = (at["ffn"][1][1], at["ffn"][1][0])
            for n in range(FP):
                behind = mlp_behind(n)
                for q in behind[:1]:
                    lower(q)
                dve.wait_ge(fg_ready, 2 * n + 2)
                dve.wait_ge(fsg_done, n + 1)
                if n >= 2:
                    dve.wait_ge(down_done, n - 1)
                link(vec.tensor_tensor(fhid[:, n % 2, :], fsg[:, n % 2, :], U[n % 2][:], ALU.mult))
                hi, lo = hid_parts[:, n % 2, 0, :], hid_parts[:, n % 2, 1, :]
                link(vec.tensor_copy(hi, fhid[:, n % 2, :]))
                vec.tensor_tensor(lo, fhid[:, n % 2, :], hi, ALU.subtract).then_inc(fh_done, 1)
                for q in behind[1:]:
                    lower(q)
            acc = (PSX[0], PSX[1], at["ffn"][0][2], at["ffn"][1][2])
            for m in range(2 * NB):
                b, half = divmod(m, 2)
                tm = (t0, t1)[m % 2]
                dve.wait_ge(fd_done, m + 1)
                if m >= 2:
                    dve.wait_ge(y_done, m - 1)
                xv = xres[:, b, half * 512:half * 512 + 512]
                link(vec.tensor_tensor(tm, acc[m][:], gbc[:, 1, half * 512:half * 512 + 512], ALU.mult))
                vec.tensor_tensor(xv, xv, tm, ALU.add).then_inc(y_done, 1)

        @block.gpsimd
        def _(pool):
            npc = nrs = 0
            pl = nc.gpsimd

            def power(dst):
                nonlocal nrs
                nrs += 1
                pool.wait_ge(rs_req, nrs)
                pl.tensor_tensor(dst, dst, c("neghalf")[:, 0:dst.shape[1]], ALU.pow).then_inc(rs_done, 1)

            pl.memset(csil[:], 0.0).then_inc(csil_ready, 1)
            pl.memset(convin[:, :, 0:TAPS - 1], 0.0).then_inc(pad_done, 1)
            pl.memset(padr[0:BH, :], 0.0).then_inc(s_pad0, 1)
            pool.wait_ge(s_pad0, 1)
            pool.dma_start(padr[0:BH, 48:48 + 15 * 64].rearrange("h (r c) -> h r c", c=64)[:, :, 0:31],
                           i["rpb_b_2"].rearrange("l h r c -> (l h) r c")).then_inc(s_pad1, 16)
            pool.wait_ge(s_pad1, 16)
            pool.dma_start(rpb_pad, padr[0:BH, :]).then_inc(s_pad2, 16)
            pool.wait_ge(s_ident, 16)
            power(rstd)
            pool.wait_ge(s_const, 16)
            pool.wait_ge(qkn_done, 2)
            start = c("ident").unsqueeze(1).broadcast_to((P, NB * GH, P))
            for dst in (X, Y):
                pl.tensor_copy(dst.rearrange("p b h j -> p (b h) j"), start).then_inc(xy0, 1)
            for n in range(LEVELS):
                if n == 0:
                    pool.wait_ge(v_free, at["BT"])
                    pool.wait_ge(a_ready, 14)
                if n >= 2:
                    pool.wait_ge(v_ready, at["W", n - 2])
                mask = c(f"level{n}").unsqueeze(1).broadcast_to((P, NB * GH, P))
                pl.tensor_tensor(BTm[:, n % 2].rearrange("p b (h j) -> p (b h) j", h=GH),
                                 BT.rearrange("p b (h j) -> p (b h) j", h=GH), mask, ALU.mult).then_inc(btm_done, 1)
            power(rsg)
            power(rs5[:, 0:2])
            power(rstd)
            power(rstd)
            power(rstd)
            pool.wait_ge(s_toep, 64)
            for b in range(NB):
                mask = c("columns")[:, b * T:(b + 1) * T].unsqueeze(1).broadcast_to((P, BH, T))
                pl.tensor_tensor(bias[b], bias[b], mask, ALU.add).then_inc(s_bias, 1)
            for nh in (2, 2, 8, 8, 8, 8):
                power(rsn[:, 0:2 * nh])
            for b in range(NB):
                power(rs5[:, 2 * b:2 * b + 2])
            for b in range(NB):
                power(rstd[:, b:b + 1])


_INS = ['x', 'attn_norm', 'w_in', 'conv_w', 'A_log', 'dt_bias', 'gdn_norm', 'w_out', 'ffn_norm', 'w_group',
        'w_router', 'w_gate', 'w_up', 'w_down', 'final_norm', 'c_2', 'ctx_2', 'c_ctx_2', 'w_mod_2', 'b_mod_2',
        'norm1_g_2', 'w_in_2', 'qn_a_2', 'kn_a_2', 'sink_a_2', 'qn_b_2', 'kn_b_2', 'rpb_b_2', 'on_a_2', 'on_b_2',
        'w_out_2', 'norm2_g_2', 'w_gate_2', 'w_up_2', 'w_down_2']


def kernel(**inputs):
    import concourse.bacc as _bacc
    from concourse.bass_utils import run_bass_kernel_spmd as _run

    nc = _bacc.Bacc("TRN2", target_bir_lowering=False, num_devices=1)
    consts, where = constants()
    arrays, aps = {}, {}
    for name in _INS + ["consts"]:
        a = consts if name == "consts" else np.ascontiguousarray(inputs[name])
        arrays[f"in_{name}_dram"] = a
        aps[name] = nc.dram_tensor(f"in_{name}_dram", a.shape, mybir.dt.from_np(a.dtype), kind="ExternalInput").ap()
    out = nc.dram_tensor("out_dram", (1, T, D), F32, kind="ExternalOutput").ap()
    two_blocks(nc, consts, where, aps, out)
    r = _run(nc, [arrays], core_ids=[0])
    return r.results[0]["out_dram"]
```
